# Optimizing a Trainium2 kernel written in Bass

```python
import math
import jax, jax.numpy as jnp
from jax import lax
import numpy as np
import jax
import jax.numpy as jnp

D_MODEL = 1024
BATCH = 1
SEQ = 512
DEPTH = 1

N_META = 16
BLOCK_Q = 128
EPS = 1e-6
NEG_INF = -1e30

SSM_WIDTH = D_MODEL // 2
SSM_GROUP = 16
SSM_GROUPS = SSM_WIDTH // SSM_GROUP
SSM_STATE = 64
DT_MIN = 1e-3
DT_MAX = 1e-1

ATT_HEADS = 4
QK_DIM = 64
V_DIM = 2 * QK_DIM
ATT_WIDTH = ATT_HEADS * V_DIM
QK_COLS = ATT_HEADS * 2 * QK_DIM

IN_COLS = SSM_WIDTH + 2 * QK_COLS + ATT_WIDTH + 2 * D_MODEL
SPLITS = (SSM_WIDTH,
          SSM_WIDTH + QK_COLS,
          SSM_WIDTH + 2 * QK_COLS,
          SSM_WIDTH + 2 * QK_COLS + ATT_WIDTH,
          SSM_WIDTH + 2 * QK_COLS + ATT_WIDTH + D_MODEL)

D_FF = ((8 * D_MODEL // 3 + 127) // 128) * 128
CONV_W = 3


def rmsnorm(x, g):
    xf = x.astype(jnp.float32)
    r = lax.rsqrt(jnp.mean(xf * xf, axis=-1, keepdims=True) + EPS)
    return (xf * r).astype(x.dtype) * g

def s5_mixer(u, a_re, a_im, log_dt, b_re, b_im, c_re, c_im, d, glu_w, glu_b):
    bsz, seq_len, _ = u.shape
    ug = u.astype(jnp.float32).reshape(bsz, seq_len, SSM_GROUPS, SSM_GROUP)
    a_re = a_re.astype(jnp.float32); a_im = a_im.astype(jnp.float32)
    dt = jnp.exp(log_dt.astype(jnp.float32))[:, None]
    mag = jnp.exp(a_re * dt)
    lb_re = mag * jnp.cos(a_im * dt)
    lb_im = mag * jnp.sin(a_im * dt)
    den = a_re * a_re + a_im * a_im
    n_re = lb_re - 1.0
    f_re = (n_re * a_re + lb_im * a_im) / den
    f_im = (lb_im * a_re - n_re * a_im) / den
    b_re = b_re.astype(jnp.float32); b_im = b_im.astype(jnp.float32)
    bb_re = f_re[..., None] * b_re - f_im[..., None] * b_im
    bb_im = f_re[..., None] * b_im + f_im[..., None] * b_re
    x_re = jnp.einsum('blgc,gpc->blgp', ug, bb_re)
    x_im = jnp.einsum('blgc,gpc->blgp', ug, bb_im)
    shp = (1, seq_len, SSM_GROUPS, SSM_STATE)
    a_re_t = jnp.broadcast_to(lb_re, shp)
    a_im_t = jnp.broadcast_to(lb_im, shp)

    def combine(left, right):
        ar_l, ai_l, br_l, bi_l = left
        ar_r, ai_r, br_r, bi_r = right
        return (ar_r * ar_l - ai_r * ai_l,
                ar_r * ai_l + ai_r * ar_l,
                ar_r * br_l - ai_r * bi_l + br_r,
                ar_r * bi_l + ai_r * br_l + bi_r)

    _, _, s_re, s_im = lax.associative_scan(combine, (a_re_t, a_im_t, x_re, x_im), axis=1)
    y = (jnp.einsum('blgp,gcp->blgc', s_re, c_re.astype(jnp.float32))
         - jnp.einsum('blgp,gcp->blgc', s_im, c_im.astype(jnp.float32))
         + d.astype(jnp.float32) * ug)
    y = jax.nn.gelu(y.reshape(bsz, seq_len, SSM_WIDTH)).astype(u.dtype)
    return y * jax.nn.sigmoid(y @ glu_w + glu_b)

def diff_attention(q, k, v, lam, slopes):
    bsz, seq_len = q.shape[:2]
    nb = seq_len // BLOCK_Q
    qb = jnp.moveaxis(q.reshape(bsz, nb, BLOCK_Q, ATT_HEADS, 2, QK_DIM), 1, 0)
    starts = jnp.arange(nb, dtype=jnp.int32) * BLOCK_Q
    kpos = jnp.arange(seq_len, dtype=jnp.int32)

    def one_block(args):
        q_blk, start = args
        s = jnp.einsum('bqhjd,bkhjd->bhjqk', q_blk, k,
                       preferred_element_type=jnp.float32)
        dist = (start + jnp.arange(BLOCK_Q, dtype=jnp.int32))[:, None] - kpos[None, :]
        s = s - slopes[None, :, None, None, None] * dist.astype(jnp.float32)[None, None, None]
        s = jnp.where(dist[None, None, None] >= 0, s, NEG_INF)
        p = jax.nn.softmax(s, axis=-1)
        w = p[:, :, 0] - lam * p[:, :, 1]
        return jnp.einsum('bhqk,bkhe->bqhe', w.astype(v.dtype), v)

    o = lax.map(one_block, (qb, starts))
    return jnp.moveaxis(o, 0, 1).reshape(bsz, seq_len, ATT_HEADS, V_DIM)

def conv_glu_ffn(h, w_up, conv_w, conv_b, w_down):
    seq_len = h.shape[1]
    up = h @ w_up
    a, b = up[..., :D_FF], up[..., D_FF:]
    a_pad = jnp.pad(a, ((0, 0), (CONV_W - 1, 0), (0, 0)))
    c = (a_pad[:, 0:seq_len] * conv_w[0] + a_pad[:, 1:seq_len + 1] * conv_w[1]
         + a_pad[:, 2:seq_len + 2] * conv_w[2] + conv_b)
    return (jax.nn.gelu(c) * b) @ w_down

def first_inputs(seed: int = 0) -> dict:
    key = jax.random.key(seed)
    ks = jax.random.split(key, 32)
    f32 = jnp.float32
    nrm = lambda k, shp, s: s * jax.random.normal(k, shp, f32)
    L_ = DEPTH
    return {
        'x': jax.random.normal(ks[0], (BATCH, SEQ, D_MODEL), f32),
        'meta_tokens': nrm(ks[1], (N_META, D_MODEL), 1.0),
        'norm1_g': 1.0 + nrm(ks[2], (L_, D_MODEL), 0.02),
        'w_in': nrm(ks[3], (L_, D_MODEL, IN_COLS), D_MODEL ** -0.5),
        'ssm_a_re': -0.5 + nrm(ks[4], (L_, SSM_GROUPS, SSM_STATE), 0.01),
        'ssm_a_im': math.pi * jnp.arange(SSM_STATE, dtype=f32)[None, None, :]
                    + nrm(ks[5], (L_, SSM_GROUPS, SSM_STATE), 0.01),
        'ssm_log_dt': jax.random.uniform(ks[6], (L_, SSM_GROUPS), f32,
                                         math.log(DT_MIN), math.log(DT_MAX)),
        'ssm_b_re': nrm(ks[7], (L_, SSM_GROUPS, SSM_STATE, SSM_GROUP), (2 * SSM_GROUP) ** -0.5),
        'ssm_b_im': nrm(ks[8], (L_, SSM_GROUPS, SSM_STATE, SSM_GROUP), (2 * SSM_GROUP) ** -0.5),
        'ssm_c_re': nrm(ks[9], (L_, SSM_GROUPS, SSM_GROUP, SSM_STATE), (2 * SSM_STATE) ** -0.5),
        'ssm_c_im': nrm(ks[10], (L_, SSM_GROUPS, SSM_GROUP, SSM_STATE), (2 * SSM_STATE) ** -0.5),
        'ssm_d': nrm(ks[11], (L_, SSM_GROUPS, SSM_GROUP), 1.0),
        'ssm_glu_w': nrm(ks[12], (L_, SSM_WIDTH, SSM_WIDTH), SSM_WIDTH ** -0.5),
        'ssm_glu_b': nrm(ks[13], (L_, SSM_WIDTH), 0.01),
        'q_norm_g': 1.0 + nrm(ks[14], (L_, QK_DIM), 0.02),
        'k_norm_g': 1.0 + nrm(ks[15], (L_, QK_DIM), 0.02),
        'lam_q1': nrm(ks[16], (L_, QK_DIM), 0.1),
        'lam_k1': nrm(ks[17], (L_, QK_DIM), 0.1),
        'lam_q2': nrm(ks[18], (L_, QK_DIM), 0.1),
        'lam_k2': nrm(ks[19], (L_, QK_DIM), 0.1),
        'subln_g': 1.0 + nrm(ks[20], (L_, V_DIM), 0.02),
        'w_ssm_out': nrm(ks[21], (L_, SSM_WIDTH, D_MODEL), SSM_WIDTH ** -0.5),
        'w_att_out': nrm(ks[22], (L_, ATT_WIDTH, D_MODEL), ATT_WIDTH ** -0.5),
        'w_o': nrm(ks[23], (L_, D_MODEL, D_MODEL), D_MODEL ** -0.5),
        'norm2_g': 1.0 + nrm(ks[24], (L_, D_MODEL), 0.02),
        'w_up': nrm(ks[25], (L_, D_MODEL, 2 * D_FF), D_MODEL ** -0.5),
        'conv_w': nrm(ks[26], (L_, CONV_W, D_FF), CONV_W ** -0.5),
        'conv_b': nrm(ks[27], (L_, D_FF), 0.01),
        'w_down': nrm(ks[28], (L_, D_FF, D_MODEL), D_FF ** -0.5),
    }

def first_block(x, meta_tokens, norm1_g, w_in, ssm_a_re, ssm_a_im, ssm_log_dt, ssm_b_re, ssm_b_im,
              ssm_c_re, ssm_c_im, ssm_d, ssm_glu_w, ssm_glu_b, q_norm_g, k_norm_g,
              lam_q1, lam_k1, lam_q2, lam_k2, subln_g, w_ssm_out, w_att_out, w_o,
              norm2_g, w_up, conv_w, conv_b, w_down):
    bsz, seq, _ = x.shape
    seq_len = seq + N_META
    seq_pad = -(-seq_len // BLOCK_Q) * BLOCK_Q
    meta = jnp.broadcast_to(meta_tokens[None].astype(x.dtype), (bsz, N_META, D_MODEL))
    h = jnp.concatenate([meta, x, jnp.zeros((bsz, seq_pad - seq_len, D_MODEL), x.dtype)], axis=1)
    slopes = 2.0 ** (-8.0 * jnp.arange(1, ATT_HEADS + 1, dtype=jnp.float32) / ATT_HEADS)
    q_scale = QK_DIM ** -0.5

    for l in range(DEPTH):
        lam_init = 0.8 - 0.6 * math.exp(-0.3 * l)
        hn = rmsnorm(h, norm1_g[l])
        proj = hn @ w_in[l]
        u, q, k, v, g_ssm, g_att = jnp.split(proj, SPLITS, axis=-1)
        y_ssm = s5_mixer(u, ssm_a_re[l], ssm_a_im[l], ssm_log_dt[l], ssm_b_re[l], ssm_b_im[l],
                         ssm_c_re[l], ssm_c_im[l], ssm_d[l], ssm_glu_w[l], ssm_glu_b[l])
        q = rmsnorm(q.reshape(bsz, seq_pad, ATT_HEADS, 2, QK_DIM), q_norm_g[l]) * q_scale
        k = rmsnorm(k.reshape(bsz, seq_pad, ATT_HEADS, 2, QK_DIM), k_norm_g[l])
        v = v.reshape(bsz, seq_pad, ATT_HEADS, V_DIM)
        lam = (jnp.exp(jnp.sum(lam_q1[l] * lam_k1[l]).astype(jnp.float32))
               - jnp.exp(jnp.sum(lam_q2[l] * lam_k2[l]).astype(jnp.float32)) + lam_init)
        o = diff_attention(q, k, v, lam, slopes)
        y_att = (rmsnorm(o, subln_g[l]) * (1.0 - lam_init)).reshape(bsz, seq_pad, ATT_WIDTH)
        mixed = (jax.nn.sigmoid(g_ssm) * (y_ssm @ w_ssm_out[l])
                 + jax.nn.sigmoid(g_att) * (y_att @ w_att_out[l]))
        h = h + mixed @ w_o[l]
        h = h + conv_glu_ffn(rmsnorm(h, norm2_g[l]), w_up[l], conv_w[l], conv_b[l], w_down[l])

    return h[:, N_META:N_META + seq]


DEPTH_2 = 2

CHUNK = 64
D_MIX = D_MODEL
GROUP_W = D_MIX // 4
NORM_EPS = 1e-6
MASK_VALUE = -1e30
GATE_FLOOR = 1e-20

A_KERNEL = 31
B_HEADS = 4
B_DK = GROUP_W // B_HEADS
B_DV = GROUP_W // B_HEADS
C_HEADS = 4
C_HEADDIM = GROUP_W // C_HEADS
C_GROUPS = 2
C_STATE = 128
C_CONV = 4
C_XBC = GROUP_W + 2 * C_GROUPS * C_STATE
D_HEADS = 4
D_Q_RANK = 256
D_KV_RANK = 128
D_NOPE = 64
D_ROPE = 32
D_VDIM = GROUP_W // D_HEADS
ROPE_THETA = 10000.0
Q_BLOCK = 128

IN_SPLITS = (GROUP_W, GROUP_W, GROUP_W,
             GROUP_W, GROUP_W, GROUP_W, GROUP_W,
             C_XBC, C_HEADS, GROUP_W,
             D_Q_RANK, D_KV_RANK, D_ROPE, GROUP_W)
N_IN = sum(IN_SPLITS)


def rms_norm(x, g, eps=NORM_EPS):
    xf = x.astype(jnp.float32)
    y = xf * lax.rsqrt(jnp.mean(jnp.square(xf), axis=-1, keepdims=True) + eps)
    return (y * g.astype(jnp.float32)).astype(x.dtype)

def layer_norm(x, g, b, eps=1e-5):
    xf = x.astype(jnp.float32)
    mu = jnp.mean(xf, axis=-1, keepdims=True)
    var = jnp.mean(jnp.square(xf - mu), axis=-1, keepdims=True)
    y = (xf - mu) * lax.rsqrt(var + eps)
    return (y * g.astype(jnp.float32) + b.astype(jnp.float32)).astype(x.dtype)

def masked_exp(mask, logd):
    return jnp.where(mask, jnp.exp(jnp.where(mask, logd, 0.0)), 0.0)

def causal_depthwise_conv(x, w, b):
    k, c = w.shape
    y = lax.conv_general_dilated(
        x, w[:, None, :].astype(x.dtype), window_strides=(1,), padding=[(k - 1, 0)],
        dimension_numbers=('NWC', 'WIO', 'NWC'), feature_group_count=c)
    return y + b.astype(x.dtype)

def apply_rotary(x, positions):
    r = x.shape[-1]
    inv_freq = ROPE_THETA ** (-jnp.arange(0, r, 2, dtype=jnp.float32) / r)
    ang = positions.astype(jnp.float32)[..., None] * inv_freq
    if x.ndim == 4:
        ang = ang[:, :, None, :]
    cos, sin = jnp.cos(ang), jnp.sin(ang)
    xf = x.astype(jnp.float32)
    x1, x2 = xf[..., : r // 2], xf[..., r // 2:]
    out = jnp.concatenate([x1 * cos - x2 * sin, x2 * cos + x1 * sin], axis=-1)
    return out.astype(x.dtype)

def conformer_conv_branch(val, glu_gate, gate, dw_w, dw_b, ln_g, ln_b, pw_w, pw_b):
    h = val * jax.nn.sigmoid(glu_gate)
    h = causal_depthwise_conv(h, dw_w, dw_b)
    h = jax.nn.silu(layer_norm(h, ln_g, ln_b))
    h = h @ pw_w + pw_b
    return h * jax.nn.silu(gate)

def hgrn2_branch(q, f_raw, v, gate, lb, norm_g):
    bsz, s, _ = q.shape
    nc = s // CHUNK
    f32 = jnp.float32
    zf = f_raw.astype(f32)
    lbf = lb.astype(f32)
    fgate = lbf + (1.0 - lbf) * jax.nn.sigmoid(zf)
    log_f = jnp.log(jnp.maximum(fgate, GATE_FLOOR))
    k = (1.0 - lbf) * jax.nn.sigmoid(-zf)

    def to_chunks(t, d):
        return t.astype(f32).reshape(bsz, nc, CHUNK, B_HEADS, d).transpose(1, 0, 3, 2, 4)

    qc, kc, gc = to_chunks(q, B_DK), to_chunks(k, B_DK), to_chunks(log_f, B_DK)
    vc = to_chunks(v, B_DV)
    causal = jnp.tril(jnp.ones((CHUNK, CHUNK), dtype=bool))[:, :, None]

    def step(state, inp):
        qt, kt, vt, gt = inp
        b = jnp.cumsum(gt, axis=2)
        o_inter = jnp.einsum('bhtk,bhkv->bhtv', qt * jnp.exp(b), state)
        diff = b[:, :, :, None, :] - b[:, :, None, :, :]
        decay = masked_exp(causal, diff)
        scores = jnp.einsum('bhtk,bhsk,bhtsk->bhts', qt, kt, decay)
        o_intra = jnp.einsum('bhts,bhsv->bhtv', scores, vt)
        b_last = b[:, :, -1:, :]
        new_state = (jnp.exp(b_last[:, :, 0, :])[..., None] * state
                     + jnp.einsum('bhsk,bhsv->bhkv', kt * jnp.exp(b_last - b), vt))
        return new_state, o_inter + o_intra

    state0 = jnp.zeros((bsz, B_HEADS, B_DK, B_DV), f32)
    _, o = lax.scan(step, state0, (qc, kc, vc, gc))
    o = o.transpose(1, 0, 3, 2, 4).reshape(bsz, s, B_HEADS, B_DV)
    o = rms_norm(o, norm_g.reshape(B_HEADS, B_DV)).astype(q.dtype)
    return o.reshape(bsz, s, B_HEADS * B_DV) * jax.nn.silu(gate)

def ssd_branch(xbc, dt_raw, z, conv_w, conv_b, dt_bias, a_log, d_skip, norm_g):
    bsz, s, _ = xbc.shape
    nc = s // CHUNK
    e = C_HEADS // C_GROUPS
    f32 = jnp.float32
    xbc = jax.nn.silu(causal_depthwise_conv(xbc, conv_w, conv_b))
    xs, bm, cm = jnp.split(xbc, [GROUP_W, GROUP_W + C_GROUPS * C_STATE], axis=-1)
    xs = xs.astype(f32).reshape(bsz, nc, CHUNK, C_GROUPS, e, C_HEADDIM)
    bm = bm.astype(f32).reshape(bsz, nc, CHUNK, C_GROUPS, C_STATE)
    cm = cm.astype(f32).reshape(bsz, nc, CHUNK, C_GROUPS, C_STATE)
    dt = jax.nn.softplus(dt_raw.astype(f32) + dt_bias.astype(f32))
    a = (dt * (-jnp.exp(a_log.astype(f32)))).reshape(bsz, nc, CHUNK, C_GROUPS, e)
    dt = dt.reshape(bsz, nc, CHUNK, C_GROUPS, e)
    a_cs = jnp.cumsum(a, axis=2)
    xdt = xs * dt[..., None]
    causal = jnp.tril(jnp.ones((CHUNK, CHUNK), dtype=bool))[:, :, None, None]
    seg = a_cs[:, :, :, None] - a_cs[:, :, None, :]
    lmat = masked_exp(causal, seg)
    cb = jnp.einsum('bclgn,bcsgn->bclsg', cm, bm)
    scores = cb[..., None] * lmat
    y_diag = jnp.einsum('bclsge,bcsgep->bclgep', scores, xdt)
    wx = xdt * jnp.exp(a_cs[:, :, -1:] - a_cs)[..., None]
    states = jnp.einsum('bclgn,bclgep->bcgepn', bm, wx)
    chunk_decay = jnp.exp(a_cs[:, :, -1])

    def step(h, inp):
        st, dc = inp
        return dc[..., None, None] * h + st, h

    h0 = jnp.zeros((bsz, C_GROUPS, e, C_HEADDIM, C_STATE), f32)
    _, prev = lax.scan(step, h0, (states.transpose(1, 0, 2, 3, 4, 5),
                                  chunk_decay.transpose(1, 0, 2, 3)))
    prev = prev.transpose(1, 0, 2, 3, 4, 5)
    y_off = jnp.einsum('bclgn,bcgepn->bclgep', cm, prev) * jnp.exp(a_cs)[..., None]
    y = y_diag + y_off + xs * d_skip.astype(f32).reshape(C_GROUPS, e)[..., None]
    y = y.reshape(bsz, s, C_GROUPS, e * C_HEADDIM)
    zg = jax.nn.silu(z.astype(f32)).reshape(bsz, s, C_GROUPS, e * C_HEADDIM)
    y = rms_norm(y * zg, norm_g.reshape(C_GROUPS, e * C_HEADDIM))
    return y.reshape(bsz, s, GROUP_W).astype(z.dtype)

def mla_branch(cq, ckv, k_rope, gate, positions, qa_g, qb_w, kva_g, kvb_w):
    bsz, s, _ = cq.shape
    q = (rms_norm(cq, qa_g) @ qb_w).reshape(bsz, s, D_HEADS, D_NOPE + D_ROPE)
    q = jnp.concatenate([q[..., :D_NOPE], apply_rotary(q[..., D_NOPE:], positions)], axis=-1)
    kv = (rms_norm(ckv, kva_g) @ kvb_w).reshape(bsz, s, D_HEADS, D_NOPE + D_VDIM)
    k_nope, v = kv[..., :D_NOPE], kv[..., D_NOPE:]
    k_r = apply_rotary(k_rope, positions)
    k = jnp.concatenate(
        [k_nope, jnp.broadcast_to(k_r[:, :, None, :], (bsz, s, D_HEADS, D_ROPE))], axis=-1)
    scale = (D_NOPE + D_ROPE) ** -0.5
    nqb = s // Q_BLOCK
    key_chunk = jnp.arange(s) // CHUNK
    q_blocks = q.reshape(bsz, nqb, Q_BLOCK, D_HEADS, D_NOPE + D_ROPE).transpose(1, 0, 2, 3, 4)
    q_chunk = key_chunk.reshape(nqb, Q_BLOCK)

    def attend(inp):
        qb, qch = inp
        sc = jnp.einsum('bqhd,bkhd->bhqk', qb, k).astype(jnp.float32) * scale
        mask = key_chunk[None, :] <= qch[:, None]
        p = jax.nn.softmax(jnp.where(mask, sc, MASK_VALUE), axis=-1).astype(v.dtype)
        return jnp.einsum('bhqk,bkhd->bqhd', p, v)

    o = lax.map(attend, (q_blocks, q_chunk))
    o = o.transpose(1, 0, 2, 3, 4).reshape(bsz, s, D_HEADS * D_VDIM)
    return o * jax.nn.silu(gate)

def second_inputs(seed: int = 0) -> dict:
    key = jax.random.key(seed)
    ks = jax.random.split(key, 24)
    f32 = jnp.float32

    def nrm(k, shape, scale):
        return jax.random.normal(k, shape, f32) * scale

    def gain(k, shape):
        return 1.0 + 0.02 * jax.random.normal(k, shape, f32)

    x = nrm(ks[0], (BATCH, SEQ, D_MODEL), 1.0)
    offsets = jax.random.randint(ks[1], (BATCH, 1), 0, 4096, dtype=jnp.int32)
    positions = offsets + jnp.arange(SEQ, dtype=jnp.int32)[None, :]
    dt0 = jnp.exp(jax.random.uniform(ks[16], (DEPTH_2, C_HEADS), f32,
                                     math.log(1e-3), math.log(1e-1)))
    return {
        'x': x,
        'positions': positions,
        'pre_norm_g': gain(ks[2], (DEPTH_2, D_MODEL)),
        'post_norm_g': gain(ks[3], (DEPTH_2, D_MODEL)),
        'w_in': nrm(ks[4], (DEPTH_2, D_MODEL, N_IN), D_MODEL ** -0.5),
        'w_out': nrm(ks[5], (DEPTH_2, D_MIX, D_MODEL), D_MIX ** -0.5),
        'a_dw_w': nrm(ks[6], (DEPTH_2, A_KERNEL, GROUP_W), A_KERNEL ** -0.5),
        'a_dw_b': nrm(ks[7], (DEPTH_2, GROUP_W), 0.02),
        'a_ln_g': gain(ks[8], (DEPTH_2, GROUP_W)),
        'a_ln_b': nrm(ks[9], (DEPTH_2, GROUP_W), 0.02),
        'a_pw_w': nrm(ks[10], (DEPTH_2, GROUP_W, GROUP_W), GROUP_W ** -0.5),
        'a_pw_b': nrm(ks[11], (DEPTH_2, GROUP_W), 0.02),
        'b_lb_logits': 1.0 + nrm(ks[12], (DEPTH_2, B_HEADS * B_DK), 0.1),
        'b_norm_g': gain(ks[13], (DEPTH_2, B_HEADS * B_DV)),
        'c_conv_w': nrm(ks[14], (DEPTH_2, C_CONV, C_XBC), C_CONV ** -0.5),
        'c_conv_b': nrm(ks[15], (DEPTH_2, C_XBC), 0.02),
        'c_dt_bias': dt0 + jnp.log(-jnp.expm1(-dt0)),
        'c_a_log': jnp.log(jax.random.uniform(ks[17], (DEPTH_2, C_HEADS), f32, 1.0, 16.0)),
        'c_d': 1.0 + nrm(ks[18], (DEPTH_2, C_HEADS), 0.1),
        'c_norm_g': gain(ks[19], (DEPTH_2, GROUP_W)),
        'd_qa_g': gain(ks[20], (DEPTH_2, D_Q_RANK)),
        'd_qb_w': nrm(ks[21], (DEPTH_2, D_Q_RANK, D_HEADS * (D_NOPE + D_ROPE)), D_Q_RANK ** -0.5),
        'd_kva_g': gain(ks[22], (DEPTH_2, D_KV_RANK)),
        'd_kvb_w': nrm(ks[23], (DEPTH_2, D_KV_RANK, D_HEADS * (D_NOPE + D_VDIM)), D_KV_RANK ** -0.5),
    }

def second_block(x, positions, pre_norm_g, post_norm_g, w_in, w_out,
              a_dw_w, a_dw_b, a_ln_g, a_ln_b, a_pw_w, a_pw_b,
              b_lb_logits, b_norm_g,
              c_conv_w, c_conv_b, c_dt_bias, c_a_log, c_d, c_norm_g,
              d_qa_g, d_qb_w, d_kva_g, d_kvb_w):
    lb_p = jax.nn.softmax(b_lb_logits.astype(jnp.float32), axis=0)
    lower_bounds = jnp.cumsum(lb_p, axis=0) - lb_p[0:1]
    split_at = [int(v) for v in np.cumsum(IN_SPLITS)[:-1]]
    for l in range(DEPTH_2):
        h = rms_norm(x, pre_norm_g[l])
        proj = h @ w_in[l]
        (a_val, a_glu, a_gate, b_q, b_f, b_i, b_gate,
         c_xbc, c_dt, c_z, d_cq, d_ckv, d_kr, d_gate) = jnp.split(proj, split_at, axis=-1)
        y_a = conformer_conv_branch(a_val, a_glu, a_gate, a_dw_w[l], a_dw_b[l],
                                    a_ln_g[l], a_ln_b[l], a_pw_w[l], a_pw_b[l])
        y_b = hgrn2_branch(b_q, b_f, b_i, b_gate, lower_bounds[l], b_norm_g[l])
        y_c = ssd_branch(c_xbc, c_dt, c_z, c_conv_w[l], c_conv_b[l], c_dt_bias[l],
                         c_a_log[l], c_d[l], c_norm_g[l])
        y_d = mla_branch(d_cq, d_ckv, d_kr, d_gate, positions, d_qa_g[l], d_qb_w[l],
                         d_kva_g[l], d_kvb_w[l])
        y = jnp.concatenate([y_a, y_b, y_c, y_d], axis=-1) @ w_out[l]
        x = x + rms_norm(y, post_norm_g[l])
    return x


def setup_inputs(seed=0):
    out = dict(first_inputs(seed))
    for name, value in second_inputs(seed + 1).items():
        if name != "x":
            out[name + "_2"] = value
    return out


def reference(
    x, meta_tokens, norm1_g, w_in, ssm_a_re, ssm_a_im, ssm_log_dt, ssm_b_re, ssm_b_im, ssm_c_re,
    ssm_c_im, ssm_d, ssm_glu_w, ssm_glu_b, q_norm_g, k_norm_g, lam_q1, lam_k1, lam_q2, lam_k2,
    subln_g, w_ssm_out, w_att_out, w_o, norm2_g, w_up, conv_w, conv_b, w_down, positions_2,
    pre_norm_g_2, post_norm_g_2, w_in_2, w_out_2, a_dw_w_2, a_dw_b_2, a_ln_g_2, a_ln_b_2,
    a_pw_w_2, a_pw_b_2, b_lb_logits_2, b_norm_g_2, c_conv_w_2, c_conv_b_2, c_dt_bias_2,
    c_a_log_2, c_d_2, c_norm_g_2, d_qa_g_2, d_qb_w_2, d_kva_g_2, d_kvb_w_2,
):
    x = first_block(
        x, meta_tokens, norm1_g, w_in, ssm_a_re, ssm_a_im, ssm_log_dt, ssm_b_re, ssm_b_im,
        ssm_c_re, ssm_c_im, ssm_d, ssm_glu_w, ssm_glu_b, q_norm_g, k_norm_g, lam_q1, lam_k1,
        lam_q2, lam_k2, subln_g, w_ssm_out, w_att_out, w_o, norm2_g, w_up, conv_w, conv_b,
        w_down,
    )
    return second_block(
        x, positions_2, pre_norm_g_2, post_norm_g_2, w_in_2, w_out_2, a_dw_w_2, a_dw_b_2,
        a_ln_g_2, a_ln_b_2, a_pw_w_2, a_pw_b_2, b_lb_logits_2, b_norm_g_2, c_conv_w_2,
        c_conv_b_2, c_dt_bias_2, c_a_log_2, c_d_2, c_norm_g_2, d_qa_g_2, d_qb_w_2, d_kva_g_2,
        d_kvb_w_2,
    )


_drawn_inputs = setup_inputs


def setup_inputs(seed=0):
    import zlib

    import numpy as np

    out = dict(_drawn_inputs(seed))
    spreads = {}
    factors = {'ssm_a_re': 8.0,
     'ssm_a_im': 2.803,
     'ssm_log_dt': 2.808,
     'ssm_b_re': 3.942,
     'ssm_b_im': 3.935,
     'ssm_c_re': 3.981,
     'ssm_c_im': 3.941,
     'ssm_glu_b': 8.0,
     'q_norm_g': 4.218,
     'k_norm_g': 4.335,
     'subln_g': 3.981,
     'conv_b': 6.959,
     'post_norm_g_2': 3.042,
     'a_dw_b_2': 4.817,
     'a_ln_g_2': 8.0,
     'a_ln_b_2': 8.0,
     'a_pw_b_2': 5.95,
     'b_norm_g_2': 6.365,
     'c_norm_g_2': 3.848,
     'd_qa_g_2': 8.0,
     'd_kva_g_2': 8.0}
    for name, (base, spread) in spreads.items():
        noise = np.random.default_rng([zlib.crc32(name.encode()), seed]).standard_normal(out[name].shape)
        drawn = base * np.exp(spread * noise) if base else spread * noise
        out[name] = jnp.asarray(drawn.astype(out[name].dtype))
    for name, factor in factors.items():
        out[name] = (out[name] * factor).astype(out[name].dtype)
    return out
```

```python
from contextlib import ExitStack, contextmanager

import numpy as np

import concourse.bass as bass
from concourse import mybir

F32 = mybir.dt.float32
I32 = mybir.dt.int32
ACT = mybir.ActivationFunctionType
ALU = mybir.AluOpType
AX = mybir.AxisListType

P = 128
D = 1024
KD = D // P
NMETA = 16
SEQ = 512
T = SEQ + NMETA
H = T // 2
WSLOTS = 4
EPS = 1e-6
NFF = 22
LAYERS = 2
NPROJ = 28
HEADS = 4
LAM_INIT = 0.8 - 0.6
TILES = [(0, NMETA)] + [(NMETA + P * i, P) for i in range(4)]
LAG = 16
NBLK = SEQ // LAG
TAPS = 31
NSC = 17000
QKR = 96

VEC1 = [("g1", 8), ("qg", 1), ("kg", 1), ("d", 4), ("glub", 4), ("g2", 8), ("cw0", NFF), ("cw1", NFF), ("cw2", NFF),
        ("cb", NFF), ("are", 16), ("aim", 16), ("ldt", 16), ("subg", 1), ("lam", 256)]
VEC2 = [("pre", 8), ("post", 8), ("dww", 2 * (TAPS + 1)), ("dwb", 2), ("lng", 2), ("lnb", 2), ("pwb", 2), ("lbl", 4),
        ("bng", 2), ("ccw", 24), ("ccb", 6), ("dtb", 1), ("alog", 1), ("dsk", 2), ("cng", 2), ("qag", 2), ("kvg", 1), ("isl", 1)]
CONSTS = [("ident", P), ("ones", P), ("pair64", P), ("rot", P), ("dist", T), ("mlamask", SEQ), ("causal", P),
          ("blk8", 8), ("negslope", HEADS), ("invf", 1), ("sgn", 1), ("sel4", 4 * P), ("keep", SEQ)]


def columns(table):
    at, out = 0, {}
    for name, n in table:
        out[name] = (at, at + n)
        at += n
    return out, at


V1, NV1 = columns(VEC1)
V2, NV2 = columns(VEC2)
CC, NCC = columns(CONSTS)

MAGIC = 12582912.0
PI2 = [6.28125, 0.0019350051879882812, 3.019916050733e-07]
PIF = 3.1415925
NEG = -1e30

NSW = 2048
SWQ, SWR, SWK, SWV, SWP = 0, 768, 1024, 1280, 1536

PER = {'act.att': {'act_full0': 7, 'act_full1': 6, 'act_step': 1, 'sc_ready': 5},
 'act.lag': {'act_full0': 2, 'act_full1': 2},
 'act.layer': {'a_x': 1,
               'a_xc': 1,
               'act_full0': 35,
               'act_full1': 14,
               'act_full2': 11,
               'act_full3': 11,
               'act_step': 7,
               'b_acc2': 1,
               'b_s': 1,
               'c_cx': 1,
               'c_d': 1,
               'c_done': 1,
               'c_dtabs': 1,
               'c_wd': 1,
               'c_yc': 1,
               'd_kr': 1,
               'd_o': 16,
               'd_q': 1,
               'd_sc': 16,
               'd_trig_arg': 1,
               'lb_arg': 1,
               'x2_ready': 1},
 'act.mla': {'act_full0': 4, 'd_o': 4, 'd_sc': 4},
 'act.proj': {'act_full0': 1, 'act_full1': 1, 'act_full2': 1, 'act_full3': 1},
 'act.s5': {'act_full0': 4, 'act_full1': 4, 'act_full3': 4, 's5_x_free': 4},
 'act.up': {'act_full0': 1, 'act_full2': 1, 'ffc': 2},
 'act.uqk': {'act_full0': 1, 'act_full1': 1, 'act_full2': 1, 'act_full3': 1},
 'act.wout': {'act_full0': 1, 'act_full1': 1, 'act_full2': 1, 'act_full3': 1},
 'dve.att': {'dve_full2': 5,
             'dve_full3': 5,
             'dve_step': 22,
             'ex_ready': 5,
             'o_norm': 1,
             'o_root': 1,
             'qk_root': 1,
             'w_comb': 5,
             'wt_ready': 5},
 'dve.lag': {'b_acc': 8, 'b_e': 8, 'dve_full2': 4, 'dve_full3': 4, 'dve_step': 16},
 'dve.layer': {'a_root': 1,
               'a_th': 1,
               'a_xt': 1,
               'b_acc': 18,
               'b_dz': 1,
               'b_e': 16,
               'b_root': 1,
               'b_th': 1,
               'c_acb': 1,
               'c_de': 1,
               'c_done': 1,
               'c_dtln': 1,
               'c_root': 1,
               'c_th': 1,
               'c_we': 1,
               'c_x': 1,
               'd_ex': 16,
               'd_root': 1,
               'd_trig': 1,
               'd_wt': 16,
               'dve_full0': 3,
               'dve_full1': 20,
               'dve_full2': 19,
               'dve_full3': 19,
               'dve_step': 213,
               'gate_th': 2,
               'lb_th': 1,
               'rms_root': 2,
               'small_in': 16},
 'dve.mix': {'dve_full0': 2, 'dve_full1': 2, 'dve_full2': 2, 'dve_full3': 2, 'dve_step': 8},
 'dve.mla': {'d_ex': 4, 'd_wt': 4, 'dve_full1': 4, 'dve_full2': 2, 'dve_full3': 2, 'dve_step': 20},
 'dve.s5': {'dve_full2': 1, 'dve_step': 16, 's5_ph': 4, 's5_s': 4, 's5_s_free': 3, 's5_x': 4},
 'dve.up': {'dve_full1': 1, 'dve_full3': 1, 'dve_step': 6, 'ffa': 2, 'ffg': 2},
 'dve.wo': {'dve_full0': 1, 'dve_full1': 1, 'dve_full2': 1, 'dve_full3': 1},
 'pe.att': {'free0': 1,
            'free1': 5,
            'free2': 5,
            'free3': 5,
            'o_norm': 1,
            'qk_n': 1,
            'qk_sq': 1,
            'w_comb': 5,
            'wt_ready': 5},
 'pe.down': {'w_ready0': 16, 'w_ready1': 16, 'w_ready2': 16, 'w_ready3': 16},
 'pe.lag': {'b_m': 8,
            'free0': 2,
            'free1': 2,
            'free2': 4,
            'free3': 4,
            'w_ready0': 16,
            'w_ready1': 16,
            'w_ready2': 16,
            'w_ready3': 16},
 'pe.layer': {'a_ca': 1,
              'a_h': 1,
              'a_sq': 1,
              'b_m': 16,
              'b_s': 1,
              'b_sq': 1,
              'b_ve': 4,
              'c_bt': 1,
              'c_cme': 1,
              'c_dt': 1,
              'c_hs': 1,
              'c_sc': 1,
              'c_sq': 1,
              'c_wx': 1,
              'c_x': 1,
              'd_ex': 16,
              'd_n': 1,
              'd_o': 16,
              'd_sq': 1,
              'd_v': 1,
              'd_wt': 16,
              'free0': 19,
              'free1': 31,
              'free2': 29,
              'free3': 30,
              'hn_ready': 1,
              'qgz': 2,
              'qst': 4,
              'sq_ready': 1,
              'w_ready0': 144,
              'w_ready1': 144,
              'w_ready2': 144,
              'w_ready3': 144,
              'y_ready': 1,
              'y_sq': 1},
 'pe.mix': {'free0': 2,
            'free1': 2,
            'free2': 2,
            'free3': 2,
            'w_ready0': 16,
            'w_ready1': 16,
            'w_ready2': 16,
            'w_ready3': 16},
 'pe.mla': {'d_ex': 4, 'd_wt': 4, 'free1': 4, 'free2': 2, 'free3': 2, 'qst': 1},
 'pe.proj': {'free0': 1,
             'free1': 1,
             'free2': 1,
             'free3': 1,
             'w_ready0': 16,
             'w_ready1': 16,
             'w_ready2': 16,
             'w_ready3': 16},
 'pe.s5': {'free0': 4,
           'free1': 4,
           'free2': 1,
           'free3': 4,
           's5_s': 4,
           'w_ready0': 32,
           'w_ready1': 32,
           'w_ready2': 32,
           'w_ready3': 32},
 'pe.up': {'free0': 1,
           'free1': 1,
           'free2': 1,
           'free3': 1,
           'w_ready0': 16,
           'w_ready1': 16,
           'w_ready2': 16,
           'w_ready3': 16},
 'pe.uqk': {'free0': 1,
            'free1': 1,
            'free2': 1,
            'free3': 1,
            'w_ready0': 16,
            'w_ready1': 16,
            'w_ready2': 16,
            'w_ready3': 16},
 'pe.wo': {'free0': 1,
           'free1': 1,
           'free2': 1,
           'free3': 1,
           'w_ready0': 16,
           'w_ready1': 16,
           'w_ready2': 16,
           'w_ready3': 16},
 'pe.wout': {'free0': 1,
             'free1': 1,
             'free2': 1,
             'free3': 1,
             'w_ready0': 16,
             'w_ready1': 16,
             'w_ready2': 16,
             'w_ready3': 16},
 'pool.lag': {'b_m': 8, 'b_t': 8, 'pool_step': 16},
 'pool.layer': {'b_kh': 1,
                'b_m': 16,
                'b_t': 16,
                'b_tok': 1,
                'b_us': 4,
                'c_acb': 1,
                'c_x': 1,
                'pool_step': 34,
                'qgz': 2,
                'x2_ready': 1},
 'pool.s5': {'pool_step': 4, 's5_ph': 4, 's5_x_free': 4},
 'sp.qkv': {'w_free0': 1, 'w_free1': 1, 'w_free2': 1, 'w_free3': 1},
 'sp.rest': {'w_free0': 1, 'w_free1': 1, 'w_free2': 1, 'w_free3': 1},
 'sp.s5': {'w_free0': 2, 'w_free1': 2, 'w_free2': 2, 'w_free3': 2}}


class Tally:

    def __init__(self, who, eng, sems):
        self.who, self.eng, self.sems, self.base, self.loops = who, eng, sems, {}, []

    def __call__(self, name, add=1):
        self.base[name] = self.base.get(name, 0) + add
        return self.now(name)

    def now(self, name):
        value = self.base.get(name, 0)
        for reg, per in self.loops:
            if per.get(name):
                value = reg * per[name] + value
        return self.sems[name], value

    def settle(self):
        self.eng.sem_inc(self.sems["settled"], 1)

    @contextmanager
    def loop(self, name, count):
        if self.loops:
            self.settle()
        start = dict(self.base)
        per = PER.get(self.who + "." + name, {})
        with self.eng.Fori(0, count) as i:
            self.loops.append((i, per))
            yield i
            self.loops.pop()
        added = {k: v - start.get(k, 0) for k, v in self.base.items() if v != start.get(k, 0)}
        assert added == per, (self.who, name, added)
        for k, v in added.items():
            self.base[k] = start.get(k, 0) + v * count


def build(nc, a, out):
    with ExitStack() as ctx:
        def sb(name, shape, dt=F32):
            return ctx.enter_context(nc.sbuf_tensor(name, shape, dt))

        SEMS = {}

        def sem(name):
            SEMS[name] = ctx.enter_context(nc.semaphore(name))
            return SEMS[name]

        PS = [ctx.enter_context(nc.psum_tensor(f"PS{p}", [P, 2, 512], F32)) for p in range(4)]
        for p in range(4):
            sem(f"act_full{p}")
            sem(f"dve_full{p}")
            sem(f"free{p}")
        for k in range(WSLOTS):
            sem(f"w_ready{k}")
            sem(f"w_free{k}")
        for name in ("par_in", "settled", "eps_ready", "v_zero", "v_ready", "s5_dt", "ys_gelu", "x_in",  "out_done", "dve_step", "act_step", "pool_step",
                     "sq_ready", "rms_root", "hn_ready", "u_ready", "proj_evac", "v_evac", "gate_evac",
                     "s5_tab", "s5_x", "s5_x_free", "s5_ph", "s5_ph_free", "s5_s", "s5_s_free", "s5_c", "s5_y",
                     "trig_arg", "trig", "lam_arg", "lam_exp",
                     "qk_sq", "qk_root", "qk_n", "sc_ready", "ex_ready", "w_comb", "wt_ready", "wt_free", "o_raw",
                     "o_root", "o_norm", "ya_ready", "glu_th", "ys_ready", "mix_ready", "h_ready",
                     "ffa", "ffa_free", "ffc", "ffg", "ff_h", "x2_ready", "hid_done", "small_in", "lb_arg", "lb_th", "b_th", "a_th", "b_kh", "b_m", "b_e", "b_t", "b_acc", "b_tok", "b_ve", "b_us", "b_s", "b_sq",
                     "b_root", "b_root_d", "a_ca", "a_xc", "a_sq", "a_root", "a_x", "a_xt", "a_h", "gates", "gate_th", "qgz",
                     "c_cx", "c_th", "c_x", "c_dtabs", "c_dtln", "c_alog", "c_dt", "c_acb", "c_bt", "c_col", "c_wd", "c_we", "c_wx", "c_d", "c_de", "c_cme",
                     "c_hs", "c_sc", "c_yc", "c_sq", "c_root", "d_sq", "d_root", "d_n", "d_trig_arg", "d_trig", "d_q", "d_k", "d_kr", "d_v",
                     "d_st", "d_sc", "d_ex", "d_wt", "d_o", "y_ready", "yo", "y_sq", "pos_in", "layer_w", "qst", "b_acc2", "b_dz", "c_done"):
            sem(name)

        ring = sb("ring", [P, WSLOTS, 1024])
        X = sb("X", [P, KD, T])
        HN = sb("HN", [P, KD, T])
        R = sb("R", [P, T])
        PJ = sb("PJ", [P, NPROJ, T])
        V = sb("V", [P, 5, 512])
        par1 = sb("params1", [P, NV1])
        cst = sb("consts", [P, NCC])
        SC = sb("SC", [P, NSC])

        def c(name, lo=0, n=None, rows=P):
            s, e = CC[name]
            return cst[0:rows, s + lo:e if n is None else s + lo + n]

        def v1(name, k=0, n=1):
            return par1[:, V1[name][0] + k:V1[name][0] + k + n]

        at = [0]

        def cut(n, *shape):
            s = at[0]
            at[0] += n
            assert at[0] <= NSC, at[0]
            v = SC[:, s:s + n]
            if len(shape) == 2:
                v = v.rearrange("p (a b) -> p a b", a=shape[0])
            if len(shape) == 3:
                v = v.rearrange("p (a b c) -> p a b c", a=shape[0], b=shape[1])
            return v

        ph_a = cut(16 * 8 * 2, 2, 128)
        ph_b = cut(16 * 66 * 2, 2, 16 * 66)
        s5c = cut(12 * 16, 12, 16)
        POS = sb("POS", [P, SEQ], I32)
        LB2 = sb("LB2", [P, 4])
        CWH = sb("CWH", [P, 32])
        junkE = sb("junkE", [P, 32])
        XS = cut(2 * 2 * T, 2, 2, T)
        PH = cut(2 * 2 * T, 2, 2, T)
        TMP = cut(4 * T, 4, T)
        PT = cut(2 * T, 2, T)
        SS = cut(2 * T, 2, T)
        CW = cut(2 * P, 2, P)
        at[0] = 0
        QS = cut(T)
        KS = cut(T)
        SQ = cut(2 * T, 2, T)
        RT = cut(2 * T, 2, T)
        SX = cut(4 * T, 2, 2, T)
        WC = cut(T)
        JK = cut(T)
        WT = cut(5 * P, 5, P)
        OR = cut(5 * P, 5, P)
        st = cut(40)
        lamc = sb("lamc", [P, 8])
        glub2 = sb("glub2", [P, 4])
        epsc = sb("epsc", [P, 4])
        junk = sb("junk", [P, 8])
        at[0] = 0
        JK2 = cut(T)
        at[0] = 0
        TH = cut(4 * T, 4, T)
        at[0] = 0
        FA = cut(514)
        CV = cut(512)
        GL = cut(512)
        hid = PJ[:].rearrange("p a b -> p (a b)")[:, 0:NFF * SEQ].rearrange("p (a b) -> p a b", a=NFF)

        PJ2 = PJ[:].rearrange("p a b -> p (a b)")[:, 0:NPROJ * SEQ].rearrange("p (a b) -> p a b", a=NPROJ)
        HNf = HN[:].rearrange("p a b -> p (a b)")
        XK = X[:, :, NMETA:T]
        SW = V[:].rearrange("p a b -> p (a b)")[:, 0:NSW + NV2]

        def v2(name, k=0, m=1, rows=P):
            s_ = NSW + V2[name][0] + k
            return SW[0:rows, s_:s_ + m]

        at[0] = 0
        FZ = cut(2 * 528, 2, 528)
        KP = cut(2 * 528, 2, 528)
        US0 = SC[:, 0:2048]
        VP = cut(2 * 528, 2, 528)
        TM = cut(2 * 2 * 512, 2, 2, 512)
        US1 = SC[:, at[0] - 2048:at[0]]
        MB = cut(2 * 2 * 512, 2, 2, 512)
        EE = cut(2 * 512, 2, 512)
        HP = cut(2 * 543, 2, 543)
        ACC = cut(2 * 512, 2, 512)
        CA = cut(2 * 512, 2, 512)
        QG = cut(2 * 512, 2, 512)
        KH = cut(2 * 512, 2, 512)
        DWH = cut(64)
        DL = cut(2 * NBLK, 2, NBLK)
        LB = cut(8)
        NTH = cut(2 * 512, 2, 512)
        QZt = cut(4 * 512, 4, 512)
        KHT = MB[:, 0].rearrange("p a b -> p (a b)").rearrange("p (t c) -> p t c", t=4)
        VT = MB[:, 1].rearrange("p a b -> p (a b)").rearrange("p (t c) -> p t c", t=4)
        FREE = [PJ2[:, 0:4, :], PJ2[:, 6:10, :]]
        VE = [x.rearrange("p a b -> p (a b)") for x in FREE]
        DZ = VE
        HNY = HNf[:, 0:4096].rearrange("p (a b) -> p a b", a=8)
        QZ = QZt[:, :, :]
        SQA = HP[:, :, 0:512]
        RB = NTH
        RA = EE[:, 0, :]
        at[0] = 0
        CX = cut(6 * 512, 6, 512)
        ACB = cut(4 * 512, 4, 512)
        EAB = cut(4 * 512, 4, 512)
        DD = cut(4 * 512, 4, 512)
        CME = cut(4 * 512, 4, 512)
        XDT = cut(1024, 4, 4, 64)
        WX = cut(1024, 4, 4, 64)
        BT = cut(1024, 4, 256)
        HS = cut(3 * 256, 3, 256)
        DT4 = cut(512)
        AC4 = cut(512)
        T4 = CX[:, 0, :]
        COL = cut(32, 4, 8)
        WCOL = cut(16, 4, 4)
        YC = CX[:, 0:2, :]
        SQC = CX[:, 2:4, :]
        RC = CX[:, 4:6, :]
        at[0] = 0
        QF = cut(4 * 512, 4, 512)
        KF = cut(4 * 512, 4, 512)
        VD = cut(1024, 4, 256)
        OD = cut(1024, 4, 256)
        QST = cut(512)
        SD = cut(2 * 512, 2, 512)
        WD = cut(512, 4, P)
        CQ = cut(2 * 512, 2, 512)
        CK = cut(512)
        RD = cut(2 * 512, 2, 512)
        SQD = cut(3 * 512, 3, 512)
        KR = cut(512)
        KT = cut(512)
        COS = cut(512)
        SIN = cut(512)
        ANG = cut(512)
        sd = cut(8)
        TQ = SQD[:, 0, :]

        GATES = (22, 23, 24, 25, 20, 21, 26, 27)

        def ps(p):
            return PS[p][:].rearrange("p a b -> p (a b)")

        def halves(p, rows=P):
            return PS[p][0:rows, :, 0:H]

        def two(ap):
            return ap.rearrange("p (a b) -> p a b", a=2)

        block = ctx.enter_context(nc.Block())

        @block.sync
        def _(sp):
            n = Tally("sp", sp, SEMS)
            n.base["w_free3"] = 1
            for t in range(KD):
                sp.dma_start(X[:, t, :], a["xT"][t]).then_inc(SEMS["x_in"], 16)
            sp.dma_start(par1[:, :], a["par1"]).then_inc(SEMS["par_in"], 16)
            sp.dma_start(POS[:, :], a["pos"]).then_inc(SEMS["pos_in"], 16)
            sp.dma_start(cst[:, :], a["cst"]).then_inc(SEMS["par_in"], 16)
            w = a["wst"]

            def load(k, src, width=1024):
                sp.wait_ge(*n(f"w_free{k}"))
                sp.dma_start(ring[:, k, 0:width], src).then_inc(SEMS[f"w_ready{k}"], 16)

            for k in range(WSLOTS):
                sp.dma_start(ring[:, k, :], w[k]).then_inc(SEMS[f"w_ready{k}"], 16)
            with n.loop("qkv", 3) as i:
                for k in range(WSLOTS):
                    load(k, w[i * 4 + (4 + k)])
            with n.loop("s5", 4) as i:
                for j in range(4):
                    load((2 * j) % 4, a["s5w"][i * 4 + j], width=512)
                    load((2 * j + 1) % 4, w[i * 4 + (16 + j)])
            with n.loop("rest", (a["wst"].shape[0] - 32) // 4) as i:
                for k in range(WSLOTS):
                    load(k, w[i * 4 + (32 + k)])
            sp.wait_ge(SEMS["x2_ready"], 1 + LAYERS)
            for t in range(KD):
                sp.dma_start(out[t], XK[:, t, :]).then_inc(SEMS["out_done"], 16)
            sp.wait_ge(SEMS["out_done"], 16 * KD)

        @block.tensor
        def _(pe):
            n = Tally("pe", pe, SEMS)
            mm = nc.tensor.matmul
            for p in range(4):
                n.base[f"free{p}"] = 1

            def put(p, counted=True):
                pe.wait_ge(*n.now(f"free{p}"))
                if counted:
                    n.base[f"free{p}"] = n.base.get(f"free{p}", 0) + 1

            def slot(k):
                pe.wait_ge(*n(f"w_ready{k}", 16))

            def freed(ins, k):
                ins.then_inc(SEMS[f"w_free{k}"], 1)

            def norm_sum(t0=0, halves=2, width=H):
                pe.wait_ge(*n("sq_ready"))
                put(0, False)
                for h in range(halves):
                    for k in range(KD):
                        ins = mm(PS[0][:, h, 0:width], c("ones"), HN[:, k, t0 + h * width:t0 + (h + 1) * width],
                                 start=(k == 0), stop=(k == KD - 1))
                ins.then_inc(SEMS["act_full0"], 1)

            pe.wait_ge(SEMS["par_in"], 32)
            norm_sum()
            pe.wait_ge(*n("hn_ready"))
            with n.loop("uqk", 3) as i:
                for k in range(WSLOTS):
                    slot(k)
                    put(k)
                    for h in range(2):
                        for b in range(KD):
                            ins = mm(PS[k][:, h, 0:H], ring[:, k, b * P:b * P + P], HN[:, b, h * H:h * H + H],
                                     start=(b == 0), stop=(b == KD - 1))
                            if h == 0 and b == 0:
                                freed(ins, (k - 1) % 4)
                    ins.then_inc(SEMS[f"act_full{k}"], 1)
            for p in range(3):
                put(p)
            for b in range(KD):
                if b % 2 == 0:
                    slot(b // 2)
                for t, (q0, rows) in enumerate(TILES):
                    ins = mm(PS[t // 2][0:rows, t % 2, :], HN[:, b, q0:q0 + rows],
                             ring[:, b // 2, (b % 2) * 512:(b % 2) * 512 + 512], start=(b == 0), stop=(b == KD - 1))
                    if b % 2 == 0 and t == 0:
                        freed(ins, (b // 2 - 1) % 4)
                    if b == KD - 1 and t in (1, 3, 4):
                        ins.then_inc(SEMS[f"act_full{t // 2}"], 1)
            with n.loop("s5", 4) as i:
                def b_u(j):
                    slot((2 * j) % 4)
                    for r, p in ((0, 1), (1, 3)):
                        put(p)
                        for h in range(2):
                            ins = mm(PS[p][:, h, 0:H], ring[:, (2 * j) % 4, r * P:r * P + P],
                                     PJ[:, i, h * H:h * H + H], start=True, stop=True)
                            if r == 0 and h == 0:
                                freed(ins, (2 * j - 1) % 4)
                        ins.then_inc(SEMS[f"act_full{p}"], 1)

                b_u(0)
                for j in range(4):
                    k = (2 * j + 1) % 4
                    slot(k)
                    put(0)
                    for h in range(2):
                        for b in range(KD):
                            ins = mm(PS[0][:, h, 0:H], ring[:, k, b * P:b * P + P], HN[:, b, h * H:h * H + H],
                                     start=(b == 0), stop=(b == KD - 1))
                    ins.then_inc(SEMS["act_full0"], 1)
                    if j < 3:
                        b_u(j + 1)
                    if j == 0:
                        put(2)
                    pe.wait_ge(*n("s5_s"))
                    for h in range(2):
                        for r in range(2):
                            ins = mm(PS[2][:, h, 0:H], CW[:, r, :], SS[:, r, h * H:h * H + H],
                                     start=(j == 0 and r == 0), stop=(j == 3 and r == 1), skip_group_check=True)
                            if h == 0 and r == 0:
                                freed(ins, (2 * j) % 4)
                    ins.then_inc(SEMS["dve_full2"] if j == 3 else SEMS["s5_s_free"], 1)

            with n.loop("att", HEADS) as h:
                pe.wait_ge(*n("qk_sq"))
                for x in range(2):
                    put(x, False)
                    for hf in range(2):
                        ins = mm(PS[x][:, hf, 0:H], c("pair64"), SQ[:, x, hf * H:hf * H + H], start=True, stop=True)
                    ins.then_inc(SEMS[f"act_full{x}"], 1)
                pe.wait_ge(*n("qk_n"))
                for t in range(len(TILES) + 1):
                    if t < len(TILES):
                        q0, rows = TILES[t]
                        keys = q0 + rows
                        for j in range(2):
                            put(2 + j)
                            n.settle()
                            q = QS[64 * j:64 * j + 64, q0:q0 + rows]
                            kk = KS[64 * j:64 * j + 64, :]
                            ins = mm(PS[2 + j][0:rows, 0, 0:min(keys, 512)], q, kk[:, 0:min(keys, 512)], start=True, stop=True)
                            if keys > 512:
                                ins = mm(PS[2 + j][0:rows, 1, 0:keys - 512], q, kk[:, 512:keys], start=True, stop=True)
                            ins.then_inc(SEMS[f"dve_full{2 + j}"], 1)
                    if t:
                        q0, rows = TILES[t - 1]
                        pe.wait_ge(*n("w_comb"))
                        put(0, False)
                        n.settle()
                        for b in range(t):
                            k0 = TILES[b][0]
                            ins = nc.tensor.transpose(ps(0)[:, b * P:b * P + rows], WC[0:rows, k0:k0 + P],
                                                      c("ident", 0, rows, rows))
                        ins.then_inc(SEMS["act_full0"], 1)
                        pe.wait_ge(*n("wt_ready"))
                        put(1)
                        for b in range(t):
                            ins = mm(PS[1][0:rows, 0, 0:P], WT[:, b, 0:rows], V[:, b, bass.ds(h * P, P)],
                                     start=(b == 0), stop=(b == t - 1))
                        ins.then_inc(SEMS["act_full1"], 1)
                pe.wait_ge(*n("o_norm"))
                put(0)
                n.settle()
                for t, (q0, rows) in enumerate(TILES):
                    ins = nc.tensor.transpose(ps(0)[:, t * P:t * P + rows], OR[0:rows, t, :], c("ident", 0, rows, rows))
                ins.then_inc(SEMS["act_full0"], 1)

            pe.wait_ge(*n("ys_gelu"))
            for m in range(4):
                if m % 2 == 0:
                    slot(m // 2)
                put(m, False)
                for h in range(2):
                    for b in range(4):
                        w0 = (m % 2) * 512 + b * P
                        ins = mm(PS[m][:, h, 0:H], ring[:, m // 2, w0:w0 + P], PJ[:, b, h * H:h * H + H],
                                 start=(b == 0), stop=(b == 3))
                        if m % 2 == 0 and h == 0 and b == 0:
                            freed(ins, (m // 2 - 1) % 4)
                ins.then_inc(SEMS[f"act_full{m}"], 1)
            pe.wait_ge(*n("ys_ready"))
            with n.loop("mix", 2) as i:
                for k in range(WSLOTS):
                    s = (2 + k) % 4
                    slot(s)
                    for x in range(2):
                        p = 2 * (k % 2) + x
                        put(p)
                        for h in range(2):
                            for b in range(4):
                                src = PJ[:, (8 + b) if x == 0 else (4 + b), h * H:h * H + H]
                                ins = mm(PS[p][:, h, 0:H], ring[:, s, (4 * x + b) * P:(4 * x + b) * P + P], src,
                                         start=(b == 0), stop=(b == 3))
                                if x == 0 and h == 0 and b == 0:
                                    freed(ins, (s - 1) % 4)
                        ins.then_inc(SEMS[f"dve_full{p}"], 1)
            pe.wait_ge(*n("mix_ready"))
            with n.loop("wo", 2) as i:
                for k in range(WSLOTS):
                    s = (2 + k) % 4
                    slot(s)
                    put(k)
                    for h in range(2):
                        for b in range(KD):
                            ins = mm(PS[k][:, h, 0:H], ring[:, s, b * P:b * P + P], PJ[:, 12 + b, h * H:h * H + H],
                                     start=(b == 0), stop=(b == KD - 1))
                            if h == 0 and b == 0:
                                freed(ins, (s - 1) % 4)
                    ins.then_inc(SEMS[f"dve_full{k}"], 1)
            norm_sum()
            pe.wait_ge(*n("hn_ready"))
            with n.loop("up", NFF // 2) as i:
                for k in range(WSLOTS):
                    s = (2 + k) % 4
                    slot(s)
                    put(k)
                    for h in range(2 if k % 2 == 0 else 1):
                        for b in range(KD):
                            dst = PS[k][:, h, 0:257] if k % 2 == 0 else PS[k][:, 0, :]
                            src = HN[:, b, 14 + 257 * h:271 + 257 * h] if k % 2 == 0 else HN[:, b, NMETA:T]
                            ins = mm(dst, ring[:, s, b * P:b * P + P], src, start=(b == 0), stop=(b == KD - 1))
                            if h == 0 and b == 0:
                                freed(ins, (s - 1) % 4)
                    ins.then_inc(SEMS[f"act_full{k}" if k % 2 == 0 else f"dve_full{k}"], 1)
            pe.wait_ge(*n("hid_done"))
            for p in range(4):
                put(p)

            def down(s, k, start=False, stop=False):
                slot(s)
                for m in range(KD):
                    ins = mm(PS[m // 2][:, m % 2, :], ring[:, s, m * P:m * P + P], hid[:, k, :], start=start, stop=stop)
                    if m == 0:
                        freed(ins, (s - 1) % 4)
                    if stop and m % 2 == 1:
                        ins.then_inc(SEMS[f"dve_full{m // 2}"], 1)

            down(2, 0, start=True)
            down(3, 1)
            with n.loop("down", 4) as i:
                for k in range(WSLOTS):
                    down(k, i * 4 + (2 + k))
            for k in range(WSLOTS):
                down(k, NFF - 4 + k, stop=(k == 3))

            with n.loop("layer", LAYERS) as l:
                norm_sum(0, 1, 512)
                pe.wait_ge(*n("hn_ready"))

                def project(k, p):
                    slot(k)
                    put(p)
                    for b in range(KD):
                        ins = mm(PS[p][:, 0, :], ring[:, k, b * P:b * P + P], HN[:, b, 0:SEQ], start=(b == 0), stop=(b == KD - 1))
                        if b == 0:
                            freed(ins, (k - 1) % 4)
                    ins.then_inc(SEMS[f"act_full{p}"], 1)

                def gate(g, p):
                    project(g % WSLOTS, p)

                with n.loop("proj", 2) as i:
                    for k in range(WSLOTS):
                        project(k, k)
                for k in range(WSLOTS):
                    project(k, k)
                with n.loop("lag", 2) as i:
                    for k in range(8):
                        if k % 2 == 0:
                            project(k // 2, k // 2 % 2)
                        p = 2 + k % 2
                        pe.wait_ge(*n("b_m"))
                        put(p)
                        for cc in range(2):
                            ins = mm(PS[p][:, cc, :], c("pair64"), MB[:, k % 2, cc, :], start=True, stop=True)
                        ins.then_inc(SEMS[f"dve_full{p}"], 1)
                put(0)
                for t in range(4):
                    for cc in range(2):
                        o = (t * 2 + cc) * P
                        ins = nc.tensor.transpose(ps(0)[:, o:o + P], KH[:, cc, t * P:t * P + P], c("ident"))
                ins.then_inc(SEMS["act_full0"], 1)
                put(1)
                for t in range(4):
                    for cc in range(2):
                        o = (t * 2 + cc) * P
                        ins = nc.tensor.transpose(ps(1)[:, o:o + P], PJ2[:, 4 + cc, t * P:t * P + P], c("ident"))
                ins.then_inc(SEMS["act_full1"], 1)
                gate(0, 0)
                gate(1, 1)
                for t in range(4):
                    p = 2 + t % 2
                    pe.wait_ge(*n("b_ve"))
                    put(p)
                    for cc in range(2):
                        for hh in range(2):
                            ins = mm(PS[p][64 * hh:64 * hh + 64, cc, :], KHT[:, t, cc * P + 64 * hh:cc * P + 64 * hh + 64],
                                     VE[t % 2][:, (2 * cc + hh) * 512:(2 * cc + hh) * 512 + 512], start=True, stop=True)
                    ins.then_inc(SEMS[f"act_full{p}"], 1)
                pe.wait_ge(*n("a_ca"))
                put(1, False)
                for cc in range(2):
                    ins = mm(PS[1][:, 0, :], c("ones"), CA[:, cc, :], start=(cc == 0), stop=(cc == 1))
                ins.then_inc(SEMS["dve_full1"], 1)
                gate(2, 2)
                gate(3, 3)
                pe.wait_ge(*n("b_s"))
                pe.wait_ge(*n("qgz", 2))
                put(0)
                for cc in range(2):
                    us = (US0, US1)[cc].rearrange("p (v i) -> p v i", i=NBLK)
                    for i in range(1, NBLK):
                        for hh in range(2):
                            ins = mm(PS[0][64 * hh:64 * hh + 64, cc, LAG * i:LAG * i + LAG], us[:, :, i - 1],
                                     QZ[:, 2 * cc + hh, LAG * i:LAG * i + LAG], start=True, stop=True)
                ins.then_inc(SEMS["dve_full0"], 1)
                pe.wait_ge(*n("a_sq"))
                put(1, False)
                for cc in range(2):
                    ins = mm(PS[1][:, 1, :], c("ones"), SQA[:, cc, :], start=(cc == 0), stop=(cc == 1))
                ins.then_inc(SEMS["act_full1"], 1)
                pe.wait_ge(*n("b_sq"))
                put(2, False)
                for cc in range(2):
                    ins = mm(PS[2][:, cc, :], c("pair64"), MB[:, 0, cc, :], start=True, stop=True)
                ins.then_inc(SEMS["act_full2"], 1)
                gate(4, 0)
                gate(5, 3)
                pe.wait_ge(*n("a_h"))
                put(1)
                for m in range(2):
                    for b in range(2):
                        o = SWP + (2 * m + b) * P
                        ins = mm(PS[1][:, m, :], SW[:, o:o + P], CA[:, b, :], start=(b == 0), stop=(b == 1))
                ins.then_inc(SEMS["dve_full1"], 1)
                gate(6, 2)
                gate(7, 3)
                pe.wait_ge(*n("c_dt"))
                for g in range(2):
                    put(2 + g)
                    for e in range(2):
                        ins = mm(PS[2 + g][:, e, :], c("sel4", (2 * g + e) * P, P, 4), AC4[0:4, :], start=True, stop=True)
                    ins.then_inc(SEMS[f"act_full{2 + g}"], 1)
                put(0)
                n.settle()
                for t in range(4):
                    for x in range(2):
                        ins = nc.tensor.transpose(ps(0)[:, t * 8 + 4 * x:t * 8 + 4 * x + 4], (DT4, AC4)[x][0:4, t * P:t * P + P],
                                                  c("ident", 0, 4, 4))
                ins.then_inc(SEMS["act_full0"], 1)
                pe.wait_ge(*n("c_x"))
                put(1)
                for t in range(4):
                    for cc in range(2):
                        o = (t * 2 + cc) * P
                        ins = nc.tensor.transpose(ps(1)[:, o:o + P], PJ2[:, 10 + cc, t * P:t * P + P], c("ident"))
                ins.then_inc(SEMS["dve_full1"], 1)
                put(0)
                for t in range(4):
                    for cc in range(2):
                        o = (t * 2 + cc) * P
                        ins = nc.tensor.transpose(ps(0)[:, o:o + P], PJ2[:, 12 + cc, t * P:t * P + P], c("ident"))
                ins.then_inc(SEMS["act_full0"], 1)
                put(3)
                for g in range(2):
                    for t in range(4):
                        ts_ = slice(t * P, t * P + P)
                        ins = mm(PS[3][:, g, ts_], PJ2[:, 12 + g, ts_], PJ2[:, 14 + g, ts_], start=True, stop=True)
                ins.then_inc(SEMS["dve_full3"], 1)
                pe.wait_ge(*n("c_wx"))
                pe.wait_ge(*n("c_bt"))
                put(2)
                for t in range(3):
                    for g in range(2):
                        o = (t * 2 + g) * P
                        ins = mm(ps(2)[:, o:o + P], BT[:, t, g * P:g * P + P],
                                 WX[:, t, 2 * g:2 * g + 2, :].rearrange("p a b -> p (a b)"), start=True, stop=True)
                ins.then_inc(SEMS["dve_full2"], 1)
                pe.wait_ge(*n("c_hs"))
                pe.wait_ge(*n("c_cme"))
                pe.wait_ge(*n("c_sc"))
                put(0)
                for h in range(HEADS):
                    g, e = h // 2, h % 2
                    for t in range(4):
                        ts_ = slice(t * P, t * P + P)
                        o = PS[0][64 * e:64 * e + 64, g, ts_]
                        ins = mm(o, XDT[:, t, h, :], DD[:, h, ts_], start=True, stop=(t == 0))
                        if t:
                            ins = mm(o, HS[:, t - 1, h * 64:h * 64 + 64], CME[:, h, ts_], start=False, stop=True)
                ins.then_inc(SEMS["dve_full0"], 1)
                pe.wait_ge(*n("c_sq"))
                put(1, False)
                for g in range(2):
                    ins = mm(PS[1][:, g, :], c("ones"), SQC[:, g, :], start=True, stop=True)
                ins.then_inc(SEMS["act_full1"], 1)
                pe.wait_ge(*n("d_sq"))
                put(0, False)
                for b in range(2):
                    mm(PS[0][:, 0, :], c("ones"), SQD[:, b, :], start=(b == 0), stop=(b == 1))
                mm(PS[0][:, 1, :], c("ones"), SQD[:, 2, :], start=True, stop=True).then_inc(SEMS["act_full0"], 1)
                put(1)
                mm(PS[1][:, 0, :], c("rot"), PJ2[:, 16, :], start=True, stop=True).then_inc(SEMS["dve_full1"], 1)
                pe.wait_ge(*n("d_n"))
                for h in range(HEADS):
                    p = 2 + h % 2
                    put(p)
                    for b in range(2):
                        mm(PS[p][0:QKR, 0, :], SW[:, SWQ + (2 * h + b) * QKR:SWQ + (2 * h + b + 1) * QKR], CQ[:, b, :],
                           start=(b == 0), stop=(b == 1))
                    for b in range(2):
                        ins = mm(PS[p][64:96, 1, :], SW[:, SWR + (2 * h + b) * 32:SWR + (2 * h + b + 1) * 32], CQ[:, b, :],
                                 start=(b == 0), stop=(b == 1))
                    ins.then_inc(SEMS[f"dve_full{p}"], 1)
                    if h % 2 == 1:
                        put(0)
                        for x in range(2):
                            hk = SWK + (h - 1 + x) * 64
                            ins = mm(PS[0][0:64, x, :], SW[:, hk:hk + 64], CK[:, :], start=True, stop=True)
                        ins.then_inc(SEMS["act_full0"], 1)
                put(1)
                for t in range(4):
                    ins = mm(ps(1)[:, t * 256:t * 256 + 256], CK[:, t * P:t * P + P], SW[:, SWV:SWV + 256], start=True, stop=True)
                ins.then_inc(SEMS["act_full1"], 1)
                pe.wait_ge(*n("d_v"))
                with n.loop("mla", HEADS) as h:
                    pe.wait_ge(*n("qst"))
                    for t in range(5):
                        if t < 4:
                            p = 2 + t % 2
                            put(p)
                            mm(PS[p][:, 0, 0:t * P + P], QST[0:QKR, t * P:t * P + P], KF[0:QKR, h, 0:t * P + P],
                               start=True, stop=True).then_inc(SEMS[f"dve_full{p}"], 1)
                        if t:
                            u = t - 1
                            pe.wait_ge(*n("d_ex"))
                            put(0, False)
                            for b in range(t):
                                ins = nc.tensor.transpose(PS[0][:, 0, b * P:b * P + P], SD[:, u % 2, b * P:b * P + P], c("ident"))
                            ins.then_inc(SEMS["act_full0"], 1)
                            pe.wait_ge(*n("d_wt"))
                            put(1)
                            for b in range(t):
                                ins = mm(PS[1][:, 0, 0:64], WD[:, b, :], VD[:, b, bass.ds(h * 64, 64)],
                                         start=(b == 0), stop=(b == t - 1))
                            ins.then_inc(SEMS["dve_full1"], 1)
                pe.wait_ge(*n("d_o", 4 * HEADS))
                put(0)
                for cc in range(2):
                    for t in range(4):
                        ins = nc.tensor.transpose(PS[0][:, cc, t * P:t * P + P], OD[:, t, cc * P:cc * P + P], c("ident"))
                ins.then_inc(SEMS["dve_full0"], 1)
                pe.wait_ge(*n("y_ready"))
                with n.loop("wout", 2) as i:
                    for k in range(WSLOTS):
                        slot(k)
                        put(k)
                        for b in range(KD):
                            ins = mm(PS[k][:, 0, :], ring[:, k, b * P:b * P + P], PJ2[:, 20 + b, :], start=(b == 0), stop=(b == KD - 1))
                            if b == 0:
                                freed(ins, (k - 1) % 4)
                        ins.then_inc(SEMS[f"act_full{k}"], 1)
                pe.wait_ge(*n("y_sq"))
                put(0, False)
                for k in range(KD):
                    ins = mm(PS[0][:, 0, :], c("ones"), PJ2[:, k, :], start=(k == 0), stop=(k == KD - 1))
                ins.then_inc(SEMS["act_full0"], 1)

        @block.scalar
        def _(act):
            n = Tally("act", act, SEMS)
            af = nc.scalar.activation

            def step(ins):
                ins.then_inc(SEMS["act_step"], 1)
                act.wait_ge(*n("act_step"))

            def mark(name):
                n.settle()
                act.drain().then_inc(SEMS[name], 1)

            act.wait_ge(SEMS["x_in"], 16 * KD)
            act.wait_ge(SEMS["eps_ready"], 1)

            def norm(src, nb=2, width=H):
                af(HN[:, :, 0:nb * width], src, ACT.Square).then_inc(SEMS["sq_ready"], 1)
                act.wait_ge(*n("act_full0"))
                af(R[:, 0:nb * width].rearrange("p (a b) -> p a b", a=nb), PS[0][:, 0:nb, 0:width], ACT.Sqrt,
                   bias=epsc[:, 0:1], scale=1.0 / D).then_inc(SEMS["rms_root"], 1)

            norm(X[:, :, :])
            act.wait_ge(SEMS["par_in"], 32)
            af(s5c[:, 0, :], par1[:, V1["ldt"][0]:V1["ldt"][1]], ACT.Exp).then_inc(SEMS["s5_dt"], 1)
            act.wait_ge(*n("trig_arg"))
            af(s5c[:, 2, :], s5c[:, 2, :], ACT.Exp)
            af(lamc[:, 2:4], lamc[:, 0:2], ACT.Exp)
            af(s5c[:, 3, :], s5c[:, 3, :], ACT.Sin)
            af(s5c[:, 4, :], s5c[:, 4, :], ACT.Sin).then_inc(SEMS["trig"], 1)
            with n.loop("uqk", 3) as i:
                for k in range(WSLOTS):
                    act.wait_ge(*n(f"act_full{k}"))
                    af(two(PJ[:, i * 4 + k, :]), halves(k), ACT.Copy).then_inc(SEMS[f"free{k}"], 1)
            mark("u_ready")
            act.wait_ge(*n("v_zero"))
            for t, (q0, rows) in enumerate(TILES):
                if t % 2 == 0:
                    act.wait_ge(*n(f"act_full{t // 2}"))
                ins = af(V[0:rows, t, :], PS[t // 2][0:rows, t % 2, :], ACT.Copy)
                if t in (1, 3, 4):
                    ins.then_inc(SEMS[f"free{t // 2}"], 1)
            mark("v_ready")
            with n.loop("s5", 4) as i:
                def x_out(j):
                    act.wait_ge(*n("s5_x_free"))
                    for r, p in ((0, 1), (1, 3)):
                        act.wait_ge(*n(f"act_full{p}"))
                        af(two(XS[:, j % 2, r, :]), halves(p), ACT.Copy).then_inc(SEMS[f"free{p}"], 1)
                    mark("s5_x")

                x_out(0)
                for j in range(4):
                    act.wait_ge(*n("act_full0"))
                    af(two(PJ[:, i * 4 + (12 + j), :]), halves(0), ACT.Tanh, scale=0.5).then_inc(SEMS["free0"], 1)
                    if j < 3:
                        x_out(j + 1)
            act.wait_ge(*n("s5_y"))
            af(PJ[:, 0:4, :], PJ[:, 0:4, :], ACT.Gelu_apprx_tanh).then_inc(SEMS["ys_gelu"], 1)
            with n.loop("att", HEADS) as h:
                af(SQ[:, 0, :], PJ[:, h + 4, :], ACT.Square)
                af(SQ[:, 1, :], PJ[:, h + 8, :], ACT.Square).then_inc(SEMS["qk_sq"], 1)
                for x in range(2):
                    act.wait_ge(*n(f"act_full{x}"))
                    ins = af(two(RT[:, x, :]), halves(x), ACT.Sqrt, bias=epsc[:, 0:1], scale=1.0 / 64)
                ins.then_inc(SEMS["qk_root"], 1)
                for t in range(len(TILES) + 1):
                    if t < len(TILES):
                        q0, rows = TILES[t]
                        keys = q0 + rows
                        act.wait_ge(*n("sc_ready"))
                        for j in range(2):
                            s = SX[0:rows, t % 2, j, 0:keys]
                            col = 2 * (t % 2) + j
                            af(s, s, ACT.Exp, bias=st[0:rows, col:col + 1], accum_out=st[0:rows, 4 + col:5 + col])
                        mark("ex_ready")
                    if t:
                        q0, rows = TILES[t - 1]
                        act.wait_ge(*n("act_full0"))
                        if t > 1:
                            af(WT[:, 1:t, 0:rows], ps(0)[:, P:t * P].rearrange("p (a b) -> p a b", b=P)[:, :, 0:rows], ACT.Copy)
                        af(WT[0:NMETA, 0, 0:rows], ps(0)[0:NMETA, 0:rows], ACT.Copy).then_inc(SEMS["wt_ready"], 1)
                        act.wait_ge(*n("act_full1"))
                        af(JK[0:rows, 0:P], PS[1][0:rows, 0, 0:P], ACT.Square, accum_out=st[0:rows, 15 + t:16 + t])
                        af(OR[0:rows, t - 1, :], PS[1][0:rows, 0, 0:P], ACT.Copy).then_inc(SEMS["free1"], 1)
                n.settle()
                step(act.drain())
                af(st[:, 24:29], st[:, 16:21], ACT.Sqrt, bias=epsc[:, 0:1], scale=1.0 / P).then_inc(SEMS["o_root"], 1)
                act.wait_ge(*n("act_full0"))
                n.settle()
                af(PJ[:, h + 4, 0:NMETA], ps(0)[:, 0:NMETA], ACT.Copy, scale=lamc[:, 6:7])
                af(PJ[:, h + 4, NMETA:T], ps(0)[:, P:P + SEQ], ACT.Copy, scale=lamc[:, 6:7]).then_inc(SEMS["free0"], 1)
            for m in range(4):
                act.wait_ge(*n(f"act_full{m}"))
                af(two(TH[:, m, :]), halves(m), ACT.Tanh, scale=0.5, bias=glub2[:, m:m + 1]).then_inc(SEMS["glu_th"], 1)
            act.wait_ge(*n("h_ready"))
            norm(X[:, :, :])
            with n.loop("up", NFF // 2) as i:
                for m in range(2):
                    act.wait_ge(*n(f"act_full{2 * m}"))
                    af(FA[:, :].rearrange("p (a b) -> p a b", a=2), PS[2 * m][:, :, 0:257], ACT.Copy).then_inc(SEMS["ffa"], 1)
                    act.wait_ge(*n("ffc"))
                    af(GL[:, :], CV[:, :], ACT.Gelu_apprx_tanh).then_inc(SEMS["ffg"], 1)

            with n.loop("layer", LAYERS) as l:
                act.wait_ge(*n("x2_ready"))
                norm(XK, 1, 512)

                def evac(dst, p):
                    act.wait_ge(*n(f"act_full{p}"))
                    n.settle()
                    af(dst, PS[p][:, 0, :], ACT.Copy).then_inc(SEMS[f"free{p}"], 1)

                with n.loop("proj", 2) as i:
                    for k in range(WSLOTS):
                        evac(PJ2[:, i * 4 + k, :], k)
                n.settle()
                step(act.drain())
                act.wait_ge(*n("lb_arg"))
                af(LB[:, 4:6], LB[:, 4:6], ACT.Tanh, scale=0.5).then_inc(SEMS["lb_th"], 1)
                af(PJ2[:, 0:2, :], PJ2[:, 0:2, :], ACT.Tanh, scale=0.5).then_inc(SEMS["b_th"], 1)
                for k in range(WSLOTS):
                    evac(PJ2[:, 8 + k, :], k)
                n.settle()
                step(act.drain())
                af(PJ2[:, 8:10, :], PJ2[:, 8:10, :], ACT.Tanh, scale=0.5).then_inc(SEMS["a_th"], 1)
                with n.loop("lag", 2) as i:
                    for k in range(WSLOTS):
                        evac(PJ2[:, i * 4 + (12 + k), :], k % 2)
                n.settle()
                step(act.drain())
                act.wait_ge(*n("act_full0"))
                af(KHT.rearrange("p a b -> p (a b)"), ps(0), ACT.Copy).then_inc(SEMS["free0"], 1)
                act.wait_ge(*n("act_full1"))
                af(VT.rearrange("p a b -> p (a b)"), ps(1), ACT.Copy).then_inc(SEMS["free1"], 1)
                mark("b_tok")
                evac(PJ2[:, GATES[0], :], 0)
                evac(PJ2[:, GATES[1], :], 1)
                for t in range(4):
                    p = 2 + t % 2
                    act.wait_ge(*n(f"act_full{p}"))
                    for cc in range(2):
                        us = (US0, US1)[cc].rearrange("p (v i) -> p i v", i=NBLK)
                        ins = af(us[:, 8 * t:8 * t + 8, :], PS[p][:, cc, :].rearrange("p (i v) -> p i v", i=8), ACT.Copy)
                    ins.then_inc(SEMS[f"free{p}"], 1)
                    mark("b_us")
                evac(PJ2[:, GATES[2], :], 2)
                evac(PJ2[:, GATES[3], :], 3)
                act.wait_ge(*n("a_xc"))
                af(SQA[:, :, :], CA[:, :, :], ACT.Square).then_inc(SEMS["a_sq"], 1)
                n.settle()
                step(act.drain())
                act.wait_ge(*n("b_s"))
                af(FREE[0], PJ2[:, 22:26, :], ACT.Tanh, scale=0.5).then_inc(SEMS["gate_th"], 1)
                act.wait_ge(*n("b_acc2"))
                af(MB[:, 0, :, :], ACC[:, :, :], ACT.Square).then_inc(SEMS["b_sq"], 1)
                act.wait_ge(*n("act_full1"))
                af(RA, PS[1][:, 1, :], ACT.Sqrt, bias=epsc[:, 1:2], scale=1.0 / 256).then_inc(SEMS["a_root"], 1)
                act.wait_ge(*n("act_full2"))
                af(RB[:, :, :], PS[2][:, :, :], ACT.Sqrt, bias=epsc[:, 0:1], scale=1.0 / 64).then_inc(SEMS["b_root"], 1)
                act.wait_ge(*n("a_x"))
                af(SQA[:, :, :], CA[:, :, :], ACT.Tanh, scale=0.5).then_inc(SEMS["a_xt"], 1)
                evac(PJ2[:, GATES[4], :], 0)
                evac(PJ2[:, GATES[5], :], 3)
                act.wait_ge(*n("c_dtabs"))
                step(af(DD[0:4, 0, :], DD[0:4, 0, :], ACT.Exp, scale=-1.0))
                af(LB2[0:4, 0:1], v2("alog", rows=4), ACT.Exp)
                af(DD[0:4, 0, :], DD[0:4, 0, :], ACT.Ln, bias=epsc[0:4, 2:3]).then_inc(SEMS["c_dtln"], 1)
                evac(PJ2[:, GATES[6], :], 2)
                evac(PJ2[:, GATES[7], :], 3)
                n.settle()
                step(act.drain())
                for x in (0, 1):
                    ins = af(FREE[1][:, 2 * x:2 * x + 2, :], PJ2[:, (20, 26)[x]:(22, 28)[x], :], ACT.Tanh, scale=0.5)
                ins.then_inc(SEMS["gate_th"], 1)
                act.wait_ge(*n("c_cx"))
                af(PJ2[:, 10:16, :], CX[:, :, :], ACT.Tanh).then_inc(SEMS["c_th"], 1)
                for g in range(2):
                    act.wait_ge(*n(f"act_full{2 + g}"))
                    af(EAB[:, 2 * g:2 * g + 2, :], PS[2 + g][:, :, :], ACT.Exp)
                    af(ACB[:, 2 * g:2 * g + 2, :], PS[2 + g][:, :, :], ACT.Copy).then_inc(SEMS[f"free{2 + g}"], 1)
                act.wait_ge(*n("act_full0"))
                af(COL.rearrange("p a b -> p (a b)"), ps(0)[:, 0:32], ACT.Copy).then_inc(SEMS["free0"], 1)
                mark("c_acb")
                act.wait_ge(*n("act_full0"))
                af(BT.rearrange("p a b -> p (a b)"), ps(0), ACT.Copy).then_inc(SEMS["free0"], 1)
                mark("c_bt")
                act.wait_ge(*n("c_wd"))
                af(WCOL[:, :, :], WCOL[:, :, :], ACT.Exp).then_inc(SEMS["c_we"], 1)
                act.wait_ge(*n("c_d"))
                af(DD[:, :, :], DD[:, :, :], ACT.Exp).then_inc(SEMS["c_de"], 1)
                act.wait_ge(*n("c_yc"))
                af(SQC[:, :, :], YC[:, :, :], ACT.Square).then_inc(SEMS["c_sq"], 1)
                act.wait_ge(*n("act_full1"))
                af(RC[:, :, :], PS[1][:, :, :], ACT.Sqrt, bias=epsc[:, 0:1], scale=1.0 / P).then_inc(SEMS["c_root"], 1)
                act.wait_ge(*n("c_done"))
                af(SQD[:, 0:2, :], PJ2[:, 18:20, :], ACT.Square)
                af(SQD[:, 2, :], PJ2[:, 17, :], ACT.Square).then_inc(SEMS["d_sq"], 1)
                act.wait_ge(*n("act_full0"))
                af(RD[:, 0, :], PS[0][:, 0, :], ACT.Sqrt, bias=epsc[:, 0:1], scale=1.0 / 256)
                af(RD[:, 1, :], PS[0][:, 1, :], ACT.Sqrt, bias=epsc[:, 0:1], scale=1.0 / P).then_inc(SEMS["d_root"], 1)
                act.wait_ge(*n("d_trig_arg"))
                af(COS, COS, ACT.Sin)
                af(SIN, SIN, ACT.Sin).then_inc(SEMS["d_trig"], 1)
                for g in range(2):
                    act.wait_ge(*n("act_full0"))
                    af(KF[0:64, 2 * g:2 * g + 2, :], PS[0][0:64, :, :], ACT.Copy).then_inc(SEMS["free0"], 1)
                act.wait_ge(*n("act_full1"))
                af(VD.rearrange("p a b -> p (a b)"), ps(1), ACT.Copy).then_inc(SEMS["free1"], 1)
                act.wait_ge(*n("d_kr"))
                for h in range(HEADS):
                    af(KF[64:QKR, h, :], KR[64:QKR, :], ACT.Copy)
                mark("d_v")
                act.wait_ge(*n("d_q"))
                with n.loop("mla", HEADS) as h:
                    af(QST[0:QKR, :], QF[0:QKR, h, :], ACT.Copy).then_inc(SEMS["qst"], 1)
                    for t in range(5):
                        if t < 4:
                            act.wait_ge(*n("d_sc"))
                            x = SD[:, t % 2, 0:t * P + P]
                            af(x, x, ACT.Exp, bias=sd[:, t % 2:t % 2 + 1], scale=QKR ** -0.5, accum_out=sd[:, 2 + t % 2:3 + t % 2])
                            mark("d_ex")
                        if t:
                            act.wait_ge(*n("act_full0"))
                            if t > 1:
                                act.wait_ge(*n("d_o"))
                            af(WD[:, 0:t, :], PS[0][:, 0, 0:t * P].rearrange("p (a b) -> p a b", b=P), ACT.Copy).then_inc(SEMS["d_wt"], 1)
                    act.wait_ge(*n("d_o"))
                with n.loop("wout", 2) as i:
                    for k in range(WSLOTS):
                        act.wait_ge(*n(f"act_full{k}"))
                        af(HNY[:, i * 4 + k, :], PS[k][:, 0, :], ACT.Copy).then_inc(SEMS[f"free{k}"], 1)
                n.settle()
                step(act.drain())
                af(PJ2[:, 0:KD, :], HNY, ACT.Square).then_inc(SEMS["y_sq"], 1)
                act.wait_ge(*n("act_full0"))
                af(R[:, 0:SEQ], PS[0][:, 0, :], ACT.Sqrt, bias=epsc[:, 0:1], scale=1.0 / D).then_inc(SEMS["rms_root"], 1)

        @block.gpsimd
        def _(pool):
            n = Tally("pool", pool, SEMS)
            tt = nc.gpsimd.tensor_tensor
            pool.wait_ge(*n("s5_tab"))
            A4 = ph_a.rearrange("p r (c b) -> p r c b", b=8)
            B4 = ph_b.rearrange("p r (c j) -> p r c j", j=66)

            def step(ins):
                ins.then_inc(SEMS["pool_step"], 1)
                pool.wait_ge(*n("pool_step"))

            with n.loop("s5", 4) as i:
                for j in range(4):
                    pool.wait_ge(*n("s5_x_free"))

                    def outer(dst, r, s):
                        x = A4[:, r, i * 4 + j, :].unsqueeze(2).broadcast_to([P, 8, 66])
                        y = B4[:, s, i * 4 + j, :].unsqueeze(1).broadcast_to([P, 8, 66])
                        return tt(dst.rearrange("p (b j) -> p b j", b=8), x, y, ALU.mult)

                    outer(PH[:, j % 2, 0, :], 0, 0)
                    outer(PT[:, 0, :], 1, 1)
                    outer(PH[:, j % 2, 1, :], 0, 1)
                    step(outer(PT[:, 1, :], 1, 0))
                    tt(PH[:, j % 2, 0, :], PH[:, j % 2, 0, :], PT[:, 0, :], ALU.subtract)
                    tt(PH[:, j % 2, 1, :], PH[:, j % 2, 1, :], PT[:, 1, :], ALU.add).then_inc(SEMS["s5_ph"], 1)
                    pool.wait_ge(*n("s5_ph"))

            with n.loop("layer", LAYERS) as l:
                pool.wait_ge(*n("x2_ready"))
                pool.dma_start(SW[:, :], a["small"][l]).then_inc(SEMS["small_in"], 16)
                pool.wait_ge(*n("b_kh"))
                n.settle()
                nc.gpsimd.memset(ACC[:, :, :], 0.0)
                n.settle()
                step(pool.drain())
                for _ in range(2):
                    pool.sem_inc(SEMS["b_acc"], 1)
                with n.loop("lag", 2) as i:
                    for k in range(8):
                        pool.wait_ge(*n("b_m"))
                        s0 = i * (-8) + (LAG - k)
                        step(tt(EE[:, :, :], EE[:, :, :], FZ[:, :, bass.ds(s0, SEQ)], ALU.mult))
                        pool.sem_inc(SEMS["b_e"], 1)
                        pool.wait_ge(*n("b_t"))
                        step(tt(ACC[:, :, :], ACC[:, :, :], TM[:, k % 2, :, :], ALU.add))
                        pool.sem_inc(SEMS["b_acc"], 1)
                step(nc.gpsimd.memset(QZ[:, :, :], 0.0))
                for hh in range(2):
                    r = slice(64 * hh, 64 * hh + 64)
                    n.settle()
                    nc.gpsimd.tensor_copy(QZ[r, hh::2, :], QG[r, :, :]).then_inc(SEMS["qgz"], 1)
                    pool.wait_ge(*n("qgz"))
                pool.wait_ge(*n("b_tok"))
                for t in range(4):
                    if t > 1:
                        pool.wait_ge(*n("b_us"))
                    x = VT[:, t, :].rearrange("p (h v) -> p h v", h=4).unsqueeze(2).broadcast_to([P, 4, 8, 64])
                    y = c("blk8").unsqueeze(1).unsqueeze(3).broadcast_to([P, 4, 8, 64])
                    tt(VE[t % 2].rearrange("p (h i v) -> p h i v", h=4, i=8), x, y, ALU.mult).then_inc(SEMS["b_ve"], 1)
                for t in range(2):
                    pool.wait_ge(*n("b_us"))
                for cc in range(2):
                    z = DZ[cc].rearrange("p (v i) -> p v i", i=NBLK)
                    n.settle()
                    ins = nc.gpsimd.tensor_copy(z, DL[:, cc, :].unsqueeze(1).broadcast_to([P, 64, NBLK]))
                ins.then_inc(SEMS["b_dz"], 1)
                pool.wait_ge(*n("c_acb"))
                pool.wait_ge(*n("c_x"))
                x = PJ2[:, 14:16, :].unsqueeze(2).broadcast_to([P, 2, 2, SEQ])
                tt(CME.rearrange("p (g e) t -> p g e t", g=2), EAB.rearrange("p (g e) t -> p g e t", g=2), x, ALU.mult)\
                    .then_inc(SEMS["c_cme"], 1)

        @block.vector
        def _(dve):
            n = Tally("dve", dve, SEMS)
            v = nc.vector
            tt, stt, ts = v.tensor_tensor, v.scalar_tensor_tensor, v.tensor_scalar

            def link(ins):
                ins.then_inc(SEMS["dve_step"], 1)
                dve.wait_ge(*n("dve_step"))

            def mark(name):
                n.settle()
                dve.drain().then_inc(SEMS[name], 1)

            def post(name):
                dve.sem_inc(SEMS[name], 1)

            def join():
                n.settle()
                link(dve.drain())

            v.memset(epsc[:, 0:1], EPS)
            v.memset(epsc[:, 1:2], 1e-5)
            v.memset(epsc[:, 2:3], 1.0)
            v.memset(V[:, 0, :], 0.0)
            v.memset(junk[:, :], 0.0).then_inc(SEMS["eps_ready"], 1)
            mark("v_zero")
            for p in range(4):
                dve.sem_inc(SEMS[f"free{p}"], 1)

            def norm(x, gain, width, t0=0):
                dve.wait_ge(*n("rms_root"))
                link(v.reciprocal(R[:, 0:width], R[:, 0:width]))
                for k in range(KD):
                    ins = stt(HN[:, k, 0:width], x[:, k, :], gain(k), R[:, 0:width], ALU.mult, ALU.mult)
                ins.then_inc(SEMS["hn_ready"], 1)

            dve.wait_ge(SEMS["par_in"], 32)
            dve.wait_ge(SEMS["x_in"], 16 * KD)
            norm(X[:, :, :], lambda k: v1("g1", k), T)
            dt, mag, sin, cos = (s5c[:, k, :] for k in (0, 2, 3, 4))
            are, aim = (par1[:, V1[k][0]:V1[k][1]] for k in ("are", "aim"))
            lam0 = V1["lam"][0]
            lamv = par1[:, lam0:lam0 + 256].rearrange("p (a b c) -> p a b c", a=2, b=2)
            link(tt(TMP[:, 0, 0:128].rearrange("p (a c) -> p a c", a=2), lamv[:, :, 0, :], lamv[:, :, 1, :], ALU.mult))
            v.tensor_reduce(lamc[:, 0:2], TMP[:, 0, 0:128].rearrange("p (a c) -> p a c", a=2), AX.X, ALU.add)
            ts(lamc[:, 5:6], v1("qg"), 0.125, None, ALU.mult)
            ts(lamc[:, 6:7], v1("subg"), 1.0 - LAM_INIT, None, ALU.mult)
            ts(glub2[:, :], par1[:, V1["glub"][0]:V1["glub"][1]], 0.5, None, ALU.mult)
            dve.wait_ge(SEMS["s5_dt"], 1)
            tt(mag, are, dt, ALU.mult)
            t5, t6 = s5c[:, 5, :], s5c[:, 6, :]
            link(tt(t5, aim, dt, ALU.mult))
            link(ts(t6, t5, 1.0 / (2 * np.pi), MAGIC, ALU.mult, ALU.add))
            link(ts(t6, t6, -MAGIC, None, ALU.add))
            for part in PI2:
                link(stt(t5, t6, -part, t5, ALU.mult, ALU.add))
            link(ts(cos, t5, float(np.pi / 2), None, ALU.add))
            link(ts(t6, cos, float(np.pi), -2 * float(np.pi), ALU.is_gt, ALU.mult))
            link(tt(cos, cos, t6, ALU.add))
            ts(cos, cos, PIF, -PIF, ALU.min, ALU.max)
            ts(sin, t5, PIF, -PIF, ALU.min, ALU.max).then_inc(SEMS["trig_arg"], 1)
            dve.wait_ge(*n("trig"))
            link(tt(lamc[:, 4:5], lamc[:, 2:3], lamc[:, 3:4], ALU.subtract))
            link(ts(lamc[:, 4:5], lamc[:, 4:5], LAM_INIT, None, ALU.add))
            ts(lamc[:, 4:5], lamc[:, 4:5], -1.0, None, ALU.mult)
            lr, li, fr, nfi, nfr, w = (s5c[:, k, :] for k in (6, 7, 8, 9, 10, 11))
            link(tt(lr, mag, cos, ALU.mult))
            tt(li, mag, sin, ALU.mult)
            link(ts(lr, lr, -1.0, None, ALU.add))
            tt(fr, lr, are, ALU.mult)
            link(tt(w, li, aim, ALU.mult))
            tt(fr, fr, w, ALU.add)
            link(tt(nfi, lr, aim, ALU.mult))
            link(tt(w, li, are, ALU.mult))
            tt(nfi, nfi, w, ALU.subtract)
            link(tt(t5, are, are, ALU.mult))
            link(tt(w, aim, aim, ALU.mult))
            link(tt(w, t5, w, ALU.add))
            link(v.reciprocal(w, w))
            link(tt(fr, fr, w, ALU.mult))
            tt(nfi, nfi, w, ALU.mult)
            link(ts(nfr, fr, -1.0, None, ALU.mult))

            B4 = ph_b.rearrange("p r (c j) -> p r c j", j=66)
            A4 = ph_a.rearrange("p r (c j) -> p r c j", j=8)
            E1 = TMP[:, 2, 0:32].rearrange("p (r c) -> p r c", r=2)
            E2 = TMP[:, 3, 0:32].rearrange("p (r c) -> p r c", r=2)

            def cmul(o, x, y, ta, tb):
                tt(o[0], x[0], y[0], ALU.mult)
                tt(ta, x[1], y[1], ALU.mult)
                tt(o[1], x[0], y[1], ALU.mult)
                link(tt(tb, x[1], y[0], ALU.mult))
                tt(o[0], o[0], ta, ALU.subtract)
                link(tt(o[1], o[1], tb, ALU.add))

            v.tensor_copy(E1[:, 0, :], cos)
            link(v.tensor_copy(E1[:, 1, :], sin))
            for tab in (B4, A4):
                v.memset(tab[:, 0, :, 0:1], 1.0)
                v.memset(tab[:, 1, :, 0:1], 0.0)
            join()

            def tmp3(k, m):
                return TMP[:, k, 0:16 * m].rearrange("p (c j) -> p c j", j=m)

            def double(tab, size, e, e2):
                m = 1
                while m < size:
                    w_ = min(m, size - m)
                    bc = [e[:, r, :].unsqueeze(2).broadcast_to([P, 16, w_]) for r in range(2)]
                    cmul([tab[:, r, :, m:m + w_] for r in range(2)], [tab[:, r, :, 0:w_] for r in range(2)], bc,
                         tmp3(0, w_), tmp3(1, w_))
                    if 2 * m < size:
                        cmul([e2[:, r, :] for r in range(2)], [e[:, r, :] for r in range(2)],
                             [e[:, r, :] for r in range(2)], TMP[:, 0, 0:16], TMP[:, 1, 0:16])
                        e, e2 = e2, e
                    m *= 2

            first = junkE[:, :].rearrange("p (r c) -> p r c", r=2)
            link(v.tensor_copy(first, E1))
            double(B4, 66, E1, E2)
            cmul([E1[:, r, :] for r in range(2)], [B4[:, r, :, 65] for r in range(2)],
                 [first[:, r, :] for r in range(2)], TMP[:, 0, 0:16], TMP[:, 1, 0:16])
            double(A4, 8, E1, E2)
            mark("s5_tab")
            for _ in range(2):
                mark("s5_x_free")
            dve.wait_ge(*n("u_ready"))
            with n.loop("s5", 4) as i:
                for j in range(4):
                    pr, pi = PH[:, j % 2, 0, :], PH[:, j % 2, 1, :]
                    xr, xi = XS[:, j % 2, 0, :], XS[:, j % 2, 1, :]
                    t0, t1, t2, t3 = (TMP[:, k, :] for k in range(4))
                    dve.wait_ge(*n("s5_ph"))
                    dve.wait_ge(*n("s5_x"))
                    tt(t0, pr, xr, ALU.mult)
                    tt(t1, pi, xi, ALU.mult)
                    tt(t2, pr, xi, ALU.mult)
                    link(tt(t3, pi, xr, ALU.mult))
                    tt(t0, t0, t1, ALU.add)
                    link(tt(t2, t2, t3, ALU.subtract))
                    decay = mag[:, bass.ds(i * 4 + j, 1)].broadcast_to([P, T])
                    v.tensor_tensor_scan(t1, decay, t0, 0.0, ALU.mult, ALU.add)
                    link(v.tensor_tensor_scan(t3, decay, t2, 0.0, ALU.mult, ALU.add))
                    if j:
                        dve.wait_ge(*n("s5_s_free"))
                    craw = ring[:, (2 * j) % 4, 256:512].rearrange("p (r c) -> p r c", r=2)
                    f1, f2, f3 = (x[:, bass.ds(i * 4 + j, 1)] for x in (fr, nfi, nfr))
                    tt(SS[:, 0, :], pr, t1, ALU.mult)
                    tt(SS[:, 1, :], pr, t3, ALU.mult)
                    tt(t0, pi, t3, ALU.mult)
                    ts(CW[:, 0, :], craw[:, 1, :], f2, None, ALU.mult)
                    ts(CW[:, 1, :], craw[:, 0, :], f2, None, ALU.mult)
                    link(tt(t2, pi, t1, ALU.mult))
                    stt(CW[:, 0, :], craw[:, 0, :], f1, CW[:, 0, :], ALU.mult, ALU.add)
                    stt(CW[:, 1, :], craw[:, 1, :], f3, CW[:, 1, :], ALU.mult, ALU.add)
                    tt(SS[:, 0, :], SS[:, 0, :], t0, ALU.subtract)
                    tt(SS[:, 1, :], SS[:, 1, :], t2, ALU.add).then_inc(SEMS["s5_s"], 1)
                    dve.wait_ge(*n("s5_s"))
                    post("s5_x_free")
                dve.wait_ge(*n("dve_full2"))
                u = two(PJ[:, i, :])
                stt(u, u, par1[:, bass.ds(i + V1["d"][0], 1)], halves(2), ALU.mult, ALU.add).then_inc(SEMS["free2"], 1)
            for x in (WC, OR, WT, st):
                v.memset(x[:], 0.0)
            mark("s5_y")
            dve.wait_ge(*n("v_ready"))
            neglam, qgs = lamc[:, 4:5], lamc[:, 5:6]
            with n.loop("att", HEADS) as h:
                dve.wait_ge(*n("qk_root"))
                link(v.reciprocal(RT[:, :, :], RT[:, :, :]))
                stt(QS[:, :], PJ[:, h + 4, :], qgs, RT[:, 0, :], ALU.mult, ALU.mult)
                stt(KS[:, :], PJ[:, h + 8, :], v1("kg"), RT[:, 1, :], ALU.mult, ALU.mult).then_inc(SEMS["qk_n"], 1)

                def scores(t):
                    q0, rows = TILES[t]
                    keys = q0 + rows
                    for j in range(2):
                        dve.wait_ge(*n(f"dve_full{2 + j}"))
                        stt(SX[0:rows, t % 2, j, 0:keys], c("dist", SEQ - P + NMETA - q0, keys, rows),
                            cst[0:rows, bass.ds(h + CC["negslope"][0], 1)], ps(2 + j)[0:rows, 0:keys],
                            ALU.mult, ALU.add).then_inc(SEMS[f"free{2 + j}"], 1)
                    join()
                    v.tensor_reduce(st[0:rows, 2 * (t % 2):2 * (t % 2) + 2], SX[0:rows, t % 2, :, 0:keys], AX.X, ALU.max,
                                    negate=True).then_inc(SEMS["sc_ready"], 1)

                scores(0)
                for t, (q0, rows) in enumerate(TILES):
                    if t + 1 < len(TILES):
                        scores(t + 1)
                    keys = q0 + rows
                    dve.wait_ge(*n("ex_ready"))
                    o = 4 + 2 * (t % 2)
                    link(v.reciprocal(st[0:rows, 8:10], st[0:rows, o:o + 2]))
                    link(tt(st[0:rows, 10:11], st[0:rows, 9:10], neglam[0:rows], ALU.mult))
                    link(ts(JK2[0:rows, 0:keys], SX[0:rows, t % 2, 1, 0:keys], st[0:rows, 10:11], None, ALU.mult))
                    if t:
                        dve.wait_ge(*n("wt_ready"))
                    stt(WC[0:rows, 0:keys], SX[0:rows, t % 2, 0, 0:keys], st[0:rows, 8:9], JK2[0:rows, 0:keys],
                        ALU.mult, ALU.add).then_inc(SEMS["w_comb"], 1)
                    dve.wait_ge(*n("w_comb"))
                n("wt_ready")
                dve.wait_ge(*n("o_root"))
                link(v.reciprocal(st[:, 24:29], st[:, 24:29]))
                tt(OR[:, :, :], OR[:, :, :], st[:, 24:29].unsqueeze(2).broadcast_to([P, 5, P]), ALU.mult)\
                    .then_inc(SEMS["o_norm"], 1)
                dve.wait_ge(*n("o_norm"))
            for m in range(4):
                dve.wait_ge(*n("glu_th"))
                ins = stt(PJ[:, 8 + m, :], TH[:, m, :], 1.0, PJ[:, m, :], ALU.add, ALU.mult)
            ins.then_inc(SEMS["ys_ready"], 1)
            with n.loop("mix", 2) as i:
                for k in range(WSLOTS):
                    p = 2 * (k % 2)
                    m = i * 4 + k
                    dve.wait_ge(*n(f"dve_full{p}"))
                    g = two(PJ[:, m + 12, :])
                    stt(g, g, 1.0, halves(p), ALU.add, ALU.mult).then_inc(SEMS[f"free{p}"], 1)
                    dve.wait_ge(*n(f"dve_full{p + 1}"))
                    stt(two(JK2[:, :]), two(PJ[:, m + 20, :]), 1.0, halves(p + 1), ALU.add, ALU.mult)\
                        .then_inc(SEMS[f"free{p + 1}"], 1)
                    join()
                    link(stt(PJ[:, m + 12, :], PJ[:, m + 12, :], 0.5, JK2[:, :], ALU.mult, ALU.add))
            post("mix_ready")
            with n.loop("wo", 2) as i:
                for k in range(WSLOTS):
                    dve.wait_ge(*n(f"dve_full{k}"))
                    x = two(X[:, i * 4 + k, :])
                    stt(x, halves(k), 0.5, x, ALU.mult, ALU.add).then_inc(SEMS[f"free{k}"], 1)
            mark("h_ready")
            norm(X[:, :, :], lambda k: v1("g2", k), T)
            with n.loop("up", NFF // 2) as i:
                for m in range(2):
                    def col(name):
                        return par1[:, bass.ds(i * 2 + (m + V1[name][0]), 1)]

                    dve.wait_ge(*n("ffa"))
                    link(ts(CV[:, :], FA[:, 2:514], col("cw2"), col("cb"), ALU.mult, ALU.add))
                    link(stt(CV[:, :], FA[:, 1:513], col("cw1"), CV[:, :], ALU.mult, ALU.add))
                    stt(CV[:, :], FA[:, 0:512], col("cw0"), CV[:, :], ALU.mult, ALU.add).then_inc(SEMS["ffc"], 1)
                    mark(f"free{2 * m}")
                    dve.wait_ge(*n("ffg"))
                    dve.wait_ge(*n(f"dve_full{2 * m + 1}"))
                    tt(hid[:, i * 2 + m, :], GL[:, :], PS[2 * m + 1][:, 0, :], ALU.mult).then_inc(SEMS[f"free{2 * m + 1}"], 1)
                    join()
            post("hid_done")
            for p in range(4):
                dve.wait_ge(*n(f"dve_full{p}"))
                x = X[:, 2 * p:2 * p + 2, NMETA:T]
                tt(x, x, PS[p][:, :, :], ALU.add).then_inc(SEMS[f"free{p}"], 1)
            mark("x2_ready")

            with n.loop("layer", LAYERS) as l:
                dve.wait_ge(*n("small_in", 16))
                norm(XK, lambda k: v2("pre", k), SEQ)
                n.settle()
                link(dve.drain())
                tt(LB[:, 4:6], v2("lbl", 2, 2), v2("lbl", 0, 2), ALU.subtract).then_inc(SEMS["lb_arg"], 1)
                ts(DWH[:, :], v2("dww", 0, 64), 0.5, None, ALU.mult)
                dve.wait_ge(*n("lb_th"))
                link(ts(LB[:, 4:6], LB[:, 4:6], 0.5, 0.5, ALU.mult, ALU.add))
                link(ts(LB[:, 0:2], LB[:, 4:6], v2("isl"), None, ALU.mult))
                link(ts(LB[:, 2:4], LB[:, 0:2], -0.5, 0.5, ALU.mult, ALU.add))
                link(tt(LB[:, 4:6], LB[:, 0:2], LB[:, 2:4], ALU.add))
                link(ts(LB[:, 6:8], LB[:, 2:4], -1.0, None, ALU.mult))
                dve.wait_ge(*n("b_th"))
                v.memset(FZ[:, :, 0:LAG], 0.0)
                v.memset(KP[:, :, 0:LAG], 0.0)
                v.memset(VP[:, :, 0:LAG], 0.0)
                v.memset(TM[:, 1, :, :], 0.0)
                for cc in range(2):
                    ts(TM[:, 0, cc, :], PJ2[:, cc, :], LB[:, 2 + cc:3 + cc], LB[:, 4 + cc:5 + cc], ALU.mult, ALU.add)
                    ts(KP[:, cc, LAG:], PJ2[:, cc, :], LB[:, 6 + cc:7 + cc], LB[:, 2 + cc:3 + cc], ALU.mult, ALU.add)
                v.tensor_copy(VP[:, :, LAG:], PJ2[:, 4:6, :])
                link(v.tensor_copy(EE[:, :, :], PJ2[:, 2:4, :]))
                link(ts(TM[:, 0, :, :], TM[:, 0, :, :], 1e-20, None, ALU.max))
                v.tensor_copy(FZ[:, :, LAG:], TM[:, 0, :, :])
                blocks = lambda x: x.rearrange("p a (b s) -> p a b s", s=LAG)
                link(v.tensor_copy(blocks(TM[:, 1, :, :])[:, :, :, 0], blocks(TM[:, 0, :, :])[:, :, :, 0]))
                link(v.memset(blocks(FZ[:, :, LAG:])[:, :, :, 0], 0.0))
                for cc in range(2):
                    ins = v.tensor_tensor_scan(MB[:, 0, cc, :], FZ[:, cc, LAG:], TM[:, 1, cc, :], 0.0, ALU.mult, ALU.add)
                link(ins)
                tt(QG[:, :, :], EE[:, :, :], MB[:, 0, :, :], ALU.mult)
                link(v.tensor_copy(DL[:, :, :], blocks(MB[:, 0, :, :])[:, :, :, LAG - 1]))
                v.memset(DL[:, :, 0:1], 0.0)
                hs_, fs_ = blocks(TM[:, 0, :, :]), blocks(FZ[:, :, LAG:])
                link(v.memset(hs_[:, :, :, LAG - 1], 1.0))
                for q in range(LAG - 2, -1, -1):
                    link(tt(hs_[:, :, :, q], fs_[:, :, :, q + 1], hs_[:, :, :, q + 1], ALU.mult))
                link(tt(KH[:, :, :], KP[:, :, LAG:], TM[:, 0, :, :], ALU.mult))
                post("b_kh")
                dve.wait_ge(*n("a_th"))
                v.memset(HP[:, :, 0:30], 0.0)
                v.memset(HP[:, :, 542:543], 0.0)
                v.memset(CA[:, :, :], 0.0)
                link(stt(HP[:, :, 30:542], PJ2[:, 8:10, :], 1.0, PJ2[:, 6:8, :], ALU.add, ALU.mult))
                for cc in range(2):
                    link(ts(CA[:, cc, :], CA[:, cc, :], v2("dwb", cc), None, ALU.add))
                with n.loop("lag", 2) as i:
                    for k in range(8):
                        s0 = i * (-8) + (LAG - k)
                        tt(MB[:, k % 2, :, :], EE[:, :, :], KP[:, :, bass.ds(s0, SEQ)], ALU.mult).then_inc(SEMS["b_m"], 1)
                        for tap in range(2):
                            for cc in range(2):
                                o = i * 16 + (2 * k + tap)
                                ins = stt(CA[:, cc, :], HP[:, cc, bass.ds(o, SEQ)],
                                          DWH[:, bass.ds(i * 16 + (32 * cc + 2 * k + tap), 1)], CA[:, cc, :], ALU.mult, ALU.add)
                            link(ins)
                        dve.wait_ge(*n("b_acc"))
                        dve.wait_ge(*n(f"dve_full{2 + k % 2}"))
                        tt(TM[:, k % 2, :, :], PS[2 + k % 2][:, :, :], VP[:, :, bass.ds(s0, SEQ)], ALU.mult)\
                            .then_inc(SEMS[f"free{2 + k % 2}"], 1)
                        mark("b_t")
                        dve.wait_ge(*n("b_e"))
                for _ in range(2):
                    dve.wait_ge(*n("b_acc"))
                post("a_ca")
                ts(CWH[:, 0:24], v2("ccw", 0, 24), 0.5, None, ALU.mult)
                link(ts(CWH[:, 24:30], v2("ccb", 0, 6), 0.5, None, ALU.mult))
                dve.wait_ge(*n("dve_full1"))
                m0 = PS[1][:, 0, :].unsqueeze(1).broadcast_to([P, 2, SEQ])
                stt(CA[:, :, :], m0, -1.0 / 256, CA[:, :, :], ALU.mult, ALU.add).then_inc(SEMS["a_xc"], 1)
                dve.wait_ge(*n("b_dz"))
                for cc in range(2):
                    us = (US0, US1)[cc]
                    ins = v.tensor_tensor_scan(us, DZ[cc], us, 0.0, ALU.mult, ALU.add)
                ins.then_inc(SEMS["b_s"], 1)
                dve.wait_ge(*n("gate_th"))
                stt(PJ2[:, 22:26, :], FREE[0], 1.0, PJ2[:, 22:26, :], ALU.add, ALU.mult)
                dve.wait_ge(*n("dve_full0"))
                link(tt(ACC[:, :, LAG:], ACC[:, :, LAG:], PS[0][:, :, LAG:], ALU.add))
                post("free0")
                post("b_acc2")
                dve.wait_ge(*n("a_root"))
                link(v.reciprocal(RA, RA))
                for cc in range(2):
                    stt(CA[:, cc, :], CA[:, cc, :], v2("lng", cc), RA, ALU.mult, ALU.mult)
                join()
                for cc in range(2):
                    ins = ts(CA[:, cc, :], CA[:, cc, :], v2("lnb", cc), None, ALU.add)
                ins.then_inc(SEMS["a_x"], 1)
                dve.wait_ge(*n("b_root"))
                link(v.reciprocal(RB[:, :, :], RB[:, :, :]))
                for cc in range(2):
                    stt(ACC[:, cc, :], ACC[:, cc, :], v2("bng", cc), RB[:, cc, :], ALU.mult, ALU.mult)
                join()
                stt(PJ2[:, 24:26, :], PJ2[:, 24:26, :], 0.5, ACC[:, :, :], ALU.mult, ALU.mult)
                dve.wait_ge(*n("a_xt"))
                stt(CA[:, :, :], SQA[:, :, :], 1.0, CA[:, :, :], ALU.add, ALU.mult).then_inc(SEMS["a_h"], 1)
                dve.wait_ge(*n("dve_full1"))
                for m in range(2):
                    ts(SQA[:, m, :], PS[1][:, m, :], 0.5, v2("pwb", m), ALU.mult, ALU.add)
                join()
                post("free1")
                link(stt(PJ2[:, 22:24, :], PJ2[:, 22:24, :], 0.5, SQA[:, :, :], ALU.mult, ALU.mult))
                U4 = DD[0:4, 1, :]
                link(ts(U4, PJ2[0:4, 16, :], v2("dtb", rows=4), None, ALU.add))
                stt(DD[0:4, 0, :], U4, -1.0, U4, ALU.mult, ALU.max).then_inc(SEMS["c_dtabs"], 1)
                for m in range(6):
                    link(ts(CX[:, m, :], PJ2[:, 10 + m, :], CWH[:, 18 + m:19 + m], CWH[:, 24 + m:25 + m], ALU.mult, ALU.add))
                    for b in (1, 2, 3):
                        ins = stt(CX[:, m, b:], PJ2[:, 10 + m, 0:SEQ - b], CWH[:, (3 - b) * 6 + m:(3 - b) * 6 + m + 1], CX[:, m, b:],
                                  ALU.mult, ALU.add)
                        link(ins)
                post("c_cx")
                dve.wait_ge(*n("c_dtln"))
                link(stt(DT4[0:4, :], U4, 0.0, DD[0:4, 0, :], ALU.max, ALU.add))
                link(ts(LB2[0:4, 0:1], LB2[0:4, 0:1], -1.0, None, ALU.mult))
                link(ts(U4, DT4[0:4, :], LB2[0:4, 0:1], None, ALU.mult))
                v.tensor_tensor_scan(AC4[0:4, :], c("keep", 0, SEQ, 4), U4, 0.0, ALU.mult, ALU.add).then_inc(SEMS["c_dt"], 1)
                dve.wait_ge(*n("c_th"))
                stt(PJ2[:, 10:16, :], PJ2[:, 10:16, :], 1.0, CX[:, :, :], ALU.add, ALU.mult).then_inc(SEMS["c_x"], 1)
                dve.wait_ge(*n("c_x"))
                dve.wait_ge(*n("c_acb"))
                last = ACB.rearrange("p h (t l) -> p t h l", l=P)[:, :, :, P - 1]
                dcol, acol = COL[:, :, 0:4], COL[:, :, 4:8]
                tt(WCOL[:, :, :], last, acol, ALU.subtract).then_inc(SEMS["c_wd"], 1)
                A4_ = ACB.rearrange("p h (t l) -> p h t l", l=P)
                D4_ = DD.rearrange("p h (t l) -> p h t l", l=P)
                for h in range(HEADS):
                    tt(D4_[:, h], A4_[:, h], acol[:, :, h].unsqueeze(2).broadcast_to([P, 4, P]), ALU.subtract)
                join()
                mask = c("causal").unsqueeze(1).broadcast_to([P, 16, P])
                tt(DD.rearrange("p h (t l) -> p (h t) l", l=P), DD.rearrange("p h (t l) -> p (h t) l", l=P), mask, ALU.add)\
                    .then_inc(SEMS["c_d"], 1)
                dve.wait_ge(*n("c_we"))
                link(tt(WCOL[:, :, :], WCOL[:, :, :], dcol, ALU.mult))
                dve.wait_ge(*n("dve_full1"))
                for t in range(4):
                    xt = ps(1)[:, t * 256:t * 256 + 256].rearrange("p (h v) -> p h v", h=4)
                    tt(XDT[:, t], xt, dcol[:, t, :].unsqueeze(2).broadcast_to([P, 4, 64]), ALU.mult)
                    tt(WX[:, t], xt, WCOL[:, t, :].unsqueeze(2).broadcast_to([P, 4, 64]), ALU.mult)
                mark("free1")
                mark("c_wx")
                dve.wait_ge(*n("dve_full2"))
                link(v.tensor_copy(HS[:, 0, :], ps(2)[:, 0:256]))
                for t in (1, 2):
                    for h in range(HEADS):
                        q = slice(h * 64, h * 64 + 64)
                        dec = EAB[:, h, t * P + P - 1:t * P + P]
                        ins = stt(HS[:, t, q], HS[:, t - 1, q], dec, ps(2)[:, t * 256 + h * 64:t * 256 + h * 64 + 64],
                                  ALU.mult, ALU.add)
                    link(ins)
                post("free2")
                post("c_hs")
                dve.wait_ge(*n("gate_th"))
                for x in (0, 1):
                    z = PJ2[:, (20, 26)[x]:(22, 28)[x], :]
                    stt(z, FREE[1][:, 2 * x:2 * x + 2, :], 1.0, z, ALU.add, ALU.mult)
                dve.wait_ge(*n("c_de"))
                dve.wait_ge(*n("dve_full3"))
                for g in range(2):
                    cb = PS[3][:, g, :].unsqueeze(1).broadcast_to([P, 2, SEQ])
                    tt(DD[:, 2 * g:2 * g + 2, :], DD[:, 2 * g:2 * g + 2, :], cb, ALU.mult)
                mark("free3")
                mark("c_sc")
                dve.wait_ge(*n("dve_full0"))
                for g in range(2):
                    stt(YC[:, g, :], PJ2[:, 10 + g, :], v2("dsk", g), PS[0][:, g, :], ALU.mult, ALU.add)
                join()
                post("free0")
                stt(YC[:, :, :], YC[:, :, :], 0.5, PJ2[:, 20:22, :], ALU.mult, ALU.mult).then_inc(SEMS["c_yc"], 1)
                dve.wait_ge(*n("c_root"))
                link(v.reciprocal(RC[:, :, :], RC[:, :, :]))
                for g in range(2):
                    ins = stt(PJ2[:, 20 + g, :], YC[:, g, :], v2("cng", g), RC[:, g, :], ALU.mult, ALU.mult)
                ins.then_inc(SEMS["c_done"], 1)
                dve.wait_ge(SEMS["pos_in"], 16)
                dve.wait_ge(*n("c_done"))
                link(v.tensor_copy(ANG, POS[:, :]))
                link(ts(ANG, ANG, c("invf"), None, ALU.mult))
                link(ts(KT, ANG, 1.0 / (2 * np.pi), MAGIC, ALU.mult, ALU.add))
                link(ts(KT, KT, -MAGIC, None, ALU.add))
                for part in PI2:
                    link(stt(ANG, KT, -part, ANG, ALU.mult, ALU.add))
                link(ts(COS, ANG, float(np.pi / 2), None, ALU.add))
                link(ts(KT, COS, float(np.pi), -2 * float(np.pi), ALU.is_gt, ALU.mult))
                link(tt(COS, COS, KT, ALU.add))
                ts(SIN, ANG, PIF, -PIF, ALU.min, ALU.max)
                link(ts(COS, COS, PIF, -PIF, ALU.min, ALU.max))
                post("d_trig_arg")
                dve.wait_ge(*n("d_root"))
                link(v.reciprocal(RD[:, :, :], RD[:, :, :]))
                for b in range(2):
                    stt(CQ[:, b, :], PJ2[:, 18 + b, :], v2("qag", b), RD[:, 0, :], ALU.mult, ALU.mult)
                stt(CK, PJ2[:, 17, :], v2("kvg"), RD[:, 1, :], ALU.mult, ALU.mult).then_inc(SEMS["d_n"], 1)
                dve.wait_ge(*n("d_trig"))
                link(ts(SIN, SIN, c("sgn"), None, ALU.mult))
                rr = slice(64, QKR)
                dve.wait_ge(*n("dve_full1"))
                tt(KR[rr, :], PJ2[rr, 16, :], COS[rr, :], ALU.mult)
                link(tt(KT[rr, :], PS[1][rr, 0, :], SIN[rr, :], ALU.mult))
                post("free1")
                tt(KR[rr, :], KR[rr, :], KT[rr, :], ALU.add).then_inc(SEMS["d_kr"], 1)
                for h in range(HEADS):
                    p = 2 + h % 2
                    dve.wait_ge(*n(f"dve_full{p}"))
                    tt(QF[0:QKR, h, :], PS[p][0:QKR, 0, :], COS[0:QKR, :], ALU.mult)
                    link(tt(TQ[rr, :], PS[p][rr, 1, :], SIN[rr, :], ALU.mult))
                    post(f"free{p}")
                    link(tt(QF[rr, h, :], QF[rr, h, :], TQ[rr, :], ALU.add))
                post("d_q")
                with n.loop("mla", HEADS) as h:
                    def scores(t):
                        p = 2 + t % 2
                        w_ = t * P + P
                        dve.wait_ge(*n(f"dve_full{p}"))
                        link(tt(SD[:, t % 2, 0:w_], PS[p][:, 0, 0:w_], c("mlamask", SEQ - w_, w_), ALU.add))
                        post(f"free{p}")
                        link(v.tensor_reduce(sd[:, 4:5], SD[:, t % 2, 0:w_], AX.X, ALU.max, negate=True))
                        link(ts(sd[:, t % 2:t % 2 + 1], sd[:, 4:5], QKR ** -0.5, None, ALU.mult))
                        post("d_sc")

                    scores(0)
                    for t in range(4):
                        if t < 3:
                            if t:
                                dve.wait_ge(*n("d_wt"))
                            scores(t + 1)
                        dve.wait_ge(*n("d_ex"))
                        link(v.reciprocal(sd[:, 5:6], sd[:, 2 + t % 2:3 + t % 2]))
                        dve.wait_ge(*n("dve_full1"))
                        link(ts(OD[:, t, bass.ds(h * 64, 64)], PS[1][:, 0, 0:64], sd[:, 5:6], None, ALU.mult))
                        post("free1")
                        post("d_o")
                    for _ in range(2):
                        n("d_wt")
                dve.wait_ge(*n("dve_full0"))
                link(stt(PJ2[:, 26:28, :], PJ2[:, 26:28, :], 0.5, PS[0][:, :, :], ALU.mult, ALU.mult))
                post("free0")
                post("y_ready")
                dve.wait_ge(*n("rms_root"))
                link(v.reciprocal(R[:, 0:SEQ], R[:, 0:SEQ]))
                for k in range(KD):
                    ins = stt(PJ2[:, 8 + k, :], HNY[:, k, :], v2("post", k), R[:, 0:SEQ], ALU.mult, ALU.mult)
                link(ins)
                tt(XK, XK, PJ2[:, 8:16, :], ALU.add).then_inc(SEMS["x2_ready"], 1)


def chunks(w, cols):
    w = w[:, cols]
    return w.reshape(w.shape[0] // P, P, w.shape[1]).transpose(1, 0, 2).reshape(P, -1)


def slices(lo, n):
    return [slice(lo + P * k, lo + P * k + P) for k in range(n)]


def table(spec, values):
    out = np.zeros((P, sum(n for _, n in spec)), np.float32)
    at = 0
    for name, n in spec:
        v = values[name]
        assert v.shape[1] == n, name
        out[:v.shape[0], at:at + n] = v
        at += n
    return out


def layout(x):
    f = {k: np.asarray(v) for k, v in x.items()}
    z = {}
    z["xT"] = np.ascontiguousarray(np.concatenate([f["meta_tokens"], f["x"][0]], 0).T).reshape(KD, P, T)
    w = f["w_in"][0]
    slots = [chunks(w, s) for s in slices(0, 12)]
    wv = w[:, 1536:2048].reshape(KD, P, 512)
    slots += [wv[2 * k:2 * k + 2].transpose(1, 0, 2).reshape(P, 1024) for k in range(4)]
    slots += [chunks(w, s) for s in slices(2048, 16)]
    g = f["ssm_glu_w"][0]
    slots += [np.concatenate([chunks(g, s) for s in slices(256 * k, 2)], 1) for k in range(2)]
    slots += [np.concatenate([chunks(f["w_ssm_out"][0], s), chunks(f["w_att_out"][0], s)], 1) for s in slices(0, 8)]
    slots += [chunks(f["w_o"][0], s) for s in slices(0, 8)]
    up = f["w_up"][0]
    for a_, b_ in zip(slices(0, NFF), slices(NFF * P, NFF)):
        slots += [chunks(up, a_), chunks(up, b_)]
    slots += list(f["w_down"][0].reshape(NFF, P, D))
    order = [3 * 256 + 256, 3 * 256, 3 * 256 + 512, 0, 256]
    c0 = 7 * 256
    for l in range(LAYERS):
        w2 = f["w_in_2"][l]
        for o in order:
            slots += [chunks(w2, s) for s in slices(o, 2)]
        slots += [chunks(w2, s) for s in slices(c0, 6)]
        misc = np.zeros((D, P), np.float32)
        misc[:, 0:4] = w2[:, c0 + 768:c0 + 772]
        misc[:, 64:96] = w2[:, c0 + 1412:c0 + 1444]
        slots += [chunks(misc, slice(0, P)), chunks(w2, slice(c0 + 1284, c0 + 1412))]
        for o in (c0 + 1028, 512, 6 * 256, c0 + 772, c0 + 1444):
            slots += [chunks(w2, s) for s in slices(o, 2)]
        wo2 = f["w_out_2"][l].reshape(4, 256, D)[[2, 0, 1, 3]].reshape(D, D)
        slots += [chunks(wo2, s) for s in slices(0, 8)]
    z["wst"] = np.stack(slots)
    s5w = np.zeros((16, P, 4, P), np.float32)
    for k in range(16):
        for g2 in range(2):
            ch = slice(32 * (k % 4) + 16 * g2, 32 * (k % 4) + 16 * g2 + 16)
            st_ = slice(64 * g2, 64 * g2 + 64)
            s5w[k, ch, 0, st_] = f["ssm_b_re"][0, 2 * k + g2].T
            s5w[k, ch, 1, st_] = f["ssm_b_im"][0, 2 * k + g2].T
            s5w[k, st_, 2, ch] = f["ssm_c_re"][0, 2 * k + g2].T
            s5w[k, st_, 3, ch] = f["ssm_c_im"][0, 2 * k + g2].T
    z["s5w"] = s5w.reshape(16, P, 512)

    def cols(v):
        return v.reshape(-1, P).T

    z["par1"] = table(VEC1, {
        "g1": cols(f["norm1_g"][0]), "qg": np.tile(f["q_norm_g"][0], 2)[:, None], "kg": np.tile(f["k_norm_g"][0], 2)[:, None],
        "d": cols(f["ssm_d"][0].reshape(-1)), "glub": cols(f["ssm_glu_b"][0]), "g2": cols(f["norm2_g"][0]),
        "cw0": cols(f["conv_w"][0, 0]), "cw1": cols(f["conv_w"][0, 1]), "cw2": cols(f["conv_w"][0, 2]),
        "cb": cols(f["conv_b"][0]), "are": cols(f["ssm_a_re"][0].reshape(-1)), "aim": cols(f["ssm_a_im"][0].reshape(-1)),
        "ldt": cols(np.repeat(f["ssm_log_dt"][0], 64)), "subg": f["subln_g"][0][:, None],
        "lam": np.broadcast_to(np.concatenate([f[k][0] for k in ("lam_q1", "lam_k1", "lam_q2", "lam_k2")])[None], (P, 256))})
    r = np.arange(P)[:, None]
    rot = np.zeros((P, P), np.float32)
    for k in range(16):
        rot[64 + 16 + k, 64 + k] = 1.0
        rot[64 + k, 64 + 16 + k] = 1.0
    dist = r - (np.arange(T)[None] - (SEQ - P + NMETA))
    tri = np.where(r[:64 * 0 + P] <= np.arange(P)[None], 0.0, NEG)
    mla = np.zeros((P, SEQ))
    mla[:64, SEQ - 64:] = NEG
    sel4 = np.zeros((P, 4, P))
    for k in range(4):
        sel4[k, k] = 1.0
    invf = np.zeros((P, 1))
    invf[64:96, 0] = np.tile(np.float32(10000.0) ** (-np.arange(0, 32, 2, dtype=np.float32) / np.float32(32)), 2)
    keep = np.ones((P, SEQ))
    keep[:, ::P] = 0.0
    small = []
    swap = np.r_[16:32, 0:16]
    for l in range(LAYERS):
        qb = f["d_qb_w_2"][l].reshape(2, P, 4, QKR)
        kvb = f["d_kvb_w_2"][l].reshape(P, 4, 2, 64)
        pw = f["a_pw_w_2"][l].reshape(2, P, 2, P)
        par = table(VEC2, {
            "pre": cols(f["pre_norm_g_2"][l]), "post": cols(f["post_norm_g_2"][l]),
            "dww": np.concatenate([f["a_dw_w_2"][l], np.zeros((1, 256), np.float32)]).reshape(32, 2, P).transpose(2, 1, 0).reshape(P, 64),
            "dwb": cols(f["a_dw_b_2"][l]), "lng": cols(f["a_ln_g_2"][l]), "lnb": cols(f["a_ln_b_2"][l]), "pwb": cols(f["a_pw_b_2"][l]),
            "lbl": cols(f["b_lb_logits_2"].reshape(-1)), "bng": cols(f["b_norm_g_2"][l]), "ccw": cols(f["c_conv_w_2"][l].reshape(-1)),
            "ccb": cols(f["c_conv_b_2"][l]), "dtb": f["c_dt_bias_2"][l][:, None], "alog": f["c_a_log_2"][l][:, None],
            "dsk": cols(np.repeat(f["c_d_2"][l], 64)), "cng": cols(f["c_norm_g_2"][l]), "qag": cols(f["d_qa_g_2"][l]),
            "kvg": cols(f["d_kva_g_2"][l]), "isl": np.full((P, 1), float(l), np.float32)})
        small.append(np.concatenate([
            qb.transpose(1, 2, 0, 3).reshape(P, -1), qb[..., 64:][..., swap].transpose(1, 2, 0, 3).reshape(P, -1),
            kvb[:, :, 0].reshape(P, -1), kvb[:, :, 1].reshape(P, -1), pw.transpose(1, 2, 0, 3).reshape(P, -1), par], 1))
    z["small"] = np.stack(small)
    z["pos"] = np.broadcast_to(f["positions_2"].astype(np.int32), (P, SEQ)).copy()
    sgn = np.ones((P, 1))
    sgn[64:80] = -1.0
    z["cst"] = table(CONSTS, {
        "ident": np.eye(P), "ones": np.ones((P, P)), "pair64": np.kron(np.eye(2), np.ones((64, 64))), "rot": rot,
        "dist": np.where(dist >= 0, dist, -NEG), "mlamask": mla, "causal": tri, "blk8": (r // LAG == np.arange(8)[None]) * 1.0,
        "negslope": np.broadcast_to(-2.0 ** (-8.0 * np.arange(1, 5) / 4)[None], (P, 4)), "invf": invf, "sgn": sgn,
        "sel4": sel4.reshape(P, 512), "keep": keep})
    return z


def kernel(**inputs):
    import concourse.bacc as bacc
    from concourse.bass_utils import run_bass_kernel_spmd

    nc = bacc.Bacc("TRN2", target_bir_lowering=False, num_devices=1)
    arrays = layout(inputs)
    aps = {k: nc.dram_tensor(k, v.shape, mybir.dt.from_np(v.dtype), kind="ExternalInput").ap() for k, v in arrays.items()}
    out = nc.dram_tensor("outT", (KD, P, SEQ), F32, kind="ExternalOutput").ap()
    build(nc, aps, out)
    r = run_bass_kernel_spmd(nc, [arrays], core_ids=[0])
    return np.ascontiguousarray(r.results[0]["outT"].reshape(D, SEQ).T)[None]
```

```python
from contextlib import ExitStack, contextmanager

import numpy as np

import concourse.bass as bass
from concourse import mybir

F32 = mybir.dt.float32
I32 = mybir.dt.int32
ACT = mybir.ActivationFunctionType
ALU = mybir.AluOpType
AX = mybir.AxisListType

P = 128
D = 1024
KD = D // P
NMETA = 16
SEQ = 512
T = SEQ + NMETA
H = T // 2
WSLOTS = 4
EPS = 1e-6
NFF = 22
LAYERS = 2
NPROJ = 28
HEADS = 4
LAM_INIT = 0.8 - 0.6
TILES = [(0, NMETA)] + [(NMETA + P * i, P) for i in range(4)]
LAG = 16
NBLK = SEQ // LAG
TAPS = 31
NSC = 17000
QKR = 96

VEC1 = [("g1", 8), ("qg", 1), ("kg", 1), ("d", 4), ("glub", 4), ("g2", 8), ("cw0", NFF), ("cw1", NFF), ("cw2", NFF),
        ("cb", NFF), ("are", 16), ("aim", 16), ("ldt", 16), ("subg", 1), ("lam", 256)]
VEC2 = [("pre", 8), ("post", 8), ("dww", 2 * (TAPS + 1)), ("dwb", 2), ("lng", 2), ("lnb", 2), ("pwb", 2), ("lbl", 4),
        ("bng", 2), ("ccw", 24), ("ccb", 6), ("dtb", 1), ("alog", 1), ("dsk", 2), ("cng", 2), ("qag", 2), ("kvg", 1), ("isl", 1)]
CONSTS = [("ident", P), ("ones", P), ("pair64", P), ("rot", P), ("dist", T), ("mlamask", SEQ), ("causal", P),
          ("blk8", 8), ("negslope", HEADS + 1), ("invf", 1), ("sgn", 1), ("sel4", 4 * P), ("keep", SEQ)]


def columns(table):
    at, out = 0, {}
    for name, n in table:
        out[name] = (at, at + n)
        at += n
    return out, at


V1, NV1 = columns(VEC1)
V2, NV2 = columns(VEC2)
CC, NCC = columns(CONSTS)

MAGIC = 12582912.0
PI2 = [6.28125, 0.0019350051879882812, 3.019916050733e-07]
PIF = 3.1415925
NEG = -1e30

NSW = 2048
SWQ, SWR, SWK, SWV, SWP = 0, 768, 1024, 1280, 1536

PER = {'act.att': {'act_full0': 5, 'act_full1': 5, 'sc_ready': 5},
 'act.lag': {'act_full0': 2, 'act_full1': 2},
 'act.layer': {'a_x': 1,
               'a_xc': 1,
               'act_full0': 36,
               'act_full1': 14,
               'act_full2': 13,
               'act_full3': 13,
               'act_step': 6,
               'b_acc2': 1,
               'b_s': 1,
               'c_cx': 1,
               'c_d': 1,
               'c_dtabs': 1,
               'c_wd': 1,
               'c_yc': 1,
               'd_q': 1,
               'd_sc': 18,
               'd_v': 1,
               'lb_arg': 1,
               'x2_ready': 8},
 'act.mla': {'act_full0': 4, 'd_sc': 4},
 'act.proj': {'act_full0': 1, 'act_full1': 1, 'act_full2': 1, 'act_full3': 1},
 'act.s5': {'act_full0': 6, 'act_full1': 4, 'act_full3': 4, 's5_x_free': 4},
 'act.up': {'act_full0': 1, 'act_full2': 1, 'ffc': 2},
 'act.uqk': {'act_full0': 1, 'act_full1': 1, 'act_full2': 1, 'act_full3': 1},
 'act.wo': {'h_ready': 4},
 'act.wout': {'act_full0': 1, 'act_full1': 1, 'act_full2': 1, 'act_full3': 1},
 'dve.att': {'dve_full2': 5, 'dve_full3': 5, 'dve_step': 15, 'ex_ready': 5, 'w_comb': 5, 'wt_ready': 5},
 'dve.lag': {'b_acc': 8, 'b_e': 8, 'dve_full2': 4, 'dve_full3': 4, 'dve_step': 16},
 'dve.layer': {'a_root': 1,
               'a_th': 1,
               'a_xt': 1,
               'b_acc': 18,
               'b_e': 16,
               'b_root': 1,
               'b_th': 1,
               'b_us': 4,
               'c_acb': 1,
               'c_de': 1,
               'c_dtln': 1,
               'c_root': 1,
               'c_th': 1,
               'c_we': 1,
               'c_x': 1,
               'd_root': 1,
               'dve_full0': 3,
               'dve_full1': 19,
               'dve_full2': 18,
               'dve_full3': 18,
               'dve_step': 167,
               'gate_th': 2,
               'lb_th': 1,
               'rms_root': 2,
               'small_in': 16},
 'dve.mix': {'dve_full0': 2, 'dve_full1': 2, 'dve_full2': 2, 'dve_full3': 2, 'dve_step': 8},
 'dve.mla': {'dve_full1': 4, 'dve_full2': 2, 'dve_full3': 2, 'dve_step': 13},
 'dve.s5': {'dve_full2': 1, 'dve_step': 20, 'qk_root': 2, 's5_ph': 4, 's5_s': 4, 's5_s_free': 3, 's5_x': 4},
 'dve.up': {'dve_full1': 1, 'dve_full3': 1, 'dve_step': 6, 'ffa': 2, 'ffg': 2},
 'dve.wo': {'dve_full0': 1, 'dve_full1': 1, 'dve_full2': 1, 'dve_full3': 1},
 'pe.att': {'free1': 5, 'free2': 5, 'free3': 5, 'qst': 1, 'w_comb': 5, 'wt_ready': 5},
 'pe.down': {'w_ready0': 16, 'w_ready1': 16, 'w_ready2': 16, 'w_ready3': 16},
 'pe.lag': {'b_m': 8,
            'free0': 2,
            'free1': 2,
            'free2': 4,
            'free3': 4,
            'w_ready0': 16,
            'w_ready1': 16,
            'w_ready2': 16,
            'w_ready3': 16},
 'pe.layer': {'a_ca': 1,
              'a_h': 1,
              'a_sq': 1,
              'b_m': 17,
              'b_s': 1,
              'b_sq': 1,
              'b_ve': 4,
              'c_bt': 1,
              'c_cme': 1,
              'c_dt': 1,
              'c_hs': 1,
              'c_sc': 1,
              'c_sq': 1,
              'c_wx': 1,
              'c_x': 1,
              'd_ex': 18,
              'd_n': 1,
              'd_o': 16,
              'd_sq': 1,
              'd_v': 1,
              'd_wt': 16,
              'free0': 21,
              'free1': 31,
              'free2': 30,
              'free3': 31,
              'hn_ready': 8,
              'qgz': 2,
              'qst': 5,
              'sq_ready': 8,
              'w_ready0': 144,
              'w_ready1': 144,
              'w_ready2': 144,
              'w_ready3': 144,
              'y_ready': 1,
              'y_sq': 8},
 'pe.mix': {'free0': 2,
            'free1': 2,
            'free2': 2,
            'free3': 2,
            'w_ready0': 16,
            'w_ready1': 16,
            'w_ready2': 16,
            'w_ready3': 16},
 'pe.mla': {'d_ex': 4, 'd_wt': 4, 'free1': 4, 'free2': 2, 'free3': 2, 'qst': 1},
 'pe.proj': {'free0': 1,
             'free1': 1,
             'free2': 1,
             'free3': 1,
             'w_ready0': 16,
             'w_ready1': 16,
             'w_ready2': 16,
             'w_ready3': 16},
 'pe.s5': {'free0': 6,
           'free1': 4,
           'free2': 1,
           'free3': 4,
           'qk_sq': 1,
           's5_cw': 4,
           's5_s': 4,
           'w_ready0': 32,
           'w_ready1': 32,
           'w_ready2': 32,
           'w_ready3': 32},
 'pe.up': {'free0': 1,
           'free1': 1,
           'free2': 1,
           'free3': 1,
           'w_ready0': 16,
           'w_ready1': 16,
           'w_ready2': 16,
           'w_ready3': 16},
 'pe.uqk': {'free0': 1,
            'free1': 1,
            'free2': 1,
            'free3': 1,
            'w_ready0': 16,
            'w_ready1': 16,
            'w_ready2': 16,
            'w_ready3': 16},
 'pe.wo': {'free0': 1,
           'free1': 1,
           'free2': 1,
           'free3': 1,
           'w_ready0': 16,
           'w_ready1': 16,
           'w_ready2': 16,
           'w_ready3': 16},
 'pe.wout': {'free0': 1,
             'free1': 1,
             'free2': 1,
             'free3': 1,
             'w_ready0': 16,
             'w_ready1': 16,
             'w_ready2': 16,
             'w_ready3': 16},
 'pool.lag': {'b_m': 8, 'b_t': 8, 'pool_step': 16},
 'pool.layer': {'b_kh': 1,
                'b_m': 17,
                'b_t': 17,
                'b_tok': 1,
                'b_us': 4,
                'c_acb': 1,
                'c_cme': 1,
                'c_x': 1,
                'd_qe': 1,
                'pool_step': 37,
                'qgz': 2,
                'x2_ready': 8,
                'yo': 8},
 'pool.s5': {'dve_full2': 1,
             'pool_step': 12,
             's5_ph': 4,
             's5_s_free': 3,
             's5_x_free': 4,
             'w_ready0': 32,
             'w_ready2': 32},
 'sp.qkv': {'w_free0': 1, 'w_free1': 1, 'w_free2': 1, 'w_free3': 1},
 'sp.rest': {'w_free0': 1, 'w_free1': 1, 'w_free2': 1, 'w_free3': 1},
 'sp.s5': {'w_free0': 2, 'w_free1': 2, 'w_free2': 2, 'w_free3': 2}}


class Tally:

    def __init__(self, who, eng, sems):
        self.who, self.eng, self.sems, self.base, self.loops = who, eng, sems, {}, []

    def __call__(self, name, add=1):
        self.base[name] = self.base.get(name, 0) + add
        return self.now(name)

    def now(self, name):
        value = self.base.get(name, 0)
        for reg, per in self.loops:
            if per.get(name):
                value = reg * per[name] + value
        return self.sems[name], value

    def settle(self):
        self.eng.sem_inc(self.sems["settled"], 1)

    @contextmanager
    def loop(self, name, count):
        if self.loops:
            self.settle()
        start = dict(self.base)
        per = PER.get(self.who + "." + name, {})
        with self.eng.Fori(0, count) as i:
            self.loops.append((i, per))
            yield i
            self.loops.pop()
        added = {k: v - start.get(k, 0) for k, v in self.base.items() if v != start.get(k, 0)}
        assert added == per, (self.who, name, added)
        for k, v in added.items():
            self.base[k] = start.get(k, 0) + v * count


def build(nc, a, out):
    with ExitStack() as ctx:
        def sb(name, shape, dt=F32):
            return ctx.enter_context(nc.sbuf_tensor(name, shape, dt))

        SEMS = {}

        def sem(name):
            SEMS[name] = ctx.enter_context(nc.semaphore(name))
            return SEMS[name]

        PS = [ctx.enter_context(nc.psum_tensor(f"PS{p}", [P, 2, 512], F32)) for p in range(4)]
        for p in range(4):
            sem(f"act_full{p}")
            sem(f"dve_full{p}")
            sem(f"free{p}")
        for k in range(KD):
            sem(f"x_in{k}")
        for k in range(WSLOTS):
            sem(f"w_ready{k}")
            sem(f"w_free{k}")
        for name in ("par_in", "ones_in", "settled", "eps_ready", "v_zero", "v_ready", "s5_dt", "ys_gelu", "out_done", "dve_step", "act_step", "pool_step",
                     "sq_ready", "rms_root", "hn_ready", "u_ready", "proj_evac", "v_evac", "gate_evac",
                     "s5_tab", "s5_x", "s5_cw", "s5_x_free", "s5_ph", "s5_ph_free", "s5_s", "s5_s_free", "s5_c", "s5_y",
                     "trig_arg", "trig", "lam_arg", "lam_exp",
                     "qk_sq", "qk_root", "qk_n", "sc_ready", "ex_ready", "w_comb", "wt_ready", "wt_free", "o_raw",
                     "o_root", "o_norm", "ya_ready", "glu_th", "ys_ready", "mix_ready", "h_ready",
                     "ffa", "ffa_free", "ffc", "ffg", "ff_h", "x2_ready", "hid_done", "small_in", "lb_arg", "lb_th", "b_th", "a_th", "b_kh", "b_m", "b_e", "b_t", "b_acc", "b_tok", "b_ve", "b_us", "b_s", "b_sq",
                     "b_root", "b_root_d", "a_ca", "a_xc", "a_sq", "a_root", "a_x", "a_xt", "a_h", "gates", "gate_th", "qgz",
                     "c_cx", "c_th", "c_x", "c_dtabs", "c_dtln", "c_alog", "c_dt", "c_acb", "c_bt", "c_col", "c_wd", "c_we", "c_wx", "c_d", "c_de", "c_cme",
                     "c_hs", "c_sc", "c_yc", "c_sq", "c_root", "d_sq", "d_root", "d_n", "d_qe", "d_trig_arg", "d_trig", "d_q", "d_k", "d_kr", "d_v",
                     "d_st", "d_sc", "d_ex", "d_wt", "d_o", "y_ready", "yo", "y_sq", "pos_in", "layer_w", "qst", "b_acc2", "c_done"):
            sem(name)

        ring = sb("ring", [P, WSLOTS, 1024])
        X = sb("X", [P, KD, T])
        HN = sb("HN", [P, KD, T])
        R = sb("R", [P, T])
        PJ = sb("PJ", [P, NPROJ, T])
        V = sb("V", [P, 5, 512])
        par1 = sb("params1", [P, NV1])
        cst = sb("consts", [P, NCC])
        SC = sb("SC", [P, NSC])

        def c(name, lo=0, n=None, rows=P):
            s, e = CC[name]
            return cst[0:rows, s + lo:e if n is None else s + lo + n]

        def v1(name, k=0, n=1):
            return par1[:, V1[name][0] + k:V1[name][0] + k + n]

        at = [0]

        def cut(n, *shape):
            s = at[0]
            at[0] += n
            assert at[0] <= NSC, at[0]
            v = SC[:, s:s + n]
            if len(shape) == 2:
                v = v.rearrange("p (a b) -> p a b", a=shape[0])
            if len(shape) == 3:
                v = v.rearrange("p (a b c) -> p a b c", a=shape[0], b=shape[1])
            return v

        ph_a = cut(16 * 8 * 2, 2, 128)
        ph_b = cut(16 * 66 * 2, 2, 16 * 66)
        s5c = cut(12 * 16, 12, 16)
        POS = sb("POS", [P, SEQ], I32)
        COS = sb("COS", [P, SEQ])
        SIN = sb("SIN", [P, SEQ])
        LB2 = sb("LB2", [P, 4])
        CWH = sb("CWH", [P, 32])
        junkE = sb("junkE", [P, 32])
        XS = cut(2 * 2 * T, 2, 2, T)
        PH = cut(2 * 2 * T, 2, 2, T)
        TMP = cut(4 * T, 4, T)
        PT = cut(2 * T, 2, T)
        SS = cut(2 * T, 2, T)
        CW = cut(4 * P, 2, 2, P)
        CWF = cut(4 * P, 2, 2, P)
        SQ = cut(2 * T, 2, T)
        RT = cut(2 * T, 2, T)
        at[0] = 0
        QS = cut(T)
        KS = cut(T)
        SX = cut(3 * 2 * T, 3, 2, T)
        WC = cut(2 * T, 2, T)
        JK = cut(P)
        WT = cut(5 * P, 5, P)
        OR = cut(HEADS * 5 * P, HEADS * 5, P)
        st = cut(68)
        MX, SM, RC5, RA5, OS = 0, 6, 12, 22, 28
        lamc = sb("lamc", [P, 8])
        glub2 = sb("glub2", [P, 4])
        epsc = sb("epsc", [P, 4])
        junk = sb("junk", [P, 8])
        at[0] = 0
        JK2 = cut(T)
        at[0] = 0
        TH = cut(4 * T, 4, T)
        at[0] = 0
        FA = cut(514)
        CV = cut(512)
        GL = cut(512)
        ANG = cut(512)
        KT = cut(512)
        hid = PJ[:].rearrange("p a b -> p (a b)")[:, 0:NFF * SEQ].rearrange("p (a b) -> p a b", a=NFF)

        PJ2 = PJ[:].rearrange("p a b -> p (a b)")[:, 0:NPROJ * SEQ].rearrange("p (a b) -> p a b", a=NPROJ)
        HNf = HN[:].rearrange("p a b -> p (a b)")
        XK = X[:, :, NMETA:T]
        SW = V[:].rearrange("p a b -> p (a b)")[:, 0:NSW + NV2]

        def v2(name, k=0, m=1, rows=P):
            s_ = NSW + V2[name][0] + k
            return SW[0:rows, s_:s_ + m]

        at[0] = 0
        FZ = cut(2 * 528, 2, 528)
        KP = cut(2 * 528, 2, 528)
        US0 = SC[:, 0:2048]
        VP = cut(2 * 528, 2, 528)
        TM = cut(2 * 2 * 512, 2, 2, 512)
        US1 = SC[:, at[0] - 2048:at[0]]
        MB = cut(2 * 2 * 512, 2, 2, 512)
        EE = cut(2 * 512, 2, 512)
        HP = cut(2 * 543, 2, 543)
        ACC = cut(2 * 512, 2, 512)
        CA = cut(2 * 512, 2, 512)
        QG = cut(2 * 512, 2, 512)
        KH = cut(2 * 512, 2, 512)
        DWH = cut(64)
        DL = cut(2 * NBLK, 2, NBLK)
        LB = cut(8)
        NTH = cut(2 * 512, 2, 512)
        QZt = cut(4 * 512, 4, 512)
        KHT = MB[:, 0].rearrange("p a b -> p (a b)").rearrange("p (t c) -> p t c", t=4)
        VT = MB[:, 1].rearrange("p a b -> p (a b)").rearrange("p (t c) -> p t c", t=4)
        FREE = [PJ2[:, 0:4, :], PJ2[:, 6:10, :]]
        VE = [x.rearrange("p a b -> p (a b)") for x in FREE]
        DZ = VE
        HNY = HN[:, :, 0:SEQ]
        QZ = QZt[:, :, :]
        SQA = HP[:, :, 0:512]
        RB = NTH
        RA = EE[:, 0, :]
        at[0] = 0
        CX = cut(6 * 512, 6, 512)
        ACB = cut(4 * 512, 4, 512)
        EAB = cut(4 * 512, 4, 512)
        DD = cut(4 * 512, 4, 512)
        CME = cut(4 * 512, 4, 512)
        XDT = cut(1024, 4, 4, 64)
        WX = cut(1024, 4, 4, 64)
        BT = cut(1024, 4, 256)
        HS = cut(3 * 256, 3, 256)
        DT4 = cut(512)
        AC4 = cut(512)
        T4 = CX[:, 0, :]
        COL = cut(32, 4, 8)
        WCOL = cut(16, 4, 4)
        YC = CX[:, 0:2, :]
        SQC = CX[:, 2:4, :]
        RC = CX[:, 4:6, :]
        at[0] = 0
        at[0] = 6 * 512
        WD = cut(2 * 512, 2, 4, P)
        OD = cut(1024, 4, 256)
        sd = cut(16)
        SQD = [QG[:, 0, :], QG[:, 1, :], EE[:, 1, :]]
        RD = KH
        KRR = SC[:, NSC - 512:NSC]
        KF = HN[:, 0:5, 0:SEQ]
        QR = HN[:, 4:8, 0:SEQ]
        QF = PJ2[:, 0:5, :]
        VD = PJ2[:, 4:6, :].rearrange("p a b -> p (a b)").rearrange("p (t c) -> p t c", t=4)
        SD = FREE[1]
        CQ = PJ2[:, 18:20, :]
        CK = PJ2[:, 17, :]
        QST = PJ2[:, 18, :]
        rr = slice(64, QKR)

        GATES = (22, 23, 24, 25, 20, 21, 26, 27)

        def ps(p):
            return PS[p][:].rearrange("p a b -> p (a b)")

        def halves(p, rows=P):
            return PS[p][0:rows, :, 0:H]

        def two(ap):
            return ap.rearrange("p (a b) -> p a b", a=2)

        block = ctx.enter_context(nc.Block())

        @block.sync
        def _(sp):
            n = Tally("sp", sp, SEMS)
            n.base["w_free3"] = 1
            sp.dma_start(cst[:, 0:3 * P], a["cst"][:, 0:3 * P]).then_inc(SEMS["ones_in"], 16)
            for t in range(KD):
                sp.dma_start(X[:, t, :], a["xT"][t]).then_inc(SEMS[f"x_in{t}"], 16)
            sp.dma_start(par1[:, :], a["par1"]).then_inc(SEMS["par_in"], 16)
            sp.dma_start(POS[:, :], a["pos"]).then_inc(SEMS["pos_in"], 16)
            sp.dma_start(cst[:, 3 * P:], a["cst"][:, 3 * P:]).then_inc(SEMS["par_in"], 16)
            w = a["wst"]

            def load(k, src, width=1024):
                sp.wait_ge(*n(f"w_free{k}"))
                sp.dma_start(ring[:, k, 0:width], src).then_inc(SEMS[f"w_ready{k}"], 16)

            for k in range(WSLOTS):
                sp.dma_start(ring[:, k, :], w[k]).then_inc(SEMS[f"w_ready{k}"], 16)
            with n.loop("qkv", 3) as i:
                for k in range(WSLOTS):
                    load(k, w[i * 4 + (4 + k)])
            with n.loop("s5", 4) as i:
                for j in range(4):
                    load((2 * j) % 4, a["s5w"][i * 4 + j], width=512)
                    load((2 * j + 1) % 4, w[i * 4 + (16 + j)])
            with n.loop("rest", (a["wst"].shape[0] - 32) // 4) as i:
                for k in range(WSLOTS):
                    load(k, w[i * 4 + (32 + k)])
            for t in range(KD):
                sp.wait_ge(SEMS["x2_ready"], LAYERS * KD + t + 1)
                sp.dma_start(out[t], XK[:, t, :]).then_inc(SEMS["out_done"], 16)
            sp.wait_ge(SEMS["out_done"], 16 * KD)

        @block.tensor
        def _(pe):
            n = Tally("pe", pe, SEMS)
            mm = nc.tensor.matmul
            for p in range(4):
                n.base[f"free{p}"] = 1

            def put(p, counted=True):
                pe.wait_ge(*n.now(f"free{p}"))
                if counted:
                    n.base[f"free{p}"] = n.base.get(f"free{p}", 0) + 1

            def slot(k):
                pe.wait_ge(*n(f"w_ready{k}", 16))

            def freed(ins, k):
                ins.then_inc(SEMS[f"w_free{k}"], 1)

            def norm_sum(t0=0, halves=2, width=H):
                put(0, False)
                for h in range(halves):
                    for k in range(KD):
                        if h == 0:
                            pe.wait_ge(*n("sq_ready"))
                        ins = mm(PS[0][:, h, 0:width], c("ones"), HN[:, k, t0 + h * width:t0 + (h + 1) * width],
                                 start=(k == 0), stop=(k == KD - 1))
                ins.then_inc(SEMS["act_full0"], 1)
                n("hn_ready", KD)

            def chunk_in(b):
                s, value = n.now("hn_ready")
                pe.wait_ge(s, value - (KD - 1 - b))

            pe.wait_ge(SEMS["ones_in"], 16)
            norm_sum()
            pe.wait_ge(SEMS["par_in"], 32)
            with n.loop("uqk", 3) as i:
                for k in range(WSLOTS):
                    slot(k)
                    put(k)
                    for h in range(2):
                        for b in range(KD):
                            if k == 0 and h == 0:
                                chunk_in(b)
                            ins = mm(PS[k][:, h, 0:H], ring[:, k, b * P:b * P + P], HN[:, b, h * H:h * H + H],
                                     start=(b == 0), stop=(b == KD - 1))
                            if h == 0 and b == 0:
                                freed(ins, (k - 1) % 4)
                    ins.then_inc(SEMS[f"act_full{k}"], 1)
            for p in range(3):
                put(p)
            for b in range(KD):
                if b % 2 == 0:
                    slot(b // 2)
                for t, (q0, rows) in enumerate(TILES):
                    ins = mm(PS[t // 2][0:rows, t % 2, :], HN[:, b, q0:q0 + rows],
                             ring[:, b // 2, (b % 2) * 512:(b % 2) * 512 + 512], start=(b == 0), stop=(b == KD - 1))
                    if b % 2 == 0 and t == 0:
                        freed(ins, (b // 2 - 1) % 4)
                    if b == KD - 1 and t in (1, 3, 4):
                        ins.then_inc(SEMS[f"act_full{t // 2}"], 1)
            with n.loop("s5", 4) as i:
                def b_u(j):
                    slot((2 * j) % 4)
                    for r, p in ((0, 1), (1, 3)):
                        put(p)
                        for h in range(2):
                            ins = mm(PS[p][:, h, 0:H], ring[:, (2 * j) % 4, r * P:r * P + P],
                                     PJ[:, i, h * H:h * H + H], start=True, stop=True)
                            if r == 0 and h == 0:
                                freed(ins, (2 * j - 1) % 4)
                        ins.then_inc(SEMS[f"act_full{p}"], 1)

                b_u(0)
                for j in range(4):
                    k = (2 * j + 1) % 4
                    slot(k)
                    put(0)
                    for h in range(2):
                        for b in range(KD):
                            ins = mm(PS[0][:, h, 0:H], ring[:, k, b * P:b * P + P], HN[:, b, h * H:h * H + H],
                                     start=(b == 0), stop=(b == KD - 1))
                    ins.then_inc(SEMS["act_full0"], 1)
                    if j < 3:
                        b_u(j + 1)
                    if j in (1, 2):
                        if j == 1:
                            pe.wait_ge(*n("qk_sq"))
                        put(0)
                        for h in range(2):
                            ins = mm(PS[0][:, h, 0:H], c("pair64"), SQ[:, j - 1, h * H:h * H + H], start=True, stop=True)
                        ins.then_inc(SEMS["act_full0"], 1)
                    if j == 0:
                        put(2)
                    pe.wait_ge(*n("s5_cw"))
                    pe.wait_ge(*n("s5_s"))
                    for h in range(2):
                        for r in range(2):
                            ins = mm(PS[2][:, h, 0:H], CW[:, j % 2, r, :], SS[:, r, h * H:h * H + H],
                                     start=(j == 0 and r == 0), stop=(j == 3 and r == 1), skip_group_check=True)
                            if h == 0 and r == 0:
                                freed(ins, (2 * j) % 4)
                    ins.then_inc(SEMS["dve_full2"] if j == 3 else SEMS["s5_s_free"], 1)

            def score(t):
                q0, rows = TILES[t]
                keys = q0 + rows
                for j in range(2):
                    put(2 + j)
                    n.settle()
                    q = QS[64 * j:64 * j + 64, q0:q0 + rows]
                    kk = KS[64 * j:64 * j + 64, :]
                    ins = mm(PS[2 + j][0:rows, 0, 0:min(keys, 512)], q, kk[:, 0:min(keys, 512)], start=True, stop=True)
                    if keys > 512:
                        ins = mm(PS[2 + j][0:rows, 1, 0:keys - 512], q, kk[:, 512:keys], start=True, stop=True)
                    ins.then_inc(SEMS[f"dve_full{2 + j}"], 1)

            def turn(t):
                q0, rows = TILES[t]
                pe.wait_ge(*n("w_comb"))
                put(0, False)
                n.settle()
                for b in range(t + 1):
                    k0 = TILES[b][0]
                    ins = nc.tensor.transpose(ps(0)[:, b * P:b * P + rows], WC[0:rows, t % 2, k0:k0 + P],
                                              c("ident", 0, rows, rows))
                ins.then_inc(SEMS["act_full0"], 1)

            def weigh(h, t):
                q0, rows = TILES[t]
                pe.wait_ge(*n("wt_ready"))
                put(1)
                for b in range(t + 1):
                    ins = mm(PS[1][0:rows, 0, 0:P], WT[:, b, 0:rows], V[:, b, bass.ds(h * P, P)],
                             start=(b == 0), stop=(b == t))
                ins.then_inc(SEMS["act_full1"], 1)

            n("wt_ready", 2)
            pe.wait_ge(*n("qk_n", HEADS))
            pe.wait_ge(*n("qst"))
            score(0)
            score(1)
            with n.loop("att", HEADS) as h:
                score(2)
                turn(0)
                score(3)
                weigh(h, 0)
                turn(1)
                score(4)
                weigh(h, 1)
                turn(2)
                weigh(h, 2)
                turn(3)
                pe.wait_ge(*n("qst"))
                score(0)
                weigh(h, 3)
                turn(4)
                score(1)
                weigh(h, 4)
            pe.wait_ge(*n("o_norm"))
            for h in range(HEADS):
                put(h)
                for t, (q0, rows) in enumerate(TILES):
                    ins = nc.tensor.transpose(ps(h)[:, t * P:t * P + rows], OR[0:rows, h * 5 + t, :], c("ident", 0, rows, rows))
                ins.then_inc(SEMS[f"act_full{h}"], 1)

            pe.wait_ge(*n("ys_gelu"))
            for m in range(4):
                if m % 2 == 0:
                    slot(m // 2)
                put(m, False)
                for h in range(2):
                    for b in range(4):
                        w0 = (m % 2) * 512 + b * P
                        ins = mm(PS[m][:, h, 0:H], ring[:, m // 2, w0:w0 + P], PJ[:, b, h * H:h * H + H],
                                 start=(b == 0), stop=(b == 3))
                        if m % 2 == 0 and h == 0 and b == 0:
                            freed(ins, (m // 2 - 1) % 4)
                ins.then_inc(SEMS[f"act_full{m}"], 1)
            pe.wait_ge(*n("ys_ready"))
            with n.loop("mix", 2) as i:
                for k in range(WSLOTS):
                    s = (2 + k) % 4
                    slot(s)
                    for x in range(2):
                        p = 2 * (k % 2) + x
                        put(p)
                        for h in range(2):
                            for b in range(4):
                                src = PJ[:, (8 + b) if x == 0 else (4 + b), h * H:h * H + H]
                                ins = mm(PS[p][:, h, 0:H], ring[:, s, (4 * x + b) * P:(4 * x + b) * P + P], src,
                                         start=(b == 0), stop=(b == 3))
                                if x == 0 and h == 0 and b == 0:
                                    freed(ins, (s - 1) % 4)
                        ins.then_inc(SEMS[f"dve_full{p}"], 1)
            pe.wait_ge(*n("mix_ready"))
            with n.loop("wo", 2) as i:
                for k in range(WSLOTS):
                    s = (2 + k) % 4
                    slot(s)
                    put(k)
                    for h in range(2):
                        for b in range(KD):
                            ins = mm(PS[k][:, h, 0:H], ring[:, s, b * P:b * P + P], PJ[:, 12 + b, h * H:h * H + H],
                                     start=(b == 0), stop=(b == KD - 1))
                            if h == 0 and b == 0:
                                freed(ins, (s - 1) % 4)
                    ins.then_inc(SEMS[f"dve_full{k}"], 1)
            norm_sum()
            with n.loop("up", NFF // 2) as i:
                for k in range(WSLOTS):
                    s = (2 + k) % 4
                    slot(s)
                    put(k)
                    for h in range(2 if k % 2 == 0 else 1):
                        for b in range(KD):
                            dst = PS[k][:, h, 0:257] if k % 2 == 0 else PS[k][:, 0, :]
                            src = HN[:, b, 14 + 257 * h:271 + 257 * h] if k % 2 == 0 else HN[:, b, NMETA:T]
                            if k == 0 and h == 0:
                                chunk_in(b)
                            ins = mm(dst, ring[:, s, b * P:b * P + P], src, start=(b == 0), stop=(b == KD - 1))
                            if h == 0 and b == 0:
                                freed(ins, (s - 1) % 4)
                    ins.then_inc(SEMS[f"act_full{k}" if k % 2 == 0 else f"dve_full{k}"], 1)
            pe.wait_ge(*n("hid_done"))
            for p in range(4):
                put(p)

            def down(s, k, start=False, stop=False):
                slot(s)
                for m in range(KD):
                    ins = mm(PS[m // 2][:, m % 2, :], ring[:, s, m * P:m * P + P], hid[:, k, :], start=start, stop=stop)
                    if m == 0:
                        freed(ins, (s - 1) % 4)
                    if stop and m % 2 == 1:
                        ins.then_inc(SEMS[f"dve_full{m // 2}"], 1)

            down(2, 0, start=True)
            down(3, 1)
            with n.loop("down", 4) as i:
                for k in range(WSLOTS):
                    down(k, i * 4 + (2 + k))
            for k in range(WSLOTS):
                down(k, NFF - 4 + k, stop=(k == 3))

            with n.loop("layer", LAYERS) as l:
                norm_sum(0, 1, 512)

                def project(k, p, first=False):
                    slot(k)
                    put(p)
                    for b in range(KD):
                        if first:
                            chunk_in(b)
                        ins = mm(PS[p][:, 0, :], ring[:, k, b * P:b * P + P], HN[:, b, 0:SEQ], start=(b == 0), stop=(b == KD - 1))
                        if b == 0:
                            freed(ins, (k - 1) % 4)
                    ins.then_inc(SEMS[f"act_full{p}"], 1)

                def gate(g, p):
                    project(g % WSLOTS, p)

                with n.loop("proj", 2) as i:
                    for k in range(WSLOTS):
                        project(k, k, k == 0)
                for k in range(WSLOTS):
                    project(k, k)
                with n.loop("lag", 2) as i:
                    for k in range(8):
                        if k % 2 == 0:
                            project(k // 2, k // 2 % 2)
                        p = 2 + k % 2
                        pe.wait_ge(*n("b_m"))
                        put(p)
                        for cc in range(2):
                            ins = mm(PS[p][:, cc, :], c("pair64"), MB[:, k % 2, cc, :], start=True, stop=True)
                        ins.then_inc(SEMS[f"dve_full{p}"], 1)
                pe.wait_ge(*n("b_m"))
                put(0)
                for t in range(4):
                    for cc in range(2):
                        o = (t * 2 + cc) * P
                        ins = nc.tensor.transpose(ps(0)[:, o:o + P], KH[:, cc, t * P:t * P + P], c("ident"))
                ins.then_inc(SEMS["act_full0"], 1)
                put(1)
                for t in range(4):
                    for cc in range(2):
                        o = (t * 2 + cc) * P
                        ins = nc.tensor.transpose(ps(1)[:, o:o + P], PJ2[:, 4 + cc, t * P:t * P + P], c("ident"))
                ins.then_inc(SEMS["act_full1"], 1)
                gate(0, 0)
                gate(1, 1)
                for t in range(4):
                    p = 2 + t % 2
                    pe.wait_ge(*n("b_ve"))
                    put(p)
                    for cc in range(2):
                        for hh in range(2):
                            ins = mm(PS[p][64 * hh:64 * hh + 64, cc, :], KHT[:, t, cc * P + 64 * hh:cc * P + 64 * hh + 64],
                                     VE[t % 2][:, (2 * cc + hh) * 512:(2 * cc + hh) * 512 + 512], start=True, stop=True)
                    ins.then_inc(SEMS[f"act_full{p}"], 1)
                pe.wait_ge(*n("a_ca"))
                put(1, False)
                for cc in range(2):
                    ins = mm(PS[1][:, 0, :], c("ones"), CA[:, cc, :], start=(cc == 0), stop=(cc == 1))
                ins.then_inc(SEMS["dve_full1"], 1)
                gate(2, 2)
                pe.wait_ge(*n("d_sq"))
                put(0)
                for b in range(2):
                    mm(PS[0][:, 0, :], c("ones"), SQD[b], start=(b == 0), stop=(b == 1))
                mm(PS[0][:, 1, :], c("ones"), SQD[2], start=True, stop=True).then_inc(SEMS["act_full0"], 1)
                gate(3, 3)
                pe.wait_ge(*n("b_s"))
                pe.wait_ge(*n("qgz", 2))
                put(0)
                for cc in range(2):
                    us = (US0, US1)[cc].rearrange("p (v i) -> p v i", i=NBLK)
                    for i in range(1, NBLK):
                        for hh in range(2):
                            ins = mm(PS[0][64 * hh:64 * hh + 64, cc, LAG * i:LAG * i + LAG], us[:, :, i - 1],
                                     QZ[:, 2 * cc + hh, LAG * i:LAG * i + LAG], start=True, stop=True)
                ins.then_inc(SEMS["dve_full0"], 1)
                pe.wait_ge(*n("a_sq"))
                put(1, False)
                for cc in range(2):
                    ins = mm(PS[1][:, 1, :], c("ones"), SQA[:, cc, :], start=(cc == 0), stop=(cc == 1))
                ins.then_inc(SEMS["act_full1"], 1)
                pe.wait_ge(*n("b_sq"))
                put(2, False)
                for cc in range(2):
                    ins = mm(PS[2][:, cc, :], c("pair64"), MB[:, 0, cc, :], start=True, stop=True)
                ins.then_inc(SEMS["act_full2"], 1)
                gate(4, 0)
                gate(5, 3)
                pe.wait_ge(*n("a_h"))
                put(1)
                for m in range(2):
                    for b in range(2):
                        o = SWP + (2 * m + b) * P
                        ins = mm(PS[1][:, m, :], SW[:, o:o + P], CA[:, b, :], start=(b == 0), stop=(b == 1))
                ins.then_inc(SEMS["dve_full1"], 1)
                gate(6, 2)
                gate(7, 3)
                put(0)
                mm(PS[0][:, 0, :], c("rot"), PJ2[:, 16, :], start=True, stop=True).then_inc(SEMS["act_full0"], 1)
                pe.wait_ge(*n("d_n"))
                for h in range(HEADS):
                    p = 2 + h % 2
                    put(p)
                    for b in range(2):
                        mm(PS[p][0:QKR, 0, :], SW[:, SWQ + (2 * h + b) * QKR:SWQ + (2 * h + b + 1) * QKR], CQ[:, b, :],
                           start=(b == 0), stop=(b == 1))
                    for b in range(2):
                        ins = mm(PS[p][64:96, 1, :], SW[:, SWR + (2 * h + b) * 32:SWR + (2 * h + b + 1) * 32], CQ[:, b, :],
                                 start=(b == 0), stop=(b == 1))
                    ins.then_inc(SEMS[f"act_full{p}"], 1)
                pe.wait_ge(*n("c_dt"))
                for g in range(2):
                    put(2 + g)
                    for e in range(2):
                        ins = mm(PS[2 + g][:, e, :], c("sel4", (2 * g + e) * P, P, 4), AC4[0:4, :], start=True, stop=True)
                    ins.then_inc(SEMS[f"act_full{2 + g}"], 1)
                put(0)
                n.settle()
                for t in range(4):
                    for x in range(2):
                        ins = nc.tensor.transpose(ps(0)[:, t * 8 + 4 * x:t * 8 + 4 * x + 4], (DT4, AC4)[x][0:4, t * P:t * P + P],
                                                  c("ident", 0, 4, 4))
                ins.then_inc(SEMS["act_full0"], 1)
                pe.wait_ge(*n("c_x"))
                put(1)
                for t in range(4):
                    for cc in range(2):
                        o = (t * 2 + cc) * P
                        ins = nc.tensor.transpose(ps(1)[:, o:o + P], PJ2[:, 10 + cc, t * P:t * P + P], c("ident"))
                ins.then_inc(SEMS["dve_full1"], 1)
                put(0)
                for t in range(4):
                    for cc in range(2):
                        o = (t * 2 + cc) * P
                        ins = nc.tensor.transpose(ps(0)[:, o:o + P], PJ2[:, 12 + cc, t * P:t * P + P], c("ident"))
                ins.then_inc(SEMS["act_full0"], 1)
                put(3)
                for g in range(2):
                    for t in range(4):
                        ts_ = slice(t * P, t * P + P)
                        ins = mm(PS[3][:, g, ts_], PJ2[:, 12 + g, ts_], PJ2[:, 14 + g, ts_], start=True, stop=True)
                ins.then_inc(SEMS["dve_full3"], 1)
                for g in range(2):
                    put(0)
                    for x in range(2):
                        hk = SWK + (2 * g + x) * 64
                        ins = mm(PS[0][0:64, x, :], SW[:, hk:hk + 64], CK, start=True, stop=True)
                    ins.then_inc(SEMS["act_full0"], 1)
                pe.wait_ge(*n("c_wx"))
                pe.wait_ge(*n("c_bt"))
                put(2)
                for t in range(3):
                    for g in range(2):
                        o = (t * 2 + g) * P
                        ins = mm(ps(2)[:, o:o + P], BT[:, t, g * P:g * P + P],
                                 WX[:, t, 2 * g:2 * g + 2, :].rearrange("p a b -> p (a b)"), start=True, stop=True)
                ins.then_inc(SEMS["dve_full2"], 1)
                put(1)
                for t in range(4):
                    ins = mm(ps(1)[:, t * 256:t * 256 + 256], CK[:, t * P:t * P + P], SW[:, SWV:SWV + 256], start=True, stop=True)
                ins.then_inc(SEMS["act_full1"], 1)
                pe.wait_ge(*n("c_hs"))
                pe.wait_ge(*n("c_cme"))
                pe.wait_ge(*n("c_sc"))
                put(0)
                for h in range(HEADS):
                    g, e = h // 2, h % 2
                    for t in range(4):
                        ts_ = slice(t * P, t * P + P)
                        o = PS[0][64 * e:64 * e + 64, g, ts_]
                        ins = mm(o, XDT[:, t, h, :], DD[:, h, ts_], start=True, stop=(t == 0))
                        if t:
                            ins = mm(o, HS[:, t - 1, h * 64:h * 64 + 64], CME[:, h, ts_], start=False, stop=True)
                ins.then_inc(SEMS["dve_full0"], 1)
                def d_score(h, t):
                    p = 2 + t % 2
                    put(p)
                    mm(PS[p][:, 0, 0:t * P + P], QST[0:QKR, t * P:t * P + P], KF[0:QKR, h, 0:t * P + P],
                       start=True, stop=True).then_inc(SEMS[f"dve_full{p}"], 1)

                def d_turn(t):
                    pe.wait_ge(*n("d_ex"))
                    put(0, False)
                    for b in range(t + 1):
                        ins = nc.tensor.transpose(PS[0][:, t % 2, b * P:b * P + P], SD[:, t, b * P:b * P + P], c("ident"))
                    ins.then_inc(SEMS["act_full0"], 1)

                def d_weigh(h, t):
                    pe.wait_ge(*n("d_wt"))
                    put(1)
                    for b in range(t + 1):
                        ins = mm(PS[1][:, t % 2, 0:64], WD[:, t % 2, b, :], VD[:, b, bass.ds(h * 64, 64)],
                                 start=(b == 0), stop=(b == t))
                    ins.then_inc(SEMS["dve_full1"], 1)

                pe.wait_ge(*n("d_v"))
                pe.wait_ge(*n("qst"))
                d_score(0, 0)
                d_score(0, 1)
                pe.wait_ge(*n("c_sq"))
                put(1)
                for g in range(2):
                    ins = mm(PS[1][:, g, :], c("ones"), SQC[:, g, :], start=True, stop=True)
                ins.then_inc(SEMS["act_full1"], 1)
                with n.loop("mla", HEADS) as h:
                    d_score(h, 2)
                    d_turn(0)
                    d_score(h, 3)
                    d_turn(1)
                    d_weigh(h, 0)
                    d_turn(2)
                    d_weigh(h, 1)
                    pe.wait_ge(*n("qst"))
                    d_score(h + 1, 0)
                    d_turn(3)
                    d_weigh(h, 2)
                    d_score(h + 1, 1)
                    d_weigh(h, 3)
                pe.wait_ge(*n("d_ex", 2))
                pe.wait_ge(*n("d_o", 4 * HEADS))
                put(0)
                for cc in range(2):
                    for t in range(4):
                        ins = nc.tensor.transpose(PS[0][:, cc, t * P:t * P + P], OD[:, t, cc * P:cc * P + P], c("ident"))
                ins.then_inc(SEMS["dve_full0"], 1)
                pe.wait_ge(*n("y_ready"))
                with n.loop("wout", 2) as i:
                    for k in range(WSLOTS):
                        slot(k)
                        put(k)
                        for b in range(KD):
                            ins = mm(PS[k][:, 0, :], ring[:, k, b * P:b * P + P], PJ2[:, 20 + b, :], start=(b == 0), stop=(b == KD - 1))
                            if b == 0:
                                freed(ins, (k - 1) % 4)
                        ins.then_inc(SEMS[f"act_full{k}"], 1)
                put(0, False)
                for k in range(KD):
                    pe.wait_ge(*n("y_sq"))
                    ins = mm(PS[0][:, 0, :], c("ones"), PJ2[:, k, :], start=(k == 0), stop=(k == KD - 1))
                ins.then_inc(SEMS["act_full0"], 1)

        @block.scalar
        def _(act):
            n = Tally("act", act, SEMS)
            af = nc.scalar.activation

            def step(ins):
                ins.then_inc(SEMS["act_step"], 1)
                act.wait_ge(*n("act_step"))

            def mark(name):
                n.settle()
                act.drain().then_inc(SEMS[name], 1)

            act.wait_ge(SEMS["eps_ready"], 1)

            def norm(src, ready, nb=2, width=H):
                for k in range(KD):
                    ready(k)
                    af(HN[:, k, 0:nb * width], src[:, k, :], ACT.Square).then_inc(SEMS["sq_ready"], 1)
                root(nb, width)

            def root(nb=2, width=H):
                act.wait_ge(*n("act_full0"))
                af(R[:, 0:nb * width].rearrange("p (a b) -> p a b", a=nb), PS[0][:, 0:nb, 0:width], ACT.Sqrt,
                   bias=epsc[:, 0:1], scale=1.0 / D).then_inc(SEMS["rms_root"], 1)

            norm(X[:, :, :], lambda k: act.wait_ge(SEMS[f"x_in{k}"], 16))
            act.wait_ge(SEMS["par_in"], 32)
            af(s5c[:, 0, :], par1[:, V1["ldt"][0]:V1["ldt"][1]], ACT.Exp).then_inc(SEMS["s5_dt"], 1)
            act.wait_ge(*n("trig_arg"))
            af(s5c[:, 2, :], s5c[:, 2, :], ACT.Exp)
            af(lamc[:, 2:4], lamc[:, 0:2], ACT.Exp)
            af(s5c[:, 3, :], s5c[:, 3, :], ACT.Sin)
            af(s5c[:, 4, :], s5c[:, 4, :], ACT.Sin).then_inc(SEMS["trig"], 1)
            with n.loop("uqk", 3) as i:
                for k in range(WSLOTS):
                    act.wait_ge(*n(f"act_full{k}"))
                    af(two(PJ[:, i * 4 + k, :]), halves(k), ACT.Copy).then_inc(SEMS[f"free{k}"], 1)
            mark("u_ready")
            act.wait_ge(*n("v_zero"))
            for t, (q0, rows) in enumerate(TILES):
                if t % 2 == 0:
                    act.wait_ge(*n(f"act_full{t // 2}"))
                ins = af(V[0:rows, t, :], PS[t // 2][0:rows, t % 2, :], ACT.Copy)
                if t in (1, 3, 4):
                    ins.then_inc(SEMS[f"free{t // 2}"], 1)
            mark("v_ready")
            with n.loop("s5", 4) as i:
                def x_out(j):
                    act.wait_ge(*n("s5_x_free"))
                    for r, p in ((0, 1), (1, 3)):
                        act.wait_ge(*n(f"act_full{p}"))
                        af(two(XS[:, j % 2, r, :]), halves(p), ACT.Copy).then_inc(SEMS[f"free{p}"], 1)
                    mark("s5_x")

                x_out(0)
                af(SQ[:, 0, :], PJ[:, i + 4, :], ACT.Square)
                af(SQ[:, 1, :], PJ[:, i + 8, :], ACT.Square).then_inc(SEMS["qk_sq"], 1)
                for j in range(4):
                    act.wait_ge(*n("act_full0"))
                    af(two(PJ[:, i * 4 + (12 + j), :]), halves(0), ACT.Tanh, scale=0.5).then_inc(SEMS["free0"], 1)
                    if j < 3:
                        x_out(j + 1)
                    if j in (1, 2):
                        act.wait_ge(*n("act_full0"))
                        af(two(RT[:, j - 1, :]), halves(0), ACT.Sqrt, bias=epsc[:, 0:1], scale=1.0 / 64)\
                            .then_inc(SEMS["free0"], 1)
                        mark("qk_root")
            act.wait_ge(*n("s5_y"))
            af(PJ[:, 0:4, :], PJ[:, 0:4, :], ACT.Gelu_apprx_tanh).then_inc(SEMS["ys_gelu"], 1)
            def queries(h):
                af(QS[:, :], PJ[:, h + 4, :], ACT.Copy)
                af(KS[:, :], PJ[:, h + 8, :], ACT.Copy).then_inc(SEMS["qst"], 1)

            def exps(t):
                q0, rows = TILES[t]
                act.wait_ge(*n("sc_ready"))
                for j in range(2):
                    x = SX[0:rows, t % 3, j, 0:q0 + rows]
                    col = 2 * (t % 3) + j
                    af(x, x, ACT.Exp, bias=st[0:rows, MX + col:MX + col + 1], accum_out=st[0:rows, SM + col:SM + col + 1])
                mark("ex_ready")

            def turned(t):
                q0, rows = TILES[t]
                act.wait_ge(*n("act_full0"))
                if t:
                    af(WT[:, 1:t + 1, 0:rows], ps(0)[:, P:(t + 1) * P].rearrange("p (a b) -> p a b", b=P)[:, :, 0:rows], ACT.Copy)
                af(WT[0:NMETA, 0, 0:rows], ps(0)[0:NMETA, 0:rows], ACT.Copy).then_inc(SEMS["wt_ready"], 1)

            def weighed(h, t):
                q0, rows = TILES[t]
                act.wait_ge(*n("act_full1"))
                n.settle()
                rs = st[0:rows, RC5 + 2 * t:RC5 + 2 * t + 1]
                af(JK[0:rows, 0:P], PS[1][0:rows, 0, 0:P], ACT.Square, scale=rs, accum_out=st[0:rows, bass.ds(h * 5 + (OS + t), 1)])
                af(OR[0:rows, h * 5 + t, :], PS[1][0:rows, 0, 0:P], ACT.Copy, scale=rs).then_inc(SEMS["free1"], 1)

            for _ in range(2):
                act.sem_inc(SEMS["wt_ready"], 1)
            act.wait_ge(*n("qk_n", HEADS))
            queries(0)
            exps(0)
            exps(1)
            with n.loop("att", HEADS) as h:
                exps(2)
                turned(0)
                weighed(h, 0)
                exps(3)
                turned(1)
                weighed(h, 1)
                exps(4)
                queries(h + 1)
                turned(2)
                weighed(h, 2)
                turned(3)
                exps(0)
                weighed(h, 3)
                turned(4)
                exps(1)
                weighed(h, 4)
            n.settle()
            step(act.drain())
            af(st[:, OS:OS + 5 * HEADS], st[:, OS:OS + 5 * HEADS], ACT.Sqrt, bias=epsc[:, 0:1], scale=1.0 / P)\
                .then_inc(SEMS["o_root"], 1)
            for h in range(HEADS):
                act.wait_ge(*n(f"act_full{h}"))
                af(PJ[:, h + 4, 0:NMETA], ps(h)[:, 0:NMETA], ACT.Copy, scale=lamc[:, 6:7])
                af(PJ[:, h + 4, NMETA:T], ps(h)[:, P:P + SEQ], ACT.Copy, scale=lamc[:, 6:7]).then_inc(SEMS[f"free{h}"], 1)
            for m in range(4):
                act.wait_ge(*n(f"act_full{m}"))
                af(two(TH[:, m, :]), halves(m), ACT.Tanh, scale=0.5, bias=glub2[:, m:m + 1]).then_inc(SEMS["glu_th"], 1)
            with n.loop("wo", 2) as i:
                for k in range(WSLOTS):
                    act.wait_ge(*n("h_ready"))
                    af(HN[:, i * 4 + k, :], X[:, i * 4 + k, :], ACT.Square).then_inc(SEMS["sq_ready"], 1)
            root()
            with n.loop("up", NFF // 2) as i:
                for m in range(2):
                    act.wait_ge(*n(f"act_full{2 * m}"))
                    af(FA[:, :].rearrange("p (a b) -> p a b", a=2), PS[2 * m][:, :, 0:257], ACT.Copy).then_inc(SEMS["ffa"], 1)
                    act.wait_ge(*n("ffc"))
                    af(GL[:, :], CV[:, :], ACT.Gelu_apprx_tanh).then_inc(SEMS["ffg"], 1)

            act.wait_ge(*n("d_trig_arg"))
            af(COS[:, :], COS[:, :], ACT.Sin)
            af(SIN[:, :], SIN[:, :], ACT.Sin).then_inc(SEMS["d_trig"], 1)

            with n.loop("layer", LAYERS) as l:
                norm(XK, lambda k: act.wait_ge(*n("x2_ready")), 1, 512)

                def evac(dst, p):
                    act.wait_ge(*n(f"act_full{p}"))
                    n.settle()
                    af(dst, PS[p][:, 0, :], ACT.Copy).then_inc(SEMS[f"free{p}"], 1)

                with n.loop("proj", 2) as i:
                    for k in range(WSLOTS):
                        evac(PJ2[:, i * 4 + k, :], k)
                n.settle()
                step(act.drain())
                act.wait_ge(*n("lb_arg"))
                af(LB[:, 4:6], LB[:, 4:6], ACT.Tanh, scale=0.5).then_inc(SEMS["lb_th"], 1)
                af(PJ2[:, 0:2, :], PJ2[:, 0:2, :], ACT.Tanh, scale=0.5).then_inc(SEMS["b_th"], 1)
                for k in range(WSLOTS):
                    evac(PJ2[:, 8 + k, :], k)
                n.settle()
                step(act.drain())
                af(PJ2[:, 8:10, :], PJ2[:, 8:10, :], ACT.Tanh, scale=0.5).then_inc(SEMS["a_th"], 1)
                with n.loop("lag", 2) as i:
                    for k in range(WSLOTS):
                        evac(PJ2[:, i * 4 + (12 + k), :], k % 2)
                n.settle()
                step(act.drain())
                act.wait_ge(*n("act_full0"))
                af(KHT.rearrange("p a b -> p (a b)"), ps(0), ACT.Copy).then_inc(SEMS["free0"], 1)
                act.wait_ge(*n("act_full1"))
                af(VT.rearrange("p a b -> p (a b)"), ps(1), ACT.Copy).then_inc(SEMS["free1"], 1)
                mark("b_tok")
                evac(PJ2[:, GATES[0], :], 0)
                evac(PJ2[:, GATES[1], :], 1)
                for t in range(4):
                    p = 2 + t % 2
                    act.wait_ge(*n(f"act_full{p}"))
                    for cc in range(2):
                        us = (US0, US1)[cc].rearrange("p (v i) -> p i v", i=NBLK)
                        ins = af(us[:, 8 * t:8 * t + 8, :], PS[p][:, cc, :].rearrange("p (i v) -> p i v", i=8), ACT.Copy)
                    ins.then_inc(SEMS[f"free{p}"], 1)
                    mark("b_us")
                for b in range(2):
                    af(SQD[b], CQ[:, b, :], ACT.Square)
                af(SQD[2], CK, ACT.Square).then_inc(SEMS["d_sq"], 1)
                evac(PJ2[:, GATES[2], :], 2)
                act.wait_ge(*n("act_full0"))
                af(RD[:, 0, :], PS[0][:, 0, :], ACT.Sqrt, bias=epsc[:, 0:1], scale=1.0 / 256)
                af(RD[:, 1, :], PS[0][:, 1, :], ACT.Sqrt, bias=epsc[:, 0:1], scale=1.0 / P).then_inc(SEMS["free0"], 1)
                mark("d_root")
                evac(PJ2[:, GATES[3], :], 3)
                act.wait_ge(*n("a_xc"))
                af(SQA[:, :, :], CA[:, :, :], ACT.Square).then_inc(SEMS["a_sq"], 1)
                n.settle()
                step(act.drain())
                act.wait_ge(*n("b_s"))
                af(FREE[0], PJ2[:, 22:26, :], ACT.Tanh, scale=0.5).then_inc(SEMS["gate_th"], 1)
                act.wait_ge(*n("b_acc2"))
                af(MB[:, 0, :, :], ACC[:, :, :], ACT.Square).then_inc(SEMS["b_sq"], 1)
                act.wait_ge(*n("act_full1"))
                af(RA, PS[1][:, 1, :], ACT.Sqrt, bias=epsc[:, 1:2], scale=1.0 / 256).then_inc(SEMS["a_root"], 1)
                act.wait_ge(*n("act_full2"))
                af(RB[:, :, :], PS[2][:, :, :], ACT.Sqrt, bias=epsc[:, 0:1], scale=1.0 / 64).then_inc(SEMS["b_root"], 1)
                act.wait_ge(*n("a_x"))
                af(SQA[:, :, :], CA[:, :, :], ACT.Tanh, scale=0.5).then_inc(SEMS["a_xt"], 1)
                evac(PJ2[:, GATES[4], :], 0)
                evac(PJ2[:, GATES[5], :], 3)
                act.wait_ge(*n("c_dtabs"))
                step(af(DD[0:4, 0, :], DD[0:4, 0, :], ACT.Exp, scale=-1.0))
                af(LB2[0:4, 0:1], v2("alog", rows=4), ACT.Exp)
                af(DD[0:4, 0, :], DD[0:4, 0, :], ACT.Ln, bias=epsc[0:4, 2:3]).then_inc(SEMS["c_dtln"], 1)
                evac(PJ2[:, GATES[6], :], 2)
                evac(PJ2[:, GATES[7], :], 3)
                act.wait_ge(*n("act_full0"))
                af(KRR[rr, :], PS[0][rr, 0, :], ACT.Copy).then_inc(SEMS["free0"], 1)

                def query(h):
                    p = 2 + h % 2
                    act.wait_ge(*n(f"act_full{p}"))
                    af(QF[0:QKR, h, :], PS[p][0:QKR, 0, :], ACT.Copy, scale=QKR ** -0.5)
                    af(QR[rr, h, :], PS[p][rr, 1, :], ACT.Copy, scale=QKR ** -0.5).then_inc(SEMS[f"free{p}"], 1)

                query(0)
                query(1)
                n.settle()
                step(act.drain())
                for x in (0, 1):
                    ins = af(FREE[1][:, 2 * x:2 * x + 2, :], PJ2[:, (20, 26)[x]:(22, 28)[x], :], ACT.Tanh, scale=0.5)
                ins.then_inc(SEMS["gate_th"], 1)
                act.wait_ge(*n("c_cx"))
                af(PJ2[:, 10:16, :], CX[:, :, :], ACT.Tanh).then_inc(SEMS["c_th"], 1)
                query(2)
                query(3)
                mark("d_qe")
                for g in range(2):
                    act.wait_ge(*n(f"act_full{2 + g}"))
                    af(EAB[:, 2 * g:2 * g + 2, :], PS[2 + g][:, :, :], ACT.Exp)
                    af(ACB[:, 2 * g:2 * g + 2, :], PS[2 + g][:, :, :], ACT.Copy).then_inc(SEMS[f"free{2 + g}"], 1)
                act.wait_ge(*n("act_full0"))
                af(COL.rearrange("p a b -> p (a b)"), ps(0)[:, 0:32], ACT.Copy).then_inc(SEMS["free0"], 1)
                mark("c_acb")
                act.wait_ge(*n("act_full0"))
                af(BT.rearrange("p a b -> p (a b)"), ps(0), ACT.Copy).then_inc(SEMS["free0"], 1)
                mark("c_bt")
                for g in range(2):
                    act.wait_ge(*n("act_full0"))
                    af(KF[0:64, 2 * g:2 * g + 2, :], PS[0][0:64, :, :], ACT.Copy).then_inc(SEMS["free0"], 1)
                act.wait_ge(*n("c_wd"))
                af(WCOL[:, :, :], WCOL[:, :, :], ACT.Exp).then_inc(SEMS["c_we"], 1)
                act.wait_ge(*n("c_d"))
                af(DD[:, :, :], DD[:, :, :], ACT.Exp).then_inc(SEMS["c_de"], 1)
                act.wait_ge(*n("act_full1"))
                af(VD.rearrange("p a b -> p (a b)"), ps(1), ACT.Copy).then_inc(SEMS["free1"], 1)
                mark("d_v")

                def d_queries(h):
                    af(QST[0:QKR, :], QF[0:QKR, h, :], ACT.Copy).then_inc(SEMS["qst"], 1)

                def d_exps(t):
                    act.wait_ge(*n("d_sc"))
                    x = SD[:, t, 0:t * P + P]
                    af(x, x, ACT.Exp, bias=sd[:, t:t + 1], accum_out=sd[:, 4 + t:5 + t])
                    mark("d_ex")

                def d_turned(t):
                    act.wait_ge(*n("act_full0"))
                    af(WD[:, t % 2, 0:t + 1, :], PS[0][:, t % 2, 0:t * P + P].rearrange("p (a b) -> p a b", b=P), ACT.Copy)\
                        .then_inc(SEMS["d_wt"], 1)

                act.wait_ge(*n("d_v"))
                act.wait_ge(*n("d_q"))
                d_queries(0)
                act.wait_ge(*n("c_yc"))
                af(SQC[:, :, :], YC[:, :, :], ACT.Square).then_inc(SEMS["c_sq"], 1)
                d_exps(0)
                d_exps(1)
                act.wait_ge(*n("act_full1"))
                af(RC[:, :, :], PS[1][:, :, :], ACT.Sqrt, bias=epsc[:, 0:1], scale=1.0 / P).then_inc(SEMS["free1"], 1)
                mark("c_root")
                with n.loop("mla", HEADS) as h:
                    d_exps(2)
                    d_turned(0)
                    d_exps(3)
                    d_queries(h + 1)
                    d_turned(1)
                    d_turned(2)
                    d_exps(0)
                    d_turned(3)
                    d_exps(1)
                with n.loop("wout", 2) as i:
                    for k in range(WSLOTS):
                        act.wait_ge(*n(f"act_full{k}"))
                        af(PJ2[:, i * 4 + k, :], PS[k][:, 0, :], ACT.Square).then_inc(SEMS["y_sq"], 1)
                        af(HNY[:, i * 4 + k, :], PS[k][:, 0, :], ACT.Copy).then_inc(SEMS[f"free{k}"], 1)
                act.wait_ge(*n("act_full0"))
                af(R[:, 0:SEQ], PS[0][:, 0, :], ACT.Sqrt, bias=epsc[:, 0:1], scale=1.0 / D).then_inc(SEMS["rms_root"], 1)

        @block.gpsimd
        def _(pool):
            n = Tally("pool", pool, SEMS)
            tt = nc.gpsimd.tensor_tensor
            pool.wait_ge(*n("s5_tab"))
            A4 = ph_a.rearrange("p r (c b) -> p r c b", b=8)
            B4 = ph_b.rearrange("p r (c j) -> p r c j", j=66)

            def step(ins):
                ins.then_inc(SEMS["pool_step"], 1)
                pool.wait_ge(*n("pool_step"))

            for k in (0, 2):
                n(f"w_ready{k}", 4 * 16)
            with n.loop("s5", 4) as i:
                for j in range(4):
                    pool.wait_ge(*n(f"w_ready{2 * j % 4}", 16))
                    craw = ring[:, (2 * j) % 4, 256:512].rearrange("p (r c) -> p r c", r=2)
                    n.settle()
                    for x, f in ((0, 8), (1, 9)):
                        ins = tt(CWF[:, x, :, :], craw, s5c[:, f, bass.ds(i * 4 + j, 1)].unsqueeze(2).broadcast_to([P, 2, P]), ALU.mult)
                    step(ins)
                    if j == 1:
                        pool.wait_ge(*n.now("dve_full2"))
                    else:
                        pool.wait_ge(*(n("s5_s_free") if j else n.now("s5_s_free")))
                    tt(CW[:, j % 2, 0, :], CWF[:, 0, 0, :], CWF[:, 1, 1, :], ALU.add)
                    step(tt(CW[:, j % 2, 1, :], CWF[:, 1, 0, :], CWF[:, 0, 1, :], ALU.subtract))
                    pool.sem_inc(SEMS["s5_cw"], 1)
                    pool.wait_ge(*n("s5_x_free"))

                    def outer(dst, r, s):
                        x = A4[:, r, i * 4 + j, :].unsqueeze(2).broadcast_to([P, 8, 66])
                        y = B4[:, s, i * 4 + j, :].unsqueeze(1).broadcast_to([P, 8, 66])
                        return tt(dst.rearrange("p (b j) -> p b j", b=8), x, y, ALU.mult)

                    outer(PH[:, j % 2, 0, :], 0, 0)
                    outer(PT[:, 0, :], 1, 1)
                    outer(PH[:, j % 2, 1, :], 0, 1)
                    step(outer(PT[:, 1, :], 1, 0))
                    tt(PH[:, j % 2, 0, :], PH[:, j % 2, 0, :], PT[:, 0, :], ALU.subtract)
                    tt(PH[:, j % 2, 1, :], PH[:, j % 2, 1, :], PT[:, 1, :], ALU.add).then_inc(SEMS["s5_ph"], 1)
                    pool.wait_ge(*n("s5_ph"))
                n("s5_s_free")
                n("dve_full2")

            with n.loop("layer", LAYERS) as l:
                pool.wait_ge(*n("x2_ready", KD))
                pool.dma_start(SW[:, :], a["small"][l]).then_inc(SEMS["small_in"], 16)
                pool.wait_ge(*n("b_kh"))
                n.settle()
                nc.gpsimd.memset(ACC[:, :, :], 0.0)
                n.settle()
                step(pool.drain())
                pool.sem_inc(SEMS["b_acc"], 1)
                with n.loop("lag", 2) as i:
                    for k in range(8):
                        pool.wait_ge(*n("b_m"))
                        s0 = i * (-8) + (LAG - k)
                        step(tt(EE[:, :, :], EE[:, :, :], FZ[:, :, bass.ds(s0, SEQ)], ALU.mult))
                        pool.sem_inc(SEMS["b_e"], 1)
                        pool.wait_ge(*n("b_t"))
                        step(tt(ACC[:, :, :], ACC[:, :, :], TM[:, 1 - k % 2, :, :], ALU.add))
                        pool.sem_inc(SEMS["b_acc"], 1)
                pool.wait_ge(*n("b_t"))
                step(tt(ACC[:, :, :], ACC[:, :, :], TM[:, 1, :, :], ALU.add))
                pool.sem_inc(SEMS["b_acc"], 1)
                n("b_m")
                step(nc.gpsimd.memset(QZ[:, :, :], 0.0))
                for hh in range(2):
                    r = slice(64 * hh, 64 * hh + 64)
                    n.settle()
                    nc.gpsimd.tensor_copy(QZ[r, hh::2, :], QG[r, :, :]).then_inc(SEMS["qgz"], 1)
                    pool.wait_ge(*n("qgz"))
                pool.wait_ge(*n("b_tok"))
                for t in range(4):
                    if t > 1:
                        pool.wait_ge(*n("b_us"))
                    x = VT[:, t, :].rearrange("p (h v) -> p h v", h=4).unsqueeze(2).broadcast_to([P, 4, 8, 64])
                    y = c("blk8").unsqueeze(1).unsqueeze(3).broadcast_to([P, 4, 8, 64])
                    tt(VE[t % 2].rearrange("p (h i v) -> p h i v", h=4, i=8), x, y, ALU.mult).then_inc(SEMS["b_ve"], 1)
                n("b_us", 2)
                pool.wait_ge(*n("c_acb"))
                pool.wait_ge(*n("c_x"))
                x = PJ2[:, 14:16, :].unsqueeze(2).broadcast_to([P, 2, 2, SEQ])
                tt(CME.rearrange("p (g e) t -> p g e t", g=2), EAB.rearrange("p (g e) t -> p g e t", g=2), x, ALU.mult)\
                    .then_inc(SEMS["c_cme"], 1)
                pool.wait_ge(*n("c_cme"))
                pool.wait_ge(*n("d_qe"))
                wide = lambda x, m: x.unsqueeze(1).broadcast_to([QKR - 64, m, SEQ])
                tt(QF[rr, 0:HEADS, :], QF[rr, 0:HEADS, :], wide(COS[rr, :], HEADS), ALU.mult)
                tt(QR[rr, :, :], QR[rr, :, :], wide(SIN[rr, :], HEADS), ALU.mult)
                tt(PJ2[rr, 16, :], PJ2[rr, 16, :], COS[rr, :], ALU.mult)
                step(tt(KRR[rr, :], KRR[rr, :], SIN[rr, :], ALU.mult))
                tt(QF[rr, 0:HEADS, :], QF[rr, 0:HEADS, :], QR[rr, :, :], ALU.add)
                step(tt(KF[rr, 0:HEADS, :], wide(PJ2[rr, 16, :], HEADS), wide(KRR[rr, :], HEADS), ALU.add))
                pool.sem_inc(SEMS["d_q"], 1)
                for k in range(KD):
                    pool.wait_ge(*n("yo"))
                    n.settle()
                    tt(XK[:, k, :], XK[:, k, :], PJ2[:, 8 + k, :], ALU.add).then_inc(SEMS["x2_ready"], 1)

        @block.vector
        def _(dve):
            n = Tally("dve", dve, SEMS)
            v = nc.vector
            tt, stt, ts = v.tensor_tensor, v.scalar_tensor_tensor, v.tensor_scalar

            def link(ins):
                ins.then_inc(SEMS["dve_step"], 1)
                dve.wait_ge(*n("dve_step"))

            def mark(name):
                n.settle()
                dve.drain().then_inc(SEMS[name], 1)

            def post(name):
                dve.sem_inc(SEMS[name], 1)

            def join():
                n.settle()
                link(dve.drain())

            v.memset(epsc[:, 0:1], EPS)
            v.memset(epsc[:, 1:2], 1e-5)
            v.memset(epsc[:, 2:3], 1.0)
            v.memset(V[:, 0, :], 0.0)
            v.memset(junk[:, :], 0.0).then_inc(SEMS["eps_ready"], 1)
            mark("v_zero")
            for p in range(4):
                dve.sem_inc(SEMS[f"free{p}"], 1)

            def norm(x, gain, width, t0=0):
                dve.wait_ge(*n("rms_root"))
                link(v.reciprocal(R[:, 0:width], R[:, 0:width]))
                for k in range(KD):
                    stt(HN[:, k, 0:width], x[:, k, :], gain(k), R[:, 0:width], ALU.mult, ALU.mult).then_inc(SEMS["hn_ready"], 1)

            dve.wait_ge(SEMS["par_in"], 32)
            for k in range(KD):
                dve.wait_ge(SEMS[f"x_in{k}"], 16)
            norm(X[:, :, :], lambda k: v1("g1", k), T)
            dt, mag, sin, cos = (s5c[:, k, :] for k in (0, 2, 3, 4))
            are, aim = (par1[:, V1[k][0]:V1[k][1]] for k in ("are", "aim"))
            lam0 = V1["lam"][0]
            lamv = par1[:, lam0:lam0 + 256].rearrange("p (a b c) -> p a b c", a=2, b=2)
            link(tt(TMP[:, 0, 0:128].rearrange("p (a c) -> p a c", a=2), lamv[:, :, 0, :], lamv[:, :, 1, :], ALU.mult))
            v.tensor_reduce(lamc[:, 0:2], TMP[:, 0, 0:128].rearrange("p (a c) -> p a c", a=2), AX.X, ALU.add)
            ts(lamc[:, 5:6], v1("qg"), 0.125, None, ALU.mult)
            ts(lamc[:, 6:7], v1("subg"), 1.0 - LAM_INIT, None, ALU.mult)
            ts(glub2[:, :], par1[:, V1["glub"][0]:V1["glub"][1]], 0.5, None, ALU.mult)
            dve.wait_ge(SEMS["s5_dt"], 1)
            tt(mag, are, dt, ALU.mult)
            t5, t6 = s5c[:, 5, :], s5c[:, 6, :]
            link(tt(t5, aim, dt, ALU.mult))
            link(ts(t6, t5, 1.0 / (2 * np.pi), MAGIC, ALU.mult, ALU.add))
            link(ts(t6, t6, -MAGIC, None, ALU.add))
            for part in PI2:
                link(stt(t5, t6, -part, t5, ALU.mult, ALU.add))
            link(ts(cos, t5, float(np.pi / 2), None, ALU.add))
            link(ts(t6, cos, float(np.pi), -2 * float(np.pi), ALU.is_gt, ALU.mult))
            link(tt(cos, cos, t6, ALU.add))
            ts(cos, cos, PIF, -PIF, ALU.min, ALU.max)
            ts(sin, t5, PIF, -PIF, ALU.min, ALU.max).then_inc(SEMS["trig_arg"], 1)
            dve.wait_ge(*n("trig"))
            link(tt(lamc[:, 4:5], lamc[:, 2:3], lamc[:, 3:4], ALU.subtract))
            link(ts(lamc[:, 4:5], lamc[:, 4:5], LAM_INIT, None, ALU.add))
            ts(lamc[:, 4:5], lamc[:, 4:5], -1.0, None, ALU.mult)
            lr, li, fr, nfi, w = (s5c[:, k, :] for k in (6, 7, 8, 9, 10))
            link(tt(lr, mag, cos, ALU.mult))
            tt(li, mag, sin, ALU.mult)
            link(ts(lr, lr, -1.0, None, ALU.add))
            tt(fr, lr, are, ALU.mult)
            link(tt(w, li, aim, ALU.mult))
            tt(fr, fr, w, ALU.add)
            link(tt(nfi, lr, aim, ALU.mult))
            link(tt(w, li, are, ALU.mult))
            tt(nfi, nfi, w, ALU.subtract)
            link(tt(t5, are, are, ALU.mult))
            link(tt(w, aim, aim, ALU.mult))
            link(tt(w, t5, w, ALU.add))
            link(v.reciprocal(w, w))
            link(tt(fr, fr, w, ALU.mult))
            tt(nfi, nfi, w, ALU.mult)

            B4 = ph_b.rearrange("p r (c j) -> p r c j", j=66)
            A4 = ph_a.rearrange("p r (c j) -> p r c j", j=8)
            E1 = TMP[:, 2, 0:32].rearrange("p (r c) -> p r c", r=2)
            E2 = TMP[:, 3, 0:32].rearrange("p (r c) -> p r c", r=2)

            def cmul(o, x, y, ta, tb):
                tt(o[0], x[0], y[0], ALU.mult)
                tt(ta, x[1], y[1], ALU.mult)
                tt(o[1], x[0], y[1], ALU.mult)
                link(tt(tb, x[1], y[0], ALU.mult))
                tt(o[0], o[0], ta, ALU.subtract)
                link(tt(o[1], o[1], tb, ALU.add))

            v.tensor_copy(E1[:, 0, :], cos)
            link(v.tensor_copy(E1[:, 1, :], sin))
            for tab in (B4, A4):
                v.memset(tab[:, 0, :, 0:1], 1.0)
                v.memset(tab[:, 1, :, 0:1], 0.0)
            join()

            def tmp3(k, m):
                return TMP[:, k, 0:16 * m].rearrange("p (c j) -> p c j", j=m)

            def double(tab, size, e, e2):
                m = 1
                while m < size:
                    w_ = min(m, size - m)
                    bc = [e[:, r, :].unsqueeze(2).broadcast_to([P, 16, w_]) for r in range(2)]
                    cmul([tab[:, r, :, m:m + w_] for r in range(2)], [tab[:, r, :, 0:w_] for r in range(2)], bc,
                         tmp3(0, w_), tmp3(1, w_))
                    if 2 * m < size:
                        cmul([e2[:, r, :] for r in range(2)], [e[:, r, :] for r in range(2)],
                             [e[:, r, :] for r in range(2)], TMP[:, 0, 0:16], TMP[:, 1, 0:16])
                        e, e2 = e2, e
                    m *= 2

            first = junkE[:, :].rearrange("p (r c) -> p r c", r=2)
            link(v.tensor_copy(first, E1))
            double(B4, 66, E1, E2)
            cmul([E1[:, r, :] for r in range(2)], [B4[:, r, :, 65] for r in range(2)],
                 [first[:, r, :] for r in range(2)], TMP[:, 0, 0:16], TMP[:, 1, 0:16])
            double(A4, 8, E1, E2)
            mark("s5_tab")
            for _ in range(2):
                mark("s5_x_free")
            dve.wait_ge(*n("u_ready"))
            with n.loop("s5", 4) as i:
                for j in range(4):
                    pr, pi = PH[:, j % 2, 0, :], PH[:, j % 2, 1, :]
                    xr, xi = XS[:, j % 2, 0, :], XS[:, j % 2, 1, :]
                    t0, t1, t2, t3 = (TMP[:, k, :] for k in range(4))
                    dve.wait_ge(*n("s5_ph"))
                    dve.wait_ge(*n("s5_x"))
                    tt(t0, pr, xr, ALU.mult)
                    tt(t1, pi, xi, ALU.mult)
                    tt(t2, pr, xi, ALU.mult)
                    link(tt(t3, pi, xr, ALU.mult))
                    tt(t0, t0, t1, ALU.add)
                    link(tt(t2, t2, t3, ALU.subtract))
                    decay = mag[:, bass.ds(i * 4 + j, 1)].broadcast_to([P, T])
                    v.tensor_tensor_scan(t1, decay, t0, 0.0, ALU.mult, ALU.add)
                    link(v.tensor_tensor_scan(t3, decay, t2, 0.0, ALU.mult, ALU.add))
                    if j:
                        dve.wait_ge(*n("s5_s_free"))
                    tt(SS[:, 0, :], pr, t1, ALU.mult)
                    tt(SS[:, 1, :], pr, t3, ALU.mult)
                    tt(t0, pi, t3, ALU.mult)
                    link(tt(t2, pi, t1, ALU.mult))
                    tt(SS[:, 0, :], SS[:, 0, :], t0, ALU.subtract)
                    tt(SS[:, 1, :], SS[:, 1, :], t2, ALU.add).then_inc(SEMS["s5_s"], 1)
                    dve.wait_ge(*n("s5_s"))
                    post("s5_x_free")
                    if j in (2, 3):
                        x = j - 2
                        chunk = PJ[:, i + 4 * (x + 1), :]
                        link(stt(chunk, chunk, (lamc[:, 5:6], v1("kg"))[x], RT[:, x, :], ALU.mult, ALU.mult))
                        if x == 1:
                            post("qk_n")
                    if j in (1, 2):
                        dve.wait_ge(*n("qk_root"))
                        link(v.reciprocal(RT[:, j - 1, :], RT[:, j - 1, :]))
                dve.wait_ge(*n("dve_full2"))
                u = two(PJ[:, i, :])
                stt(u, u, par1[:, bass.ds(i + V1["d"][0], 1)], halves(2), ALU.mult, ALU.add).then_inc(SEMS["free2"], 1)
            for x in (WC[:, :, 0:P], OR[:, 0::5, :], WT[:, 0, :], st):
                v.memset(x, 0.0)
            mark("s5_y")
            dve.wait_ge(*n("v_ready"))
            neglam = lamc[:, 4:5]

            def scores(h, t):
                q0, rows = TILES[t]
                keys = q0 + rows
                for j in range(2):
                    dve.wait_ge(*n(f"dve_full{2 + j}"))
                    stt(SX[0:rows, t % 3, j, 0:keys], c("dist", SEQ - P + NMETA - q0, keys, rows),
                        cst[0:rows, bass.ds(h + CC["negslope"][0], 1)], ps(2 + j)[0:rows, 0:keys],
                        ALU.mult, ALU.add).then_inc(SEMS[f"free{2 + j}"], 1)
                join()
                col = MX + 2 * (t % 3)
                v.tensor_reduce(st[0:rows, col:col + 2], SX[0:rows, t % 3, :, 0:keys], AX.X, ALU.max,
                                negate=True).then_inc(SEMS["sc_ready"], 1)

            def combine(t):
                q0, rows = TILES[t]
                keys = q0 + rows
                dve.wait_ge(*n("ex_ready"))
                o, rc_ = SM + 2 * (t % 3), RC5 + 2 * t
                link(v.reciprocal(st[0:rows, rc_:rc_ + 2], st[0:rows, o:o + 2]))
                link(stt(st[0:rows, RA5:RA5 + 1], st[0:rows, o:o + 1], neglam[0:rows], st[0:rows, rc_ + 1:rc_ + 2],
                         ALU.mult, ALU.mult))
                if t != 1:
                    dve.wait_ge(*n("wt_ready", 2 if t == 0 else 1))
                stt(WC[0:rows, t % 2, 0:keys], SX[0:rows, t % 3, 1, 0:keys], st[0:rows, RA5:RA5 + 1],
                    SX[0:rows, t % 3, 0, 0:keys], ALU.mult, ALU.add).then_inc(SEMS["w_comb"], 1)
                dve.wait_ge(*n("w_comb"))

            scores(0, 0)
            scores(0, 1)
            with n.loop("att", HEADS) as h:
                scores(h, 2)
                combine(0)
                scores(h, 3)
                combine(1)
                scores(h, 4)
                combine(2)
                combine(3)
                scores(h + 1, 0)
                combine(4)
                scores(h + 1, 1)
            dve.wait_ge(*n("ex_ready", 2))
            dve.wait_ge(*n("o_root"))
            o = st[:, OS:OS + 5 * HEADS]
            link(v.reciprocal(o, o))
            tt(OR[:, :, :], OR[:, :, :], o.unsqueeze(2).broadcast_to([P, 5 * HEADS, P]), ALU.mult).then_inc(SEMS["o_norm"], 1)
            dve.wait_ge(*n("o_norm"))
            for m in range(4):
                dve.wait_ge(*n("glu_th"))
                ins = stt(PJ[:, 8 + m, :], TH[:, m, :], 1.0, PJ[:, m, :], ALU.add, ALU.mult)
            ins.then_inc(SEMS["ys_ready"], 1)
            with n.loop("mix", 2) as i:
                for k in range(WSLOTS):
                    p = 2 * (k % 2)
                    m = i * 4 + k
                    dve.wait_ge(*n(f"dve_full{p}"))
                    g = two(PJ[:, m + 12, :])
                    stt(g, g, 1.0, halves(p), ALU.add, ALU.mult).then_inc(SEMS[f"free{p}"], 1)
                    dve.wait_ge(*n(f"dve_full{p + 1}"))
                    stt(two(JK2[:, :]), two(PJ[:, m + 20, :]), 1.0, halves(p + 1), ALU.add, ALU.mult)\
                        .then_inc(SEMS[f"free{p + 1}"], 1)
                    join()
                    link(stt(PJ[:, m + 12, :], PJ[:, m + 12, :], 0.5, JK2[:, :], ALU.mult, ALU.add))
            post("mix_ready")
            with n.loop("wo", 2) as i:
                for k in range(WSLOTS):
                    dve.wait_ge(*n(f"dve_full{k}"))
                    x = two(X[:, i * 4 + k, :])
                    stt(x, halves(k), 0.5, x, ALU.mult, ALU.add).then_inc(SEMS[f"free{k}"], 1)
                    mark("h_ready")
            norm(X[:, :, :], lambda k: v1("g2", k), T)
            with n.loop("up", NFF // 2) as i:
                for m in range(2):
                    def col(name):
                        return par1[:, bass.ds(i * 2 + (m + V1[name][0]), 1)]

                    dve.wait_ge(*n("ffa"))
                    link(ts(CV[:, :], FA[:, 2:514], col("cw2"), col("cb"), ALU.mult, ALU.add))
                    link(stt(CV[:, :], FA[:, 1:513], col("cw1"), CV[:, :], ALU.mult, ALU.add))
                    stt(CV[:, :], FA[:, 0:512], col("cw0"), CV[:, :], ALU.mult, ALU.add).then_inc(SEMS["ffc"], 1)
                    mark(f"free{2 * m}")
                    dve.wait_ge(*n("ffg"))
                    dve.wait_ge(*n(f"dve_full{2 * m + 1}"))
                    tt(hid[:, i * 2 + m, :], GL[:, :], PS[2 * m + 1][:, 0, :], ALU.mult).then_inc(SEMS[f"free{2 * m + 1}"], 1)
                    join()
            post("hid_done")
            dve.wait_ge(SEMS["pos_in"], 16)
            link(v.tensor_copy(ANG, POS[:, :]))
            link(ts(ANG, ANG, c("invf"), None, ALU.mult))
            link(ts(KT, ANG, 1.0 / (2 * np.pi), MAGIC, ALU.mult, ALU.add))
            link(ts(KT, KT, -MAGIC, None, ALU.add))
            for part in PI2:
                link(stt(ANG, KT, -part, ANG, ALU.mult, ALU.add))
            link(ts(COS[:, :], ANG, float(np.pi / 2), None, ALU.add))
            link(ts(KT, COS[:, :], float(np.pi), -2 * float(np.pi), ALU.is_gt, ALU.mult))
            link(tt(COS[:, :], COS[:, :], KT, ALU.add))
            ts(SIN[:, :], ANG, PIF, -PIF, ALU.min, ALU.max)
            link(ts(COS[:, :], COS[:, :], PIF, -PIF, ALU.min, ALU.max))
            post("d_trig_arg")
            dve.wait_ge(*n("d_trig"))
            link(ts(SIN[:, :], SIN[:, :], c("sgn"), None, ALU.mult))
            for p in range(4):
                dve.wait_ge(*n(f"dve_full{p}"))
                x = X[:, 2 * p:2 * p + 2, NMETA:T]
                tt(x, x, PS[p][:, :, :], ALU.add).then_inc(SEMS["x2_ready"], 2)
                mark(f"free{p}")

            with n.loop("layer", LAYERS) as l:
                dve.wait_ge(*n("small_in", 16))
                norm(XK, lambda k: v2("pre", k), SEQ)
                n.settle()
                link(dve.drain())
                tt(LB[:, 4:6], v2("lbl", 2, 2), v2("lbl", 0, 2), ALU.subtract).then_inc(SEMS["lb_arg"], 1)
                ts(DWH[:, :], v2("dww", 0, 64), 0.5, None, ALU.mult)
                dve.wait_ge(*n("lb_th"))
                link(ts(LB[:, 4:6], LB[:, 4:6], 0.5, 0.5, ALU.mult, ALU.add))
                link(ts(LB[:, 0:2], LB[:, 4:6], v2("isl"), None, ALU.mult))
                link(ts(LB[:, 2:4], LB[:, 0:2], -0.5, 0.5, ALU.mult, ALU.add))
                link(tt(LB[:, 4:6], LB[:, 0:2], LB[:, 2:4], ALU.add))
                link(ts(LB[:, 6:8], LB[:, 2:4], -1.0, None, ALU.mult))
                dve.wait_ge(*n("b_th"))
                v.memset(FZ[:, :, 0:LAG], 0.0)
                v.memset(KP[:, :, 0:LAG], 0.0)
                v.memset(VP[:, :, 0:LAG], 0.0)
                v.memset(TM[:, 1, :, :], 0.0)
                for cc in range(2):
                    ts(TM[:, 0, cc, :], PJ2[:, cc, :], LB[:, 2 + cc:3 + cc], LB[:, 4 + cc:5 + cc], ALU.mult, ALU.add)
                    ts(KP[:, cc, LAG:], PJ2[:, cc, :], LB[:, 6 + cc:7 + cc], LB[:, 2 + cc:3 + cc], ALU.mult, ALU.add)
                v.tensor_copy(VP[:, :, LAG:], PJ2[:, 4:6, :])
                link(v.tensor_copy(EE[:, :, :], PJ2[:, 2:4, :]))
                link(ts(TM[:, 0, :, :], TM[:, 0, :, :], 1e-20, None, ALU.max))
                v.tensor_copy(FZ[:, :, LAG:], TM[:, 0, :, :])
                blocks = lambda x: x.rearrange("p a (b s) -> p a b s", s=LAG)
                link(v.tensor_copy(blocks(TM[:, 1, :, :])[:, :, :, 0], blocks(TM[:, 0, :, :])[:, :, :, 0]))
                link(v.memset(blocks(FZ[:, :, LAG:])[:, :, :, 0], 0.0))
                for cc in range(2):
                    ins = v.tensor_tensor_scan(MB[:, 0, cc, :], FZ[:, cc, LAG:], TM[:, 1, cc, :], 0.0, ALU.mult, ALU.add)
                link(ins)
                tt(QG[:, :, :], EE[:, :, :], MB[:, 0, :, :], ALU.mult)
                link(v.tensor_copy(DL[:, :, :], blocks(MB[:, 0, :, :])[:, :, :, LAG - 1]))
                v.memset(DL[:, :, 0:1], 0.0)
                hs_, fs_ = blocks(TM[:, 0, :, :]), blocks(FZ[:, :, LAG:])
                link(v.memset(hs_[:, :, :, LAG - 1], 1.0))
                for q in range(LAG - 2, -1, -1):
                    link(tt(hs_[:, :, :, q], fs_[:, :, :, q + 1], hs_[:, :, :, q + 1], ALU.mult))
                link(tt(KH[:, :, :], KP[:, :, LAG:], TM[:, 0, :, :], ALU.mult))
                post("b_kh")
                tt(MB[:, 0, :, :], EE[:, :, :], KP[:, :, LAG:], ALU.mult).then_inc(SEMS["b_m"], 1)
                link(v.memset(TM[:, 1, :, :], 0.0))
                post("b_t")
                dve.wait_ge(*n("a_th"))
                v.memset(HP[:, :, 0:30], 0.0)
                v.memset(HP[:, :, 542:543], 0.0)
                v.memset(CA[:, :, :], 0.0)
                link(stt(HP[:, :, 30:542], PJ2[:, 8:10, :], 1.0, PJ2[:, 6:8, :], ALU.add, ALU.mult))
                for cc in range(2):
                    link(ts(CA[:, cc, :], CA[:, cc, :], v2("dwb", cc), None, ALU.add))
                with n.loop("lag", 2) as i:
                    for k in range(8):
                        s0 = i * (-8) + (LAG - k)
                        dve.wait_ge(*n("b_e"))
                        tt(MB[:, 1 - k % 2, :, :], EE[:, :, :], KP[:, :, bass.ds(s0 - 1, SEQ)], ALU.mult).then_inc(SEMS["b_m"], 1)
                        for tap in range(2):
                            for cc in range(2):
                                o = i * 16 + (2 * k + tap)
                                ins = stt(CA[:, cc, :], HP[:, cc, bass.ds(o, SEQ)],
                                          DWH[:, bass.ds(i * 16 + (32 * cc + 2 * k + tap), 1)], CA[:, cc, :], ALU.mult, ALU.add)
                            link(ins)
                        dve.wait_ge(*n("b_acc"))
                        dve.wait_ge(*n(f"dve_full{2 + k % 2}"))
                        tt(TM[:, k % 2, :, :], PS[2 + k % 2][:, :, :], VP[:, :, bass.ds(s0, SEQ)], ALU.mult)\
                            .then_inc(SEMS[f"free{2 + k % 2}"], 1)
                        mark("b_t")
                for _ in range(2):
                    dve.wait_ge(*n("b_acc"))
                post("a_ca")
                ts(CWH[:, 0:24], v2("ccw", 0, 24), 0.5, None, ALU.mult)
                link(ts(CWH[:, 24:30], v2("ccb", 0, 6), 0.5, None, ALU.mult))
                dve.wait_ge(*n("dve_full1"))
                m0 = PS[1][:, 0, :].unsqueeze(1).broadcast_to([P, 2, SEQ])
                stt(CA[:, :, :], m0, -1.0 / 256, CA[:, :, :], ALU.mult, ALU.add).then_inc(SEMS["a_xc"], 1)
                dve.wait_ge(*n("b_us", 4))
                n.settle()
                for cc in range(2):
                    z = DZ[cc].rearrange("p (v i) -> p v i", i=NBLK)
                    ins = v.tensor_copy(z, DL[:, cc, :].unsqueeze(1).broadcast_to([P, 64, NBLK]))
                link(ins)
                for cc in range(2):
                    us = (US0, US1)[cc]
                    ins = v.tensor_tensor_scan(us, DZ[cc], us, 0.0, ALU.mult, ALU.add)
                ins.then_inc(SEMS["b_s"], 1)
                dve.wait_ge(*n("d_root"))
                link(v.reciprocal(RD[:, :, :], RD[:, :, :]))
                for b in range(2):
                    stt(CQ[:, b, :], CQ[:, b, :], v2("qag", b), RD[:, 0, :], ALU.mult, ALU.mult)
                stt(CK, CK, v2("kvg"), RD[:, 1, :], ALU.mult, ALU.mult).then_inc(SEMS["d_n"], 1)
                dve.wait_ge(*n("gate_th"))
                stt(PJ2[:, 22:26, :], FREE[0], 1.0, PJ2[:, 22:26, :], ALU.add, ALU.mult)
                dve.wait_ge(*n("dve_full0"))
                link(tt(ACC[:, :, LAG:], ACC[:, :, LAG:], PS[0][:, :, LAG:], ALU.add))
                post("free0")
                post("b_acc2")
                dve.wait_ge(*n("a_root"))
                link(v.reciprocal(RA, RA))
                for cc in range(2):
                    stt(CA[:, cc, :], CA[:, cc, :], v2("lng", cc), RA, ALU.mult, ALU.mult)
                join()
                for cc in range(2):
                    ins = ts(CA[:, cc, :], CA[:, cc, :], v2("lnb", cc), None, ALU.add)
                ins.then_inc(SEMS["a_x"], 1)
                dve.wait_ge(*n("b_root"))
                link(v.reciprocal(RB[:, :, :], RB[:, :, :]))
                for cc in range(2):
                    stt(ACC[:, cc, :], ACC[:, cc, :], v2("bng", cc), RB[:, cc, :], ALU.mult, ALU.mult)
                join()
                stt(PJ2[:, 24:26, :], PJ2[:, 24:26, :], 0.5, ACC[:, :, :], ALU.mult, ALU.mult)
                dve.wait_ge(*n("a_xt"))
                stt(CA[:, :, :], SQA[:, :, :], 1.0, CA[:, :, :], ALU.add, ALU.mult).then_inc(SEMS["a_h"], 1)
                dve.wait_ge(*n("dve_full1"))
                for m in range(2):
                    ts(SQA[:, m, :], PS[1][:, m, :], 0.5, v2("pwb", m), ALU.mult, ALU.add)
                join()
                post("free1")
                link(stt(PJ2[:, 22:24, :], PJ2[:, 22:24, :], 0.5, SQA[:, :, :], ALU.mult, ALU.mult))
                U4 = DD[0:4, 1, :]
                link(ts(U4, PJ2[0:4, 16, :], v2("dtb", rows=4), None, ALU.add))
                stt(DD[0:4, 0, :], U4, -1.0, U4, ALU.mult, ALU.max).then_inc(SEMS["c_dtabs"], 1)
                for m in range(6):
                    link(ts(CX[:, m, :], PJ2[:, 10 + m, :], CWH[:, 18 + m:19 + m], CWH[:, 24 + m:25 + m], ALU.mult, ALU.add))
                    for b in (1, 2, 3):
                        ins = stt(CX[:, m, b:], PJ2[:, 10 + m, 0:SEQ - b], CWH[:, (3 - b) * 6 + m:(3 - b) * 6 + m + 1], CX[:, m, b:],
                                  ALU.mult, ALU.add)
                        link(ins)
                post("c_cx")
                dve.wait_ge(*n("c_dtln"))
                link(stt(DT4[0:4, :], U4, 0.0, DD[0:4, 0, :], ALU.max, ALU.add))
                link(ts(LB2[0:4, 0:1], LB2[0:4, 0:1], -1.0, None, ALU.mult))
                link(ts(U4, DT4[0:4, :], LB2[0:4, 0:1], None, ALU.mult))
                v.tensor_tensor_scan(AC4[0:4, :], c("keep", 0, SEQ, 4), U4, 0.0, ALU.mult, ALU.add).then_inc(SEMS["c_dt"], 1)
                dve.wait_ge(*n("c_th"))
                stt(PJ2[:, 10:16, :], PJ2[:, 10:16, :], 1.0, CX[:, :, :], ALU.add, ALU.mult).then_inc(SEMS["c_x"], 1)
                dve.wait_ge(*n("c_x"))
                dve.wait_ge(*n("c_acb"))
                last = ACB.rearrange("p h (t l) -> p t h l", l=P)[:, :, :, P - 1]
                dcol, acol = COL[:, :, 0:4], COL[:, :, 4:8]
                tt(WCOL[:, :, :], last, acol, ALU.subtract).then_inc(SEMS["c_wd"], 1)
                A4_ = ACB.rearrange("p h (t l) -> p h t l", l=P)
                D4_ = DD.rearrange("p h (t l) -> p h t l", l=P)
                for h in range(HEADS):
                    tt(D4_[:, h], A4_[:, h], acol[:, :, h].unsqueeze(2).broadcast_to([P, 4, P]), ALU.subtract)
                join()
                mask = c("causal").unsqueeze(1).broadcast_to([P, 16, P])
                tt(DD.rearrange("p h (t l) -> p (h t) l", l=P), DD.rearrange("p h (t l) -> p (h t) l", l=P), mask, ALU.add)\
                    .then_inc(SEMS["c_d"], 1)
                dve.wait_ge(*n("c_we"))
                link(tt(WCOL[:, :, :], WCOL[:, :, :], dcol, ALU.mult))
                dve.wait_ge(*n("dve_full1"))
                for t in range(4):
                    xt = ps(1)[:, t * 256:t * 256 + 256].rearrange("p (h v) -> p h v", h=4)
                    tt(XDT[:, t], xt, dcol[:, t, :].unsqueeze(2).broadcast_to([P, 4, 64]), ALU.mult)
                    tt(WX[:, t], xt, WCOL[:, t, :].unsqueeze(2).broadcast_to([P, 4, 64]), ALU.mult)
                mark("free1")
                mark("c_wx")
                dve.wait_ge(*n("dve_full2"))
                link(v.tensor_copy(HS[:, 0, :], ps(2)[:, 0:256]))
                for t in (1, 2):
                    for h in range(HEADS):
                        q = slice(h * 64, h * 64 + 64)
                        dec = EAB[:, h, t * P + P - 1:t * P + P]
                        ins = stt(HS[:, t, q], HS[:, t - 1, q], dec, ps(2)[:, t * 256 + h * 64:t * 256 + h * 64 + 64],
                                  ALU.mult, ALU.add)
                    link(ins)
                post("free2")
                post("c_hs")
                dve.wait_ge(*n("gate_th"))
                for x in (0, 1):
                    z = PJ2[:, (20, 26)[x]:(22, 28)[x], :]
                    stt(z, FREE[1][:, 2 * x:2 * x + 2, :], 1.0, z, ALU.add, ALU.mult)
                dve.wait_ge(*n("c_de"))
                dve.wait_ge(*n("dve_full3"))
                for g in range(2):
                    cb = PS[3][:, g, :].unsqueeze(1).broadcast_to([P, 2, SEQ])
                    tt(DD[:, 2 * g:2 * g + 2, :], DD[:, 2 * g:2 * g + 2, :], cb, ALU.mult)
                mark("free3")
                mark("c_sc")
                dve.wait_ge(*n("dve_full0"))
                for g in range(2):
                    stt(YC[:, g, :], PJ2[:, 10 + g, :], v2("dsk", g), PS[0][:, g, :], ALU.mult, ALU.add)
                join()
                post("free0")
                stt(YC[:, :, :], YC[:, :, :], 0.5, PJ2[:, 20:22, :], ALU.mult, ALU.mult).then_inc(SEMS["c_yc"], 1)

                def scores(t):
                    p = 2 + t % 2
                    w_ = t * P + P
                    dve.wait_ge(*n(f"dve_full{p}"))
                    link(tt(SD[:, t, 0:w_], PS[p][:, 0, 0:w_], c("mlamask", SEQ - w_, w_), ALU.add))
                    post(f"free{p}")
                    v.tensor_reduce(sd[:, t:t + 1], SD[:, t, 0:w_], AX.X, ALU.max, negate=True).then_inc(SEMS["d_sc"], 1)

                def weighed(h, t):
                    dve.wait_ge(*n("dve_full1"))
                    link(v.reciprocal(sd[:, 8:9], sd[:, 4 + t:5 + t]))
                    link(ts(OD[:, t, bass.ds(h * 64, 64)], PS[1][:, t % 2, 0:64], sd[:, 8:9], None, ALU.mult))
                    post("free1")
                    post("d_o")

                scores(0)
                scores(1)
                dve.wait_ge(*n("c_root"))
                with n.loop("mla", HEADS) as h:
                    scores(2)
                    scores(3)
                    part = RC.rearrange("p a b -> p (a b)")[:, bass.ds(h * 256, 256)]
                    link(v.reciprocal(part, part))
                    weighed(h, 0)
                    weighed(h, 1)
                    scores(0)
                    weighed(h, 2)
                    scores(1)
                    weighed(h, 3)
                for g in range(2):
                    ins = stt(PJ2[:, 20 + g, :], YC[:, g, :], v2("cng", g), RC[:, g, :], ALU.mult, ALU.mult)
                link(ins)
                dve.wait_ge(*n("dve_full0"))
                link(stt(PJ2[:, 26:28, :], PJ2[:, 26:28, :], 0.5, PS[0][:, :, :], ALU.mult, ALU.mult))
                post("free0")
                post("y_ready")
                dve.wait_ge(*n("rms_root"))
                link(v.reciprocal(R[:, 0:SEQ], R[:, 0:SEQ]))
                for k in range(KD):
                    stt(PJ2[:, 8 + k, :], HNY[:, k, :], v2("post", k), R[:, 0:SEQ], ALU.mult, ALU.mult).then_inc(SEMS["yo"], 1)


def chunks(w, cols):
    w = w[:, cols]
    return w.reshape(w.shape[0] // P, P, w.shape[1]).transpose(1, 0, 2).reshape(P, -1)


def slices(lo, n):
    return [slice(lo + P * k, lo + P * k + P) for k in range(n)]


def table(spec, values):
    out = np.zeros((P, sum(n for _, n in spec)), np.float32)
    at = 0
    for name, n in spec:
        v = values[name]
        assert v.shape[1] == n, name
        out[:v.shape[0], at:at + n] = v
        at += n
    return out


def layout(x):
    f = {k: np.asarray(v) for k, v in x.items()}
    z = {}
    z["xT"] = np.ascontiguousarray(np.concatenate([f["meta_tokens"], f["x"][0]], 0).T).reshape(KD, P, T)
    w = f["w_in"][0]
    slots = [chunks(w, s) for s in slices(0, 12)]
    wv = w[:, 1536:2048].reshape(KD, P, 512)
    slots += [wv[2 * k:2 * k + 2].transpose(1, 0, 2).reshape(P, 1024) for k in range(4)]
    slots += [chunks(w, s) for s in slices(2048, 16)]
    g = f["ssm_glu_w"][0]
    slots += [np.concatenate([chunks(g, s) for s in slices(256 * k, 2)], 1) for k in range(2)]
    slots += [np.concatenate([chunks(f["w_ssm_out"][0], s), chunks(f["w_att_out"][0], s)], 1) for s in slices(0, 8)]
    slots += [chunks(f["w_o"][0], s) for s in slices(0, 8)]
    up = f["w_up"][0]
    for a_, b_ in zip(slices(0, NFF), slices(NFF * P, NFF)):
        slots += [chunks(up, a_), chunks(up, b_)]
    slots += list(f["w_down"][0].reshape(NFF, P, D))
    order = [3 * 256 + 256, 3 * 256, 3 * 256 + 512, 0, 256]
    c0 = 7 * 256
    for l in range(LAYERS):
        w2 = f["w_in_2"][l]
        for o in order:
            slots += [chunks(w2, s) for s in slices(o, 2)]
        slots += [chunks(w2, s) for s in slices(c0, 6)]
        misc = np.zeros((D, P), np.float32)
        misc[:, 0:4] = w2[:, c0 + 768:c0 + 772]
        misc[:, 64:96] = w2[:, c0 + 1412:c0 + 1444]
        slots += [chunks(misc, slice(0, P)), chunks(w2, slice(c0 + 1284, c0 + 1412))]
        for o in (c0 + 1028, 512, 6 * 256, c0 + 772, c0 + 1444):
            slots += [chunks(w2, s) for s in slices(o, 2)]
        wo2 = f["w_out_2"][l].reshape(4, 256, D)[[2, 0, 1, 3]].reshape(D, D)
        slots += [chunks(wo2, s) for s in slices(0, 8)]
    z["wst"] = np.stack(slots)
    s5w = np.zeros((16, P, 4, P), np.float32)
    for k in range(16):
        for g2 in range(2):
            ch = slice(32 * (k % 4) + 16 * g2, 32 * (k % 4) + 16 * g2 + 16)
            st_ = slice(64 * g2, 64 * g2 + 64)
            s5w[k, ch, 0, st_] = f["ssm_b_re"][0, 2 * k + g2].T
            s5w[k, ch, 1, st_] = f["ssm_b_im"][0, 2 * k + g2].T
            s5w[k, st_, 2, ch] = f["ssm_c_re"][0, 2 * k + g2].T
            s5w[k, st_, 3, ch] = f["ssm_c_im"][0, 2 * k + g2].T
    z["s5w"] = s5w.reshape(16, P, 512)

    def cols(v):
        return v.reshape(-1, P).T

    z["par1"] = table(VEC1, {
        "g1": cols(f["norm1_g"][0]), "qg": np.tile(f["q_norm_g"][0], 2)[:, None], "kg": np.tile(f["k_norm_g"][0], 2)[:, None],
        "d": cols(f["ssm_d"][0].reshape(-1)), "glub": cols(f["ssm_glu_b"][0]), "g2": cols(f["norm2_g"][0]),
        "cw0": cols(f["conv_w"][0, 0]), "cw1": cols(f["conv_w"][0, 1]), "cw2": cols(f["conv_w"][0, 2]),
        "cb": cols(f["conv_b"][0]), "are": cols(f["ssm_a_re"][0].reshape(-1)), "aim": cols(f["ssm_a_im"][0].reshape(-1)),
        "ldt": cols(np.repeat(f["ssm_log_dt"][0], 64)), "subg": f["subln_g"][0][:, None],
        "lam": np.broadcast_to(np.concatenate([f[k][0] for k in ("lam_q1", "lam_k1", "lam_q2", "lam_k2")])[None], (P, 256))})
    r = np.arange(P)[:, None]
    rot = np.zeros((P, P), np.float32)
    for k in range(16):
        rot[64 + 16 + k, 64 + k] = 1.0
        rot[64 + k, 64 + 16 + k] = 1.0
    dist = r - (np.arange(T)[None] - (SEQ - P + NMETA))
    tri = np.where(r[:64 * 0 + P] <= np.arange(P)[None], 0.0, NEG)
    mla = np.zeros((P, SEQ))
    mla[:64, SEQ - 64:] = NEG
    sel4 = np.zeros((P, 4, P))
    for k in range(4):
        sel4[k, k] = 1.0
    invf = np.zeros((P, 1))
    invf[64:96, 0] = np.tile(np.float32(10000.0) ** (-np.arange(0, 32, 2, dtype=np.float32) / np.float32(32)), 2)
    keep = np.ones((P, SEQ))
    keep[:, ::P] = 0.0
    small = []
    swap = np.r_[16:32, 0:16]
    for l in range(LAYERS):
        qb = f["d_qb_w_2"][l].reshape(2, P, 4, QKR)
        kvb = f["d_kvb_w_2"][l].reshape(P, 4, 2, 64)
        pw = f["a_pw_w_2"][l].reshape(2, P, 2, P)
        par = table(VEC2, {
            "pre": cols(f["pre_norm_g_2"][l]), "post": cols(f["post_norm_g_2"][l]),
            "dww": np.concatenate([f["a_dw_w_2"][l], np.zeros((1, 256), np.float32)]).reshape(32, 2, P).transpose(2, 1, 0).reshape(P, 64),
            "dwb": cols(f["a_dw_b_2"][l]), "lng": cols(f["a_ln_g_2"][l]), "lnb": cols(f["a_ln_b_2"][l]), "pwb": cols(f["a_pw_b_2"][l]),
            "lbl": cols(f["b_lb_logits_2"].reshape(-1)), "bng": cols(f["b_norm_g_2"][l]), "ccw": cols(f["c_conv_w_2"][l].reshape(-1)),
            "ccb": cols(f["c_conv_b_2"][l]), "dtb": f["c_dt_bias_2"][l][:, None], "alog": f["c_a_log_2"][l][:, None],
            "dsk": cols(np.repeat(f["c_d_2"][l], 64)), "cng": cols(f["c_norm_g_2"][l]), "qag": cols(f["d_qa_g_2"][l]),
            "kvg": cols(f["d_kva_g_2"][l]), "isl": np.full((P, 1), float(l), np.float32)})
        small.append(np.concatenate([
            qb.transpose(1, 2, 0, 3).reshape(P, -1), qb[..., 64:][..., swap].transpose(1, 2, 0, 3).reshape(P, -1),
            kvb[:, :, 0].reshape(P, -1), kvb[:, :, 1].reshape(P, -1), pw.transpose(1, 2, 0, 3).reshape(P, -1), par], 1))
    z["small"] = np.stack(small)
    z["pos"] = np.broadcast_to(f["positions_2"].astype(np.int32), (P, SEQ)).copy()
    sgn = np.ones((P, 1))
    sgn[64:80] = -1.0
    z["cst"] = table(CONSTS, {
        "ident": np.eye(P), "ones": np.ones((P, P)), "pair64": np.kron(np.eye(2), np.ones((64, 64))), "rot": rot,
        "dist": np.where(dist >= 0, dist, -NEG), "mlamask": mla, "causal": tri, "blk8": (r // LAG == np.arange(8)[None]) * 1.0,
        "negslope": np.broadcast_to(-2.0 ** (-8.0 * np.arange(1, HEADS + 2) / HEADS)[None], (P, HEADS + 1)), "invf": invf, "sgn": sgn,
        "sel4": sel4.reshape(P, 512), "keep": keep})
    return z


def kernel(**inputs):
    import concourse.bacc as bacc
    from concourse.bass_utils import run_bass_kernel_spmd

    nc = bacc.Bacc("TRN2", target_bir_lowering=False, num_devices=1)
    arrays = layout(inputs)
    aps = {k: nc.dram_tensor(k, v.shape, mybir.dt.from_np(v.dtype), kind="ExternalInput").ap() for k, v in arrays.items()}
    out = nc.dram_tensor("outT", (KD, P, SEQ), F32, kind="ExternalOutput").ap()
    build(nc, aps, out)
    r = run_bass_kernel_spmd(nc, [arrays], core_ids=[0])
    return np.ascontiguousarray(r.results[0]["outT"].reshape(D, SEQ).T)[None]
```
